# Optimizing a Trainium2 kernel written in Bass

```python
import math
import jax, jax.numpy as jnp
from jax import lax
import numpy as np

D_MODEL = 1024
BATCH = 1
SEQ = 512
DEPTH = 2

GRID_W = 64
NA_HEADS = 8
NA_HEAD_DIM = 64
NA_WIN_ROWS = 8
NA_WIN_COLS = 16
MLA_HEADS = 8
MLA_Q_RANK = 256
MLA_KV_RANK = 128
MLA_NOPE_DIM = 64
MLA_ROPE_DIM = 32
MLA_V_DIM = 64
ROPE_THETA = 10000.0
D_FF = 4 * D_MODEL
Q_BLOCK = 128
NORM_EPS = 1e-6
NA_WIDTH = NA_HEADS * NA_HEAD_DIM
MLA_WIDTH = MLA_HEADS * MLA_V_DIM
IN_SIZES = (NA_WIDTH, NA_WIDTH, NA_WIDTH, MLA_Q_RANK, MLA_KV_RANK, MLA_ROPE_DIM, 2 * D_MODEL)
IN_COLS = sum(IN_SIZES)
RPB_ROWS = 2 * NA_WIN_ROWS - 1
RPB_COLS = 2 * NA_WIN_COLS - 1


def rmsnorm(x, g):
    xf = x.astype(jnp.float32)
    y = xf * lax.rsqrt(jnp.mean(xf * xf, axis=-1, keepdims=True) + NORM_EPS)
    return (y * g.astype(jnp.float32)).astype(x.dtype)

def apply_rope(x, cos, sin):
    half = x.shape[-1] // 2
    x1, x2 = x[..., :half], x[..., half:]
    return jnp.concatenate([x1 * cos - x2 * sin, x2 * cos + x1 * sin], axis=-1)

def rope_tables(positions, dtype):
    inv_freq = 1.0 / (ROPE_THETA ** (jnp.arange(0, MLA_ROPE_DIM, 2, dtype=jnp.float32) / MLA_ROPE_DIM))
    ang = positions.astype(jnp.float32)[..., None] * inv_freq
    return jnp.cos(ang).astype(dtype), jnp.sin(ang).astype(dtype)

def split_cols(t, sizes):
    idx = []
    acc = 0
    for s in sizes[:-1]:
        acc += s
        idx.append(acc)
    return jnp.split(t, idx, axis=-1)

def neighborhood_attention(q, k, v, rpb):
    B, S, H, dh = q.shape
    rows = S // GRID_W
    kh = min(NA_WIN_ROWS, rows)
    kw = NA_WIN_COLS

    def to_grid(t):
        return t.reshape(B, rows, GRID_W, H, dh).transpose(1, 0, 3, 2, 4)

    qg, kg, vg = to_grid(q), to_grid(k), to_grid(v)
    col = jnp.arange(GRID_W)
    col_start = jnp.clip(col - kw // 2, 0, GRID_W - kw)
    col_idx = col_start[:, None] + jnp.arange(kw)
    col_off = col_idx - col[:, None] + (NA_WIN_COLS - 1)
    row = jnp.arange(rows)
    row_start = jnp.clip(row - kh // 2, 0, rows - kh)
    scale = dh ** -0.5

    def one_row(args):
        r, rs, q_r = args
        k_blk = lax.dynamic_slice_in_dim(kg, rs, kh, axis=0)
        v_blk = lax.dynamic_slice_in_dim(vg, rs, kh, axis=0)
        k_nb = k_blk[:, :, :, col_idx]
        v_nb = v_blk[:, :, :, col_idx]
        s = jnp.einsum('bhcd,ibhcjd->bhcij', q_r, k_nb).astype(jnp.float32) * scale
        row_off = rs + jnp.arange(kh) - r + (NA_WIN_ROWS - 1)
        bias = rpb[:, row_off[:, None, None], col_off[None, :, :]]
        s = s + bias.transpose(0, 2, 1, 3)[None].astype(jnp.float32)
        p = jax.nn.softmax(s.reshape(B, H, GRID_W, kh * kw), axis=-1)
        p = p.reshape(B, H, GRID_W, kh, kw).astype(v.dtype)
        return jnp.einsum('bhcij,ibhcjd->bhcd', p, v_nb)

    out = lax.map(one_row, (row, row_start, qg))
    return out.transpose(1, 0, 3, 2, 4).reshape(B, S, H * dh)

def mla_attention(c_q, c_kv, k_rope, w_uq, w_ukv, g_q, g_kv, cos, sin):
    B, S, _ = c_q.shape
    H = MLA_HEADS
    q = (rmsnorm(c_q, g_q) @ w_uq).reshape(B, S, H, MLA_NOPE_DIM + MLA_ROPE_DIM)
    q_nope, q_rope = q[..., :MLA_NOPE_DIM], q[..., MLA_NOPE_DIM:]
    q_rope = apply_rope(q_rope, cos[:, :, None], sin[:, :, None])
    kv = (rmsnorm(c_kv, g_kv) @ w_ukv).reshape(B, S, H, MLA_NOPE_DIM + MLA_V_DIM)
    k_nope, v = kv[..., :MLA_NOPE_DIM], kv[..., MLA_NOPE_DIM:]
    k_r = apply_rope(k_rope, cos, sin)
    nblk = S // Q_BLOCK
    scale = (MLA_NOPE_DIM + MLA_ROPE_DIM) ** -0.5
    qn = q_nope.reshape(B, nblk, Q_BLOCK, H, MLA_NOPE_DIM).transpose(1, 0, 3, 2, 4)
    qr = q_rope.reshape(B, nblk, Q_BLOCK, H, MLA_ROPE_DIM).transpose(1, 0, 3, 2, 4)

    def one_block(args):
        qn_b, qr_b = args
        s = (jnp.einsum('bhqd,bkhd->bhqk', qn_b, k_nope)
             + jnp.einsum('bhqr,bkr->bhqk', qr_b, k_r))
        p = jax.nn.softmax(s.astype(jnp.float32) * scale, axis=-1).astype(v.dtype)
        return jnp.einsum('bhqk,bkhd->bqhd', p, v)

    out = lax.map(one_block, (qn, qr))
    return out.transpose(1, 0, 2, 3, 4).reshape(B, S, H * MLA_V_DIM)

def first_inputs(seed: int = 0) -> dict:
    key = jax.random.key(seed)
    ks = jax.random.split(key, 24)
    L, D = DEPTH, D_MODEL

    def w(k, shape, fan_in):
        return jax.random.normal(k, shape, jnp.float32) * (fan_in ** -0.5)

    def gain(k, shape):
        return 1.0 + 0.05 * jax.random.normal(k, shape, jnp.float32)

    x = jax.random.normal(ks[0], (BATCH, SEQ, D), jnp.float32)
    c = jax.random.normal(ks[1], (BATCH, D), jnp.float32)
    offset = jax.random.randint(ks[2], (BATCH, 1), 0, 1024, dtype=jnp.int32)
    positions = offset + jnp.arange(SEQ, dtype=jnp.int32)[None, :]
    return {
        "x": x,
        "c": c,
        "positions": positions,
        "w_ada": w(ks[3], (L, D, 6 * D), D),
        "b_ada": 0.02 * jax.random.normal(ks[4], (L, 6 * D), jnp.float32),
        "g_mix": gain(ks[5], (L, D)),
        "w_in": w(ks[6], (L, D, IN_COLS), D),
        "b_gate": 0.02 * jax.random.normal(ks[7], (L, 2 * D), jnp.float32),
        "rpb": 0.05 * jax.random.normal(ks[8], (L, NA_HEADS, RPB_ROWS, RPB_COLS), jnp.float32),
        "g_q": gain(ks[9], (L, MLA_Q_RANK)),
        "w_uq": w(ks[10], (L, MLA_Q_RANK, MLA_HEADS * (MLA_NOPE_DIM + MLA_ROPE_DIM)), MLA_Q_RANK),
        "g_kv": gain(ks[11], (L, MLA_KV_RANK)),
        "w_ukv": w(ks[12], (L, MLA_KV_RANK, MLA_HEADS * (MLA_NOPE_DIM + MLA_V_DIM)), MLA_KV_RANK),
        "w_br_na": w(ks[13], (L, NA_WIDTH, D), NA_WIDTH),
        "w_br_mla": w(ks[14], (L, MLA_WIDTH, D), MLA_WIDTH),
        "w_out": w(ks[15], (L, D, D), D),
        "g_mlp": gain(ks[16], (L, D)),
        "w_ff1": w(ks[17], (L, D, D_FF), D),
        "w_ff2": w(ks[18], (L, D_FF, D), D_FF),
        "g_final": gain(ks[19], (D,)),
    }

def first_block(x, c, positions, w_ada, b_ada, g_mix, w_in, b_gate, rpb, g_q, w_uq, g_kv, w_ukv,
              w_br_na, w_br_mla, w_out, g_mlp, w_ff1, w_ff2, g_final):
    B, S, D = x.shape
    cos, sin = rope_tables(positions, x.dtype)
    c_act = jax.nn.silu(c)
    for l in range(DEPTH):
        mod = c_act @ w_ada[l] + b_ada[l]
        shift_a, scale_a, gate_a, shift_m, scale_m, gate_m = jnp.split(mod, 6, axis=-1)

        h = rmsnorm(x, g_mix[l]) * (1.0 + scale_a[:, None]) + shift_a[:, None]
        proj = h @ w_in[l]
        q_na, k_na, v_na, c_q, c_kv, k_rope, gate_logits = split_cols(proj, IN_SIZES)
        hd = (B, S, NA_HEADS, NA_HEAD_DIM)
        o_na = neighborhood_attention(q_na.reshape(hd), k_na.reshape(hd), v_na.reshape(hd), rpb[l])
        o_mla = mla_attention(c_q, c_kv, k_rope, w_uq[l], w_ukv[l], g_q[l], g_kv[l], cos, sin)
        gates = jax.nn.sigmoid((gate_logits + b_gate[l]).astype(jnp.float32)).astype(x.dtype)
        g_na, g_mla = gates[..., :D], gates[..., D:]
        merged = g_na * (o_na @ w_br_na[l]) + g_mla * (o_mla @ w_br_mla[l])
        x = x + gate_a[:, None] * (merged @ w_out[l])

        h = rmsnorm(x, g_mlp[l]) * (1.0 + scale_m[:, None]) + shift_m[:, None]
        x = x + gate_m[:, None] * (jnp.square(jax.nn.relu(h @ w_ff1[l])) @ w_ff2[l])
    return rmsnorm(x, g_final)


DEPTH_2 = 1

HEAD_DIM = 64
MIX_WIDTH = D_MODEL
GROUP_WIDTH = MIX_WIDTH // 4
CONV_WIDTH = 3
POOL_WINDOWS = (2, 4, 8, 16)
POOL_GROUP = GROUP_WIDTH // len(POOL_WINDOWS)
DSA_HEADS = GROUP_WIDTH // HEAD_DIM
IDX_HEADS = 8
IDX_DIM = 64
DSA_TOPK_MAX = 256
MOBA_HEADS = GROUP_WIDTH // HEAD_DIM
MOBA_BLOCK = 256
MOBA_TOPB_MAX = 3
REL_BUCKETS = 32
REL_MAX_DIST = 128
N_ATTN_HEADS = DSA_HEADS + MOBA_HEADS
D_FF_2 = -(-8 * D_MODEL // (3 * 256)) * 256
PLE_DIM = 256
MOBA_Q_BLOCK = 64
RMS_EPS = 1e-6
SPLIT_SIZES = (GROUP_WIDTH, GROUP_WIDTH, GROUP_WIDTH,
               GROUP_WIDTH,
               GROUP_WIDTH, GROUP_WIDTH, GROUP_WIDTH, IDX_HEADS * IDX_DIM, IDX_DIM, IDX_HEADS,
               GROUP_WIDTH, GROUP_WIDTH, GROUP_WIDTH)
IN_COLS_2 = sum(SPLIT_SIZES)


def rmsnorm_2(x, g):
    x32 = x.astype(jnp.float32)
    y = x32 * lax.rsqrt(jnp.mean(x32 * x32, axis=-1, keepdims=True) + RMS_EPS)
    return (y * g.astype(jnp.float32)).astype(x.dtype)

def rel_bucket(dist):
    n = jnp.maximum(dist, 0)
    max_exact = REL_BUCKETS // 2
    nf = jnp.maximum(n, 1).astype(jnp.float32)
    large = max_exact + (jnp.log(nf / max_exact) / math.log(REL_MAX_DIST / max_exact)
                         * (REL_BUCKETS - max_exact)).astype(jnp.int32)
    large = jnp.minimum(large, REL_BUCKETS - 1)
    return jnp.where(n < max_exact, n, large)

def short_conv_mixer(a_in, gate_c, gate_b, conv_w):
    h = gate_c * a_in
    y = lax.conv_general_dilated(h, conv_w[:, None, :].astype(h.dtype), window_strides=(1,),
                                 padding=[(CONV_WIDTH - 1, 0)],
                                 dimension_numbers=("NWC", "WIO", "NWC"),
                                 feature_group_count=h.shape[-1])
    return gate_b * y

def pool_mixer(v, pool_w, pool_scale):
    b, s, _ = v.shape
    v32 = v.astype(jnp.float32)
    cs = jnp.concatenate([jnp.zeros((b, 1, GROUP_WIDTH), jnp.float32), lax.cumsum(v32, axis=1)], axis=1)
    t = jnp.arange(s)
    outs = []
    for g, w in enumerate(POOL_WINDOWS):
        sl = slice(g * POOL_GROUP, (g + 1) * POOL_GROUP)
        c = cs[:, :, sl]
        upper = c[:, 1:]
        lower = jnp.concatenate([jnp.zeros((b, w - 1, POOL_GROUP), jnp.float32), c[:, :s + 1 - w]], axis=1)
        cnt = jnp.minimum(t + 1, w).astype(jnp.float32)[None, :, None]
        outs.append((upper - lower) / cnt - v32[:, :, sl])
    d = jnp.stack(outs, axis=2)
    y = jnp.einsum("bsgc,gcd->bsgd", d, pool_w.astype(jnp.float32)).reshape(b, s, GROUP_WIDTH)
    return (y * pool_scale.astype(jnp.float32)).astype(v.dtype)

def dsa_mixer(q, k, v, iq, ik, iw, bias_tab):
    b, s, nh, hd = q.shape
    topk = min(DSA_TOPK_MAX, s // 4)
    idx_scale = (IDX_HEADS ** -0.5) * (IDX_DIM ** -0.5)
    ik32 = ik.astype(jnp.float32)
    bidx = jnp.arange(b)[:, None, None]
    spos = jnp.arange(s)

    def chunk(c):
        t0 = c * Q_BLOCK
        tq = t0 + jnp.arange(Q_BLOCK)
        qc = lax.dynamic_slice_in_dim(q, t0, Q_BLOCK, axis=1).astype(jnp.float32)
        iqc = lax.dynamic_slice_in_dim(iq, t0, Q_BLOCK, axis=1).astype(jnp.float32)
        iwc = lax.dynamic_slice_in_dim(iw, t0, Q_BLOCK, axis=1).astype(jnp.float32)
        sc = jax.nn.relu(jnp.einsum("bqhd,bsd->bqhs", iqc, ik32))
        score = jnp.einsum("bqh,bqhs->bqs", iwc, sc) * idx_scale
        score = jnp.where(spos[None, None, :] <= tq[None, :, None], score, -jnp.inf)
        _, sel = lax.top_k(score, topk)
        valid = sel <= tq[None, :, None]
        kg = k[bidx, sel].astype(jnp.float32)
        vg = v[bidx, sel].astype(jnp.float32)
        logits = jnp.einsum("bqhd,bqkhd->bhqk", qc, kg) * (hd ** -0.5)
        bias = jnp.moveaxis(bias_tab.astype(jnp.float32)[:, rel_bucket(tq[None, :, None] - sel)], 0, 1)
        logits = jnp.where(valid[:, None], logits + bias, -jnp.inf)
        probs = jax.nn.softmax(logits, axis=-1)
        return jnp.einsum("bhqk,bqkhd->bqhd", probs, vg)

    out = lax.map(chunk, jnp.arange(s // Q_BLOCK))
    return out.transpose(1, 0, 2, 3, 4).reshape(b, s, nh * hd).astype(q.dtype)

def moba_mixer(q, k, v, bias_tab):
    b, s, nh, hd = q.shape
    nb = -(-s // MOBA_BLOCK)
    pad = nb * MOBA_BLOCK - s
    kp = jnp.pad(k, ((0, 0), (0, pad), (0, 0), (0, 0)))
    vp = jnp.pad(v, ((0, 0), (0, pad), (0, 0), (0, 0)))
    kblk = kp.reshape(b, nb, MOBA_BLOCK, nh, hd)
    kmean = jnp.mean(kblk.astype(jnp.float32), axis=2)
    kblk_t = kblk.transpose(0, 3, 1, 2, 4)
    vblk_t = vp.reshape(b, nb, MOBA_BLOCK, nh, hd).transpose(0, 3, 1, 2, 4)
    topb = min(MOBA_TOPB_MAX, nb - 1)
    scale = hd ** -0.5
    tab = bias_tab.astype(jnp.float32)
    bi = jnp.arange(b)[:, None, None, None]
    hi = jnp.arange(nh)[None, :, None, None]
    blk_off = jnp.arange(MOBA_BLOCK)

    def chunk(c):
        t0 = c * MOBA_Q_BLOCK
        tq = t0 + jnp.arange(MOBA_Q_BLOCK)
        ob = t0 // MOBA_BLOCK
        qc = lax.dynamic_slice_in_dim(q, t0, MOBA_Q_BLOCK, axis=1).astype(jnp.float32)
        ko = lax.dynamic_slice_in_dim(kp, ob * MOBA_BLOCK, MOBA_BLOCK, axis=1).astype(jnp.float32)
        vo = lax.dynamic_slice_in_dim(vp, ob * MOBA_BLOCK, MOBA_BLOCK, axis=1).astype(jnp.float32)
        spos_o = ob * MOBA_BLOCK + blk_off
        lo = jnp.einsum("bqhd,bshd->bhqs", qc, ko) * scale + tab[:, rel_bucket(tq[:, None] - spos_o[None, :])][None]
        lo = jnp.where((spos_o[None, :] <= tq[:, None])[None, None], lo, -jnp.inf)
        if topb == 0:
            po = jax.nn.softmax(lo, axis=-1)
            return jnp.einsum("bhqs,bshd->bqhd", po, vo)
        gate = jnp.einsum("bqhd,bnhd->bhqn", qc, kmean)
        gate = jnp.where(jnp.arange(nb)[None, None, None, :] < ob, gate, -jnp.inf)
        _, sel = lax.top_k(gate, topb)
        valid = sel < ob
        kg = kblk_t[bi, hi, sel].astype(jnp.float32)
        vg = vblk_t[bi, hi, sel].astype(jnp.float32)
        lp = jnp.einsum("bqhd,bhqnsd->bhqns", qc, kg) * scale
        spos_p = sel[..., None] * MOBA_BLOCK + blk_off
        lp = lp + tab[hi[..., None], rel_bucket(tq[None, None, :, None, None] - spos_p)]
        lp = jnp.where(valid[..., None], lp, -jnp.inf)
        npast = topb * MOBA_BLOCK
        logits = jnp.concatenate([lp.reshape(b, nh, MOBA_Q_BLOCK, npast), lo], axis=-1)
        probs = jax.nn.softmax(logits, axis=-1)
        pp = probs[..., :npast].reshape(b, nh, MOBA_Q_BLOCK, topb, MOBA_BLOCK)
        po = probs[..., npast:]
        return (jnp.einsum("bhqns,bhqnsd->bqhd", pp, vg) + jnp.einsum("bhqs,bshd->bqhd", po, vo))

    out = lax.map(chunk, jnp.arange(s // MOBA_Q_BLOCK))
    return out.transpose(1, 0, 2, 3, 4).reshape(b, s, nh * hd).astype(q.dtype)

def swiglu(h, w_gate_up, w_down):
    gu = h @ w_gate_up
    gate, up = jnp.split(gu, 2, axis=-1)
    return (jax.nn.silu(gate) * up) @ w_down

def second_inputs(seed: int = 0) -> dict:
    key = jax.random.key(seed)
    ks = jax.random.split(key, 20)
    f32 = jnp.float32

    def nrm(k, shape, scale):
        return jax.random.normal(k, shape, f32) * scale

    def gain(k, shape):
        return 1.0 + 0.05 * jax.random.normal(k, shape, f32)

    return {
        "x": nrm(ks[0], (BATCH, SEQ, D_MODEL), 1.0),
        "p": nrm(ks[1], (DEPTH_2, BATCH, SEQ, PLE_DIM), 1.0),
        "rel_bias": nrm(ks[2], (N_ATTN_HEADS, REL_BUCKETS), 0.5),
        "g_mix_pre": gain(ks[3], (DEPTH_2, D_MODEL)),
        "w_in": nrm(ks[4], (DEPTH_2, D_MODEL, IN_COLS_2), D_MODEL ** -0.5),
        "conv_w": nrm(ks[5], (DEPTH_2, CONV_WIDTH, GROUP_WIDTH), CONV_WIDTH ** -0.5),
        "pool_w": nrm(ks[6], (DEPTH_2, len(POOL_WINDOWS), POOL_GROUP, POOL_GROUP), POOL_GROUP ** -0.5),
        "pool_scale": gain(ks[7], (DEPTH_2, GROUP_WIDTH)),
        "w_out": nrm(ks[8], (DEPTH_2, MIX_WIDTH, D_MODEL), MIX_WIDTH ** -0.5),
        "g_mix_post": gain(ks[9], (DEPTH_2, D_MODEL)),
        "g_ffn_pre": gain(ks[10], (DEPTH_2, D_MODEL)),
        "w_gate_up": nrm(ks[11], (DEPTH_2, D_MODEL, 2 * D_FF_2), D_MODEL ** -0.5),
        "w_down": nrm(ks[12], (DEPTH_2, D_FF_2, D_MODEL), D_FF_2 ** -0.5),
        "g_ffn_post": gain(ks[13], (DEPTH_2, D_MODEL)),
        "g_ple": gain(ks[14], (DEPTH_2, D_MODEL)),
        "w_ple_gate": nrm(ks[15], (DEPTH_2, D_MODEL, D_MODEL), D_MODEL ** -0.5),
        "w_ple_proj": nrm(ks[16], (DEPTH_2, PLE_DIM, D_MODEL), PLE_DIM ** -0.5),
    }

def second_block(x, p, rel_bias, g_mix_pre, w_in, conv_w, pool_w, pool_scale, w_out, g_mix_post,
              g_ffn_pre, w_gate_up, w_down, g_ffn_post, g_ple, w_ple_gate, w_ple_proj):
    b, s, _ = x.shape
    split_at = tuple(int(o) for o in np.cumsum(SPLIT_SIZES)[:-1])

    def heads(t):
        return t.reshape(b, s, -1, HEAD_DIM)

    for i in range(DEPTH_2):
        h = rmsnorm_2(x, g_mix_pre[i])
        z = h @ w_in[i]
        (a_in, a_c, a_b, pv, cq, ck, cv, iq, ik, iw, dq, dk, dv) = jnp.split(z, split_at, axis=-1)
        ya = short_conv_mixer(a_in, a_c, a_b, conv_w[i])
        yb = pool_mixer(pv, pool_w[i], pool_scale[i])
        yc = dsa_mixer(heads(cq), heads(ck), heads(cv), iq.reshape(b, s, IDX_HEADS, IDX_DIM), ik, iw,
                       rel_bias[:DSA_HEADS])
        yd = moba_mixer(heads(dq), heads(dk), heads(dv), rel_bias[DSA_HEADS:])
        mix = jnp.concatenate([ya, yb, yc, yd], axis=-1) @ w_out[i]
        x = x + rmsnorm_2(mix, g_mix_post[i])
        f = swiglu(rmsnorm_2(x, g_ffn_pre[i]), w_gate_up[i], w_down[i])
        x = x + rmsnorm_2(f, g_ffn_post[i])
        gate = jax.nn.sigmoid(rmsnorm_2(x, g_ple[i]) @ w_ple_gate[i])
        x = x + gate * (p[i] @ w_ple_proj[i])
    return x


def setup_inputs(seed=0):
    out = dict(first_inputs(seed))
    for name, value in second_inputs(seed + 1).items():
        if name != "x":
            out[name + "_2"] = value
    return out


def reference(
    x, c, positions, w_ada, b_ada, g_mix, w_in, b_gate, rpb, g_q, w_uq, g_kv, w_ukv, w_br_na,
    w_br_mla, w_out, g_mlp, w_ff1, w_ff2, g_final, p_2, rel_bias_2, g_mix_pre_2, w_in_2,
    conv_w_2, pool_w_2, pool_scale_2, w_out_2, g_mix_post_2, g_ffn_pre_2, w_gate_up_2, w_down_2,
    g_ffn_post_2, g_ple_2, w_ple_gate_2, w_ple_proj_2,
):
    x = first_block(
        x, c, positions, w_ada, b_ada, g_mix, w_in, b_gate, rpb, g_q, w_uq, g_kv, w_ukv,
        w_br_na, w_br_mla, w_out, g_mlp, w_ff1, w_ff2, g_final,
    )
    return second_block(
        x, p_2, rel_bias_2, g_mix_pre_2, w_in_2, conv_w_2, pool_w_2, pool_scale_2, w_out_2,
        g_mix_post_2, g_ffn_pre_2, w_gate_up_2, w_down_2, g_ffn_post_2, g_ple_2, w_ple_gate_2,
        w_ple_proj_2,
    )


_drawn_inputs = setup_inputs


def setup_inputs(seed=0):
    import zlib

    import numpy as np

    out = dict(_drawn_inputs(seed))
    spreads = {}
    factors = {'b_gate': 8.0,
     'rpb': 7.759,
     'g_q': 8.0,
     'g_kv': 3.471,
     'pool_scale_2': 3.005,
     'g_ple_2': 23.337}
    for name, (base, spread) in spreads.items():
        noise = np.random.default_rng([zlib.crc32(name.encode()), seed]).standard_normal(out[name].shape)
        drawn = base * np.exp(spread * noise) if base else spread * noise
        out[name] = __import__('jax').numpy.asarray(drawn.astype(out[name].dtype))
    for name, factor in factors.items():
        out[name] = (out[name] * factor).astype(out[name].dtype)
    return out
```

```python
from collections import Counter
from contextlib import ExitStack, contextmanager

import numpy as np

import concourse.bass as bass
from concourse import mybir

F32 = mybir.dt.float32
F32R = mybir.dt.float32r
I32 = mybir.dt.int32
ALU = mybir.AluOpType
ACT = mybir.ActivationFunctionType
AX = mybir.AxisListType

P = 128
D = 1024
S = 512
KT = D // P
TT = S // P
DEPTH = 2
CH = 2048
NEG = -1.0e30
TAKEN = -3.0e38
EPS = 1e-6
ROWS, COLS = 8, 64
NAH = MLAH = 8
HD = 64
C_Q, C_K, C_V, C_CQ, C_CKV, C_UQ, C_UKV = 0, 2, 4, 6, 7, 8, 9
C_GNA, C_BNA, C_GMLA, C_BMLA, C_OUT, C_FF = 10, 14, 16, 20, 22, 26
FFJ = 4
C_LAYER = C_FF + 8 * FFJ
C2_Z, C2_VI, C2_OUT, C2_GU, C2_DOWN, C2_PG, C2_PP, C2_END = 0, 10, 13, 17, 39, 55, 59, 60
H2T = 22
N_CHUNK = DEPTH * C_LAYER + C2_END
TOPK = 128
V_GMIX, V_GMLP, V_BG, V_GQ, V_GKV, NV1 = 0, 8, 16, 32, 34, 35
W_GF, W_PRE, W_PS, W_CW, W_MPOST, W_FPRE, W_FPOST, W_PLE, NV2 = 0, 8, 16, 18, 24, 32, 40, 48, 56
M_SHA, M_SCA, M_GA, M_SHM, M_SCM, M_GM = (NV1 + 8 * i for i in range(6))


class View:

    def __init__(self, eng, made, per, entered):
        self.eng, self.made, self.per, self.entered = eng, made, per, entered
        self.n = Counter()
        self.p = Counter()
        self.l = None
        self.j = None
        self.last = False

    def value(self, name, n):
        prologue, layer, ff = self.per.get(name, (0, 0, 0))
        if self.l is not None:
            n = self.l * (layer + FFJ * ff) + (prologue + n)
        if self.j is not None:
            n = n + self.j * ff
        return n

    def next(self, name, k=1, unit=1):
        self.n[name] += k * unit
        return self.value(name, self.n[name])

    def count(self, name, k):
        return self.value(name, self.n[name] + k)

    def skip(self, name, k=1):
        self.n[name] += k

    def own(self, name):
        return self.value(name, self.p[name])

    def tick(self, name, unit=1):
        frame = 0 if self.l is None else 3 if self.last else 2 if self.j is not None else 1
        self.made[name][frame] += unit
        self.p[name] += unit
        return unit

    @contextmanager
    def layers(self):
        self.n, self.p = Counter(), Counter()
        with self.eng.Fori(0, DEPTH) as l:
            self.l = l
            yield
        self.n, self.p = Counter(), Counter()
        self.l = DEPTH
        self.last = True

    @contextmanager
    def ff(self):
        n0, p0 = Counter(self.n), Counter(self.p)
        self.eng.sem_inc(self.entered)
        with self.eng.Fori(0, FFJ) as j:
            self.j = j
            yield
        self.j = None
        self.n, self.p = n0, p0
        for name, (_, _, ff) in self.per.items():
            self.n[name] += FFJ * ff
            self.p[name] += FFJ * ff


SIGNALS = """
x_in consts_in pos_in c_sig cact_ready ada_done ang_ready sin_done vec_ready lin_full lin_out
sq_ready sq_used std_ready scaled_ready hi_ready act_ready x_ready vodd_in bias_in s_full
max_ready exp_done p_ready pt_full pt_copied pv_done o_copied permuted rope_done osplit_hi
osplit_ready merged_ready square_ready small2_in rel_ready rel_out wide_in ix_full ix_relu ix_used
ya_ready pool_d o_hi prod_ready p_in dve_chain fin_out
""".split()


def build(nc, per, a, out):
    made = {n: [0, 0, 0, 0] for n in SIGNALS}
    with ExitStack() as ctx:
        def sem(name):
            return ctx.enter_context(nc.semaphore(name))

        x_in = sem("x_in")
        consts_in = sem("consts_in")
        pos_in = sem("pos_in")
        c_sig = sem("c_sig")
        cact_ready = sem("cact_ready")
        ada_done = sem("ada_done")
        ang_ready = sem("ang_ready")
        sin_done = sem("sin_done")
        vec_ready = sem("vec_ready")
        lin_full = sem("lin_full")
        lin_out = sem("lin_out")
        sq_ready = sem("sq_ready")
        sq_used = sem("sq_used")
        std_ready = sem("std_ready")
        scaled_ready = sem("scaled_ready")
        hi_ready = sem("hi_ready")
        act_ready = sem("act_ready")
        x_ready = sem("x_ready")
        vodd_in = sem("vodd_in")
        bias_in = sem("bias_in")
        s_full = sem("s_full")
        max_ready = sem("max_ready")
        exp_done = sem("exp_done")
        p_ready = sem("p_ready")
        pt_full = sem("pt_full")
        pt_copied = sem("pt_copied")
        pv_done = sem("pv_done")
        o_copied = sem("o_copied")
        permuted = sem("permuted")
        rope_done = sem("rope_done")
        osplit_hi = sem("osplit_hi")
        osplit_ready = sem("osplit_ready")
        merged_ready = sem("merged_ready")
        square_ready = sem("square_ready")
        small2_in = sem("small2_in")
        rel_ready = sem("rel_ready")
        rel_out = sem("rel_out")
        wide_in = sem("wide_in")
        ix_full = sem("ix_full")
        ix_relu = sem("ix_relu")
        ix_used = sem("ix_used")
        ya_ready = sem("ya_ready")
        pool_d = sem("pool_d")
        o_hi = sem("o_hi")
        prod_ready = sem("prod_ready")
        p_in = sem("p_in")
        dve_chain = sem("dve_chain")
        fin_out = sem("fin_out")
        sems = dict(osplit_ready=osplit_ready, act_ready=act_ready, o_copied=o_copied)
        raw_landed = [sem(f"raw_landed{k}") for k in range(2)]
        ada_landed = [sem(f"ada_landed{k}") for k in range(4)]
        ada_used = sem("ada_used")
        w_hi = sem("w_hi")
        w_split = sem("w_split")
        mlp_entered = sem("mlp_entered")

        top = [nc.sbuf_base + (-nc.sbuf_base) % 64]

        def fixed(name, shape, dt=F32):
            t = nc.alloc_sbuf_tensor_at(name, [P] + shape, dt, offset=top[0])
            top[0] += (4 * int(np.prod(shape)) + 31) // 32 * 32
            return t

        x = fixed("x", [KT, S])
        act_hi = fixed("act_hi", [KT, S], F32R)
        act_lo = fixed("act_lo", [KT, S], F32R)
        raw = fixed("raw", [2, CH])
        whi = fixed("whi", [2, CH], F32R)
        wlo = fixed("wlo", [2, CH], F32R)
        ident = fixed("ident", [P])
        ones = fixed("ones", [P])
        sq = fixed("sq", [2, S])
        std = fixed("std", [S])
        rstd = fixed("rstd", [S])
        tmp = fixed("tmp", [2, S])
        cur = fixed("cur", [NV1 + 48])
        scl = fixed("scl", [2, KT])
        vec1 = fixed("vec1", [DEPTH, NV1])
        vec2 = fixed("vec2", [NV2])
        mod = fixed("mod", [DEPTH, 48])
        nmax = fixed("nmax", [3, 1])
        rsum = fixed("rsum", [3, 1])
        rinv = fixed("rinv", [3, 1])
        eps = fixed("eps", [1])
        iw = fixed("iw", [TT, 8])
        top8 = fixed("top8", [8])
        cosT = fixed("cosT", [S])
        sinT = fixed("sinT", [S])
        namask = fixed("namask", [3, 256])
        arena0 = top[0]
        arena_end = nc.sbuf_usable_end

        def at(name, kb, shape, dt=F32):
            off = arena0 + int(kb * 1024)
            assert off + 4 * int(np.prod(shape)) <= arena_end, (name, kb, arena0, arena_end)
            return nc.alloc_sbuf_tensor_at(name, [P] + shape, dt, offset=off)

        ada = at("ada", 0, [4, CH])
        xin = at("xin", 32, [TT, D])
        bada = at("bada", 48, [DEPTH * 48])
        cT = at("cT", 49, [KT])
        cact = at("cact", 49.25, [KT])
        csig = at("csig", 49.5, [KT])
        posi = at("posi", 50, [S], I32)
        ang = at("ang", 52, [2, S])
        kk = at("kk", 56, [2, S])
        invf = at("invf", 60, [2])
        o_na = at("o_na", 0, [4, S])
        o_mla = at("o_mla", 8, [4, S])
        QT = at("QT", 16, [4, S])
        KTn = at("KTn", 24, [4, S])
        Ve = at("Ve", 32, [TT, S])
        Vo = at("Vo", 40, [3, S])
        relt = at("relt", 46, [NAH, 384])
        comb = at("comb", 58, [2, 3, 256])
        p_sb = at("p_sb", 64, [3, S])
        pt_sb = at("pt_sb", 70, [2, S])
        s_sb = at("s_sb", 74, [2, S])
        qT = at("qT", 16, [MLAH, S])
        kT = at("kT", 32, [MLAH, S])
        Vm = at("Vm", 48, [TT, S])
        craw = at("craw", 56, [3, S])
        cn_hi = at("cn_hi", 62, [3, S], F32R)
        cn_lo = at("cn_lo", 68, [3, S], F32R)
        rraw = at("rraw", 74, [4, S])
        rmul = at("rmul", 82, [2, S])
        gsig = at("gsig", 16, [KT, S])
        os_hi = at("os_hi", 32, [4, S], F32R)
        os_lo = at("os_lo", 40, [4, S], F32R)
        merged = at("merged", 48, [KT, S])
        ybuf = at("ybuf", 64, [2, S])
        hid_hi = at("hid_hi", 16, [KT, S], F32R)
        hid_lo = at("hid_lo", 32, [KT, S], F32R)
        rel_u = at("rel_u", 68, [2, S])
        squ = at("squ", 72, [2, S])
        zc = at("zc", 0, [8, S])
        zq = at("zq", 16, [8, S])
        iq = at("iq", 32, [4, S])
        ik = at("ik", 40, [S])
        V2 = at("V2", 42, [TT, S])
        wide = at("wide", 50, [8, S])
        selm = at("selm", 66, [1152])
        ixr = at("ixr", 70.5, [2, S])
        p2_sb = at("p2_sb", 74.5, [3, S])
        pt2_sb = at("pt2_sb", 80.5, [2, S])
        s2_sb = at("s2_sb", 84.5, [2, S])
        relT = at("relT", 16, [8])
        onehot = at("onehot", 17, [S])
        relrow = at("relrow", 20, [640])
        caus = at("caus", 88.5, [P])
        poolw = at("poolw", 70.5, [2, P])
        pcnt = at("pcnt", 74.5, [2, S])
        ct = at("ct", 78.5, [3, S])
        mixr = at("mixr", 0, [KT, S])
        h2_hi = at("h2_hi", 0, [H2T, S], F32R)
        h2_lo = at("h2_lo", 44, [H2T, S], F32R)
        fraw = nc.alloc_sbuf_tensor_at("fraw", [P, KT, S], F32, offset=nc.sbuf_base + (-nc.sbuf_base) % 64 + 16384)
        pin = at("pin", 0, [TT, 256])
        pT = at("pT", 4, [2, S])
        pT_hi = at("pT_hi", 8, [2, S], F32R)
        pT_lo = at("pT_lo", 12, [2, S], F32R)
        pg = at("pg", 16, [KT, S])
        outb = at("outb", 32, [TT, D])

        ps = ctx.enter_context(nc.psum_tensor("ps", [P, 8, 512], F32))
        B_S, B_T, B_O, B_N = 2, 4, 6, 7
        relscr = nc.dram_tensor("relscr", (8, 640), F32).ap()

        def backward(t, o, n):
            a0 = t[:]
            return bass.AP(tensor=a0.tensor, offset=a0.offset + o, ap=[list(a0.ap[0]), [-1, n]])

        na_units, mla_units, b2_units = [], [], []
        for h in range(NAH):
            r0 = 64 * (h % 2)
            for q in range(TT):
                c0 = (0, 8, 24, 32)[q]
                vs = []
                for b in range(2):
                    c = c0 + 16 * b
                    vs.append((Ve if c % 16 == 0 else Vo)[:, c // 16, h * HD:(h + 1) * HD])
                na_units.append(dict(
                    q=QT[r0:r0 + 64, h // 2, q * P:(q + 1) * P],
                    k=KTn[r0:r0 + 64, h // 2, 8 * c0:8 * c0 + 256],
                    n=256, bias=comb[:, h % 2, (0, 1, 1, 2)[q], :], sel=None, v=vs, head=h, t=q))
        for h in range(MLAH):
            for q in range(TT):
                mla_units.append(dict(
                    q=qT[0:96, h, q * P:(q + 1) * P], k=kT[0:96, h, :], n=S, bias=None, sel=None,
                    v=[Vm[:, b, h * HD:(h + 1) * HD] for b in range(TT)], head=h, t=q))
        for h in [4, 5, 6, 7, 0, 1, 2, 3]:
            r0 = 64 * (h % 2)
            zt = (0 if h < 4 else 4) + (h % 4) // 2
            for q in range(TT):
                n = P * (q + 1)
                s0 = (0, 0, 256, 640)[q]
                b2_units.append(dict(
                    q=zq[r0:r0 + 64, zt, q * P:(q + 1) * P], k=zq[r0:r0 + 64, zt + 2, 0:n], n=n,
                    bias=backward(wide, h * S + n - 1, n), sel=selm[:, s0:s0 + n] if h < 4 and q else None,
                    v=[V2[:, b, h * HD:(h + 1) * HD] for b in range(q + 1)], head=h, t=q))

        def rpb_rows(l, h):
            o = a["rpb_rev"][bass.ds(l, 1), h]
            return bass.AP(tensor=o.tensor, offset=o.offset + 33, ap=[[1, 16], [48, 8], [1, 384]])

        def rel_wide(h):
            return bass.AP(tensor=relscr.tensor, offset=640 * h, ap=[[1, P], [1, S]])

        block = ctx.enter_context(nc.Block())

        @block.sync
        def _(sp):
            v = View(sp, made, per, mlp_entered)
            xv = a["x"].rearrange("o (r c) d -> (o c) r d", r=ROWS)
            for t in range(TT):
                sp.dma_start(xin[:, t, :], xv[16 * t:16 * t + 16]).then_inc(x_in, v.tick("x_in", 16))
            for dst, src in ((ident, "ident"), (ones, "ones"), (namask, "namask"), (vec1, "vec1"),
                             (vec2, "vec2"), (bada, "bada"), (cT, "cT"), (invf, "invf")):
                sp.dma_start(dst[:], a[src]).then_inc(consts_in, v.tick("consts_in", 16))
            sp.dma_start(posi[:], a["positions"].broadcast_to((P, S))).then_inc(pos_in, v.tick("pos_in", 16))
            for k in range(2):
                sp.dma_start(raw[:, k, :], a["w_stream"][k]).then_inc(raw_landed[k], 16)
            for k in range(4):
                sp.dma_start(ada[:, k, :], a["w_ada"][k]).then_inc(ada_landed[k], 16)
            with sp.Fori(1, 12) as i:
                for k in range(4):
                    sp.wait_ge(ada_used, 4 * i + (k - 3))
                    sp.dma_start(ada[:, k, :], a["w_ada"][bass.ds(4 * i + k, 1)]
                                 .rearrange("o p f -> (o p) f")).then_inc(ada_landed[k], 16)
            with sp.Fori(1, N_CHUNK // 2) as i:
                for k in range(2):
                    sp.wait_ge(w_split, 2 * i + (k - 1))
                    sp.dma_start(raw[:, k, :], a["w_stream"][bass.ds(2 * i + k, 1)]
                                 .rearrange("o p f -> (o p) f")).then_inc(raw_landed[k], 16)

        @block.gpsimd
        def _(pool):
            with pool.Fori(0, N_CHUNK // 2) as i:
                for k in range(2):
                    pool.wait_ge(w_hi, 2 * i + (k + 1))
                    nc.gpsimd.tensor_tensor(wlo[:, k, :], raw[:, k, :], whi[:, k, :].bitcast(F32),
                                            ALU.subtract).then_inc(w_split, 1)

        @block.scalar
        def _(act):
            v = View(act, made, per, mlp_entered)
            sc = nc.scalar

            def split_hi(c):
                k = c % 2
                if v.l is None:
                    n = 16 * (c // 2 + 1)
                else:
                    if v.last and c >= C2_END:
                        return
                    n = v.l * (8 * C_LAYER) + 16 * (c // 2 + 1)
                    if v.j is not None:
                        n = n + v.j * 64
                act.wait_ge(raw_landed[k], n)
                sc.activation(whi[:, k, :], raw[:, k, :], ACT.Copy).then_inc(w_hi, 1)

            def evac(i, dst, func=ACT.Copy, rows=slice(0, P), cols=S, **kw):
                act.wait_ge(lin_full, v.next("lin_full"))
                sc.activation(dst, ps[rows, i % 2, 0:cols], func, **kw).then_inc(lin_out, v.tick("lin_out"))
                act.wait_ge(lin_out, v.own("lin_out"))
                v.skip("lin_out")

            def norm(n_tiles, src, dim, hi=None, shift=None):
                for t in range(n_tiles):
                    if t >= 2:
                        act.wait_ge(sq_used, v.next("sq_used"))
                    sc.activation(sq[:, t % 2, :], src(t), ACT.Square).then_inc(sq_ready, v.tick("sq_ready"))
                    act.wait_ge(sq_ready, v.own("sq_ready"))
                act.wait_ge(sq_used, v.next("sq_used", min(2, n_tiles)))
                sc.activation(std[:], ps[:, B_N, :], ACT.Sqrt, bias=eps[:, 0:1],
                                       scale=1.0 / dim).then_inc(std_ready, v.tick("std_ready"))
                act.wait_ge(std_ready, v.own("std_ready"))
                for t in range(n_tiles if hi else 0):
                    act.wait_ge(scaled_ready, v.next("scaled_ready"))
                    if shift is None:
                        ins = sc.activation(hi(t), tmp[:, t % 2, :], ACT.Copy)
                    else:
                        ins = sc.activation(hi(t), tmp[:, t % 2, :], ACT.Identity, bias=shift(t))
                    ins.then_inc(hi_ready, v.tick("hi_ready"))
                    act.wait_ge(hi_ready, v.own("hi_ready"))

            def attend(units, p, pt, sb):
                for i in range(len(units) + 3):
                    if i < len(units):
                        n = units[i]["n"]
                        act.wait_ge(max_ready, v.count("max_ready", i + 1))
                        src = ps[:, B_S + i % 2, 0:n] if units[i]["bias"] is None else sb[:, i % 2, 0:n]
                        sc.activation(p[:, i % 3, 0:n], src, ACT.Exp, bias=nmax[:, i % 3, :],
                                               accum_out=rsum[:, i % 3, :]).then_inc(exp_done, v.tick("exp_done"))
                        act.wait_ge(exp_done, v.own("exp_done"))
                    w = i - 2
                    if 0 <= w < len(units):
                        n = units[w]["n"]
                        act.wait_ge(pt_full, v.count("pt_full", w + 1))
                        if w >= 2:
                            act.wait_ge(pv_done, v.count("pv_done", w - 1))
                        sc.activation(pt[:, w % 2, 0:n], ps[:, B_T + w % 2, 0:n], ACT.Copy).then_inc(pt_copied, v.tick("pt_copied"))
                        act.wait_ge(pt_copied, v.own("pt_copied"))
                    w = i - 3
                    if units is b2_units and w >= 0 and w % 8 == 7:
                        act.wait_ge(pv_done, v.count("pv_done", w + 1))
                        t = (6, 7, 4, 5)[w // 8]
                        sc.activation(act_hi[:, t, :], ps[:, B_O, :], ACT.Copy).then_inc(o_hi, v.tick("o_hi"))
                        act.wait_ge(o_hi, v.own("o_hi"))
                v.skip("max_ready", len(units))
                v.skip("pt_full", len(units))
                v.skip("pv_done", len(units))
                act.wait_ge(o_copied, v.next("o_copied", len(units) // 8))

            act.wait_ge(consts_in, v.next("consts_in", 8, 16))
            sc.activation(csig[:], cT[:], ACT.Sigmoid).then_inc(c_sig, v.tick("c_sig"))
            act.wait_ge(c_sig, v.own("c_sig"))
            act.wait_ge(ang_ready, v.next("ang_ready"))
            sc.activation(sinT[:], ang[:, 0, :], ACT.Sin)
            sc.activation(cosT[:], ang[:, 1, :], ACT.Sin).then_inc(sin_done, v.tick("sin_done"))
            act.wait_ge(sin_done, v.own("sin_done"))
            for t in range(KT):
                evac(t, x[:, t, :])
            act.wait_ge(lin_out, v.count("lin_out", 0))
            for c in range(2):
                split_hi(c)

            with v.layers():
                act.wait_ge(vec_ready, v.next("vec_ready"))
                for h in range(NAH):
                    act.dma_start(relt[:, h, :], rpb_rows(v.l, h)).then_inc(bias_in, v.tick("bias_in", 16))
                norm(KT, lambda t: x[:, t, :], D, hi=lambda t: act_hi[:, t, :],
                     shift=lambda t: cur[:, M_SHA + t:M_SHA + t + 1])
                n = 0
                for c in range(C_Q, C_V):
                    for i in range(2):
                        evac(n, (QT if c < C_K else KTn)[:, 2 * (c % 2) + i, :],
                             scale=HD ** -0.5 if c < C_K else 1.0)
                        n += 1
                    split_hi(c + 2)
                for c in range(C_V, C_CQ):
                    for t in range(TT):
                        evac(n, Ve[:, t, 256 * (c - C_V):256 * (c - C_V) + 256], cols=256)
                        n += 1
                    split_hi(c + 2)
                for o in range(3):
                    act.dma_start(Vo[0:64, o, :], Ve[64:128, o, :]).then_inc(vodd_in, v.tick("vodd_in", 16))
                    act.dma_start(Vo[64:128, o, :], Ve[0:64, o + 1, :]).then_inc(vodd_in, v.tick("vodd_in", 16))
                attend(na_units, p_sb, pt_sb, s_sb)
                for i in range(4):
                    if i < 3:
                        evac(n, craw[:, i, :])
                    else:
                        evac(n, rraw[0:64, 2, :], rows=slice(0, 64))
                    n += 1
                    if i % 2:
                        split_hi(C_CQ + i // 2 + 2)
                norm(2, lambda t: craw[:, t, :], 256, hi=lambda t: cn_hi[:, t, :])
                norm(1, lambda t: craw[:, 2, :], 128, hi=lambda t: cn_hi[:, 2, :])
                for t in range(4):
                    act.wait_ge(lin_full, v.next("lin_full"))
                    b = ps[:, n % 2, :]
                    sc.activation(qT[0:64, 2 * t, :], b[0:64, :], ACT.Copy, scale=96 ** -0.5)
                    sc.activation(qT[0:64, 2 * t + 1, :], b[64:128, :], ACT.Copy,
                                           scale=96 ** -0.5).then_inc(lin_out, v.tick("lin_out"))
                    act.wait_ge(lin_out, v.own("lin_out"))
                    v.skip("lin_out")
                    n += 1
                act.wait_ge(rope_done, v.next("rope_done"))
                for t in range(4):
                    evac(n, rraw[:, t, :], scale=96 ** -0.5)
                    n += 1
                split_hi(C_UQ + 2)
                for t in range(4):
                    act.wait_ge(lin_full, v.next("lin_full"))
                    b = ps[:, n % 2, :]
                    sc.activation(kT[0:64, 2 * t, :], b[0:64, :], ACT.Copy)
                    sc.activation(kT[0:64, 2 * t + 1, :], b[64:128, :], ACT.Copy).then_inc(lin_out, v.tick("lin_out"))
                    act.wait_ge(lin_out, v.own("lin_out"))
                    v.skip("lin_out")
                    n += 1
                for t in range(TT):
                    evac(n, Vm[:, t, :])
                    n += 1
                split_hi(C_UKV + 2)
                act.wait_ge(rope_done, v.next("rope_done"))
                attend(mla_units, p_sb, pt_sb, s_sb)
                for br in range(2):
                    for t in range(4):
                        sc.activation(os_hi[:, t, :], (o_na, o_mla)[br][:, t, :], ACT.Copy).then_inc(osplit_hi, v.tick("osplit_hi"))
                        act.wait_ge(osplit_hi, v.own("osplit_hi"))
                    for c in range(4):
                        for i in range(2):
                            t = 2 * c + i
                            k = V_BG + 8 * br + t
                            evac(n, gsig[:, t, :], ACT.Sigmoid, bias=cur[:, k:k + 1])
                            n += 1
                        split_hi((C_GNA, C_GMLA)[br] + c + 2)
                    for c in range(2):
                        for i in range(4):
                            t = 4 * c + i
                            if t >= 2:
                                act.wait_ge(merged_ready, v.next("merged_ready"))
                            evac(n, ybuf[:, t % 2, :])
                            n += 1
                        split_hi((C_BNA, C_BMLA)[br] + c + 2)
                    act.wait_ge(merged_ready, v.next("merged_ready", 2))
                for t in range(KT):
                    sc.activation(act_hi[:, t, :], merged[:, t, :], ACT.Copy).then_inc(hi_ready, v.tick("hi_ready"))
                    act.wait_ge(hi_ready, v.own("hi_ready"))

                def residual(n, c0, gate):
                    for c in range(4):
                        for i in range(2):
                            t = 2 * c + i
                            if t >= 2:
                                act.wait_ge(x_ready, v.next("x_ready"))
                            evac(n + t, ybuf[:, t % 2, :], scale=cur[:, gate + t:gate + t + 1])
                        split_hi(c0 + c + 2)
                    act.wait_ge(x_ready, v.next("x_ready", 2))

                residual(n, C_OUT, M_GA)
                n += KT
                norm(KT, lambda t: x[:, t, :], D, hi=lambda t: act_hi[:, t, :],
                     shift=lambda t: cur[:, M_SHM + t:M_SHM + t + 1])
                with v.ff():
                    for c in range(4):
                        for i in range(2):
                            t = 2 * c + i
                            evac(n + t, rel_u[:, t % 2, :], ACT.Relu)
                            if t:
                                act.wait_ge(square_ready, v.next("square_ready"))
                                sc.activation(hid_hi[:, t - 1, :], squ[:, (t - 1) % 2, :],
                                                       ACT.Copy).then_inc(hi_ready, v.tick("hi_ready"))
                                act.wait_ge(hi_ready, v.own("hi_ready"))
                        split_hi(C_FF + c + 2)
                    act.wait_ge(square_ready, v.next("square_ready"))
                    sc.activation(hid_hi[:, 7, :], squ[:, 1, :], ACT.Copy).then_inc(hi_ready, v.tick("hi_ready"))
                    act.wait_ge(hi_ready, v.own("hi_ready"))
                    residual(n + KT, C_FF + 4, M_GM)

            for dst, src in ((relT, "relT"), (onehot, "onehot"), (poolw, "poolw"), (pcnt, "pcnt"),
                             (caus, "caus")):
                d = dst[0:32] if dst is relT or dst is onehot else dst[:]
                act.dma_start(d, a[src]).then_inc(small2_in, v.tick("small2_in", 16))
            norm(KT, lambda t: x[:, t, :], D)
            for t in range(KT):
                act.wait_ge(scaled_ready, v.next("scaled_ready"))
                sc.activation(x[:, t, :].rearrange("p (r c) -> p r c", r=ROWS),
                                       tmp[:, t % 2, :].rearrange("p (c r) -> p r c", r=ROWS),
                                       ACT.Copy).then_inc(permuted, v.tick("permuted"))
                act.wait_ge(permuted, v.own("permuted"))
            act.wait_ge(permuted, v.next("permuted", KT))
            act.wait_ge(rel_ready, v.next("rel_ready"))
            act.wait_ge(lin_full, v.next("lin_full"))
            sc.activation(relrow[0:8, P - 1:P - 1 + S], ps[0:8, 0, :], ACT.Copy).then_inc(lin_out, v.tick("lin_out"))
            act.wait_ge(lin_out, v.own("lin_out"))
            act.wait_ge(lin_out, v.next("lin_out"))
            act.dma_start(relscr[:, 0:P - 1 + S], relrow[0:8, 0:P - 1 + S]).then_inc(rel_out, v.tick("rel_out", 16))
            act.wait_ge(rel_out, v.next("rel_out", 1, 16))
            for h in range(8):
                act.dma_start(wide[:, h, :], rel_wide(h)).then_inc(wide_in, v.tick("wide_in", 16))
            norm(KT, lambda t: x[:, t, :], D, hi=lambda t: act_hi[:, t, :])
            n = 1
            for c in range(10):
                for i in range(2):
                    dst = zc[:, 2 * c + i, :] if c < 4 else zq[:, 2 * c - 8 + i, :] if c < 8 \
                        else iq[:, 2 * c - 16 + i, :]
                    evac(n, dst, scale=HD ** -0.5 if c in (4, 6) else 1.0)
                    n += 1
                split_hi(c + 2)
            evac(n, ik[:])
            n += 1
            evac(n, iw[:].rearrange("p t h -> p (t h)"), cols=32, scale=8 ** -0.5 * 64 ** -0.5)
            n += 1
            split_hi(C2_VI + 2)
            for c in range(2):
                for t in range(TT):
                    evac(n, V2[:, t, 256 * c:256 * c + 256], cols=256)
                    n += 1
                split_hi(C2_VI + c + 3)
            for t in range(2):
                act.wait_ge(ya_ready, v.next("ya_ready"))
                sc.activation(act_hi[:, t, :], zc[:, t, :], ACT.Copy).then_inc(hi_ready, v.tick("hi_ready"))
                act.wait_ge(hi_ready, v.own("hi_ready"))
            for t in range(2):
                evac(n, zc[:, 6 + t, :], scale=vec2[:, W_PS + t:W_PS + t + 1])
                n += 1
            for t in range(2):
                sc.activation(act_hi[:, 2 + t, :], zc[:, 6 + t, :], ACT.Copy).then_inc(hi_ready, v.tick("hi_ready"))
                act.wait_ge(hi_ready, v.own("hi_ready"))
            for m in range(24):
                t = m // 8 + 1
                act.wait_ge(ix_full, v.next("ix_full"))
                if m >= 2:
                    act.wait_ge(ix_used, v.next("ix_used"))
                sc.activation(ixr[:, m % 2, 0:P * (t + 1)], ps[:, B_S + m % 2, 0:P * (t + 1)],
                                       ACT.Relu).then_inc(ix_relu, v.tick("ix_relu"))
                act.wait_ge(ix_relu, v.own("ix_relu"))
            act.wait_ge(ix_used, v.next("ix_used", 2))
            attend(b2_units, p2_sb, pt2_sb, s2_sb)

            def post(n, dst, n_chunks):
                for t in range(KT):
                    evac(n + t, dst[:, t, :])
                    split_hi(n_chunks(t)) if n_chunks(t) is not None else None
                norm(KT, lambda t: dst[:, t, :], D)
                act.wait_ge(x_ready, v.next("x_ready", KT))

            post(n, mixr, lambda t: C2_OUT + t // 2 + 2 if t % 2 else None)
            n += KT
            norm(KT, lambda t: x[:, t, :], D, hi=lambda t: act_hi[:, t, :])
            for c in range(H2T):
                act.wait_ge(lin_full, v.next("lin_full"))
                sc.activation(std[:], ps[:, n % 2, :], ACT.Sigmoid)
                sc.activation(sq[:, 0, :], ps[:, n % 2, :], ACT.Copy).then_inc(lin_out, v.tick("lin_out"))
                act.wait_ge(lin_out, v.own("lin_out"))
                v.skip("lin_out")
                evac(n + 1, sq[:, 1, :])
                n += 2
                split_hi(C2_GU + c + 2)
                act.wait_ge(prod_ready, v.next("prod_ready"))
                sc.activation(h2_hi[:, c, :], tmp[:, c % 2, :], ACT.Copy).then_inc(hi_ready, v.tick("hi_ready"))
                act.wait_ge(hi_ready, v.own("hi_ready"))
            for t in range(KT):
                act.wait_ge(lin_full, v.next("lin_full"))
                sc.activation(fraw[:, t, :], ps[:, n % 2, :], ACT.Copy).then_inc(lin_out, v.tick("lin_out"))
                act.wait_ge(lin_out, v.own("lin_out"))
                v.skip("lin_out")
                n += 1
                for k in range(2):
                    split_hi(C2_DOWN + 2 * t + k + 2)
            act.dma_start(pin[:], a["p_2"].rearrange("a o (t p) d -> p (a o t) d", p=P)).then_inc(p_in, v.tick("p_in", 16))
            norm(KT, lambda t: fraw[:, t, :], D)
            act.wait_ge(x_ready, v.next("x_ready", KT))
            norm(KT, lambda t: x[:, t, :], D, hi=lambda t: act_hi[:, t, :])
            for t in range(2):
                evac(n, pT[:, t, :])
                n += 1
            for t in range(2):
                sc.activation(pT_hi[:, t, :], pT[:, t, :], ACT.Copy).then_inc(hi_ready, v.tick("hi_ready"))
                act.wait_ge(hi_ready, v.own("hi_ready"))
            for c in range(4):
                for i in range(2):
                    evac(n, pg[:, 2 * c + i, :], ACT.Sigmoid)
                    n += 1
                split_hi(C2_PG + c + 2)
            for t in range(KT):
                if t >= 2:
                    act.wait_ge(x_ready, v.next("x_ready"))
                evac(n, ybuf[:, t % 2, :])
                n += 1
            act.wait_ge(x_ready, v.next("x_ready", 2))
            for t in range(TT):
                for k in range(2):
                    evac(n, outb[:, t, S * k:S * k + S])
                    n += 1
                act.dma_start(out.rearrange("o (t p) d -> t (o p) d", p=P)[t], outb[:, t, :]).then_inc(fin_out, v.tick("fin_out", 16))
            act.wait_ge(fin_out, v.next("fin_out", TT, 16))

        @block.vector
        def _(dve):
            v = View(dve, made, per, mlp_entered)
            ve = nc.vector

            def chain(ins):
                ins.then_inc(dve_chain, v.tick("dve_chain"))
                dve.wait_ge(dve_chain, v.own("dve_chain"))

            def low(dst, src, hi, done):
                ve.tensor_tensor(dst, src, hi.bitcast(F32), ALU.subtract).then_inc(sems[done], v.tick(done))
                dve.wait_ge(sems[done], v.own(done))

            def norm(n_tiles, src, scale, hi, lo, shift=None):
                dve.wait_ge(std_ready, v.next("std_ready"))
                chain(ve.reciprocal(rstd[:], std[:]))
                for t in range(n_tiles + 1):
                    if t < n_tiles:
                        ve.scalar_tensor_tensor(tmp[:, t % 2, :], src(t), scale(t), rstd[:],
                                                         ALU.mult, ALU.mult).then_inc(scaled_ready, v.tick("scaled_ready"))
                        dve.wait_ge(scaled_ready, v.own("scaled_ready"))
                    if t:
                        dve.wait_ge(hi_ready, v.next("hi_ready"))
                        h = hi(t - 1).bitcast(F32)
                        if shift is None:
                            ins = ve.tensor_tensor(lo(t - 1), tmp[:, (t - 1) % 2, :], h, ALU.subtract)
                        else:
                            ins = ve.scalar_tensor_tensor(lo(t - 1), tmp[:, (t - 1) % 2, :],
                                                          shift(t - 1), h, ALU.add, ALU.subtract)
                        ins.then_inc(act_ready, v.tick("act_ready"))
                        dve.wait_ge(act_ready, v.own("act_ready"))

            def norm_add(src, w0):
                dve.wait_ge(std_ready, v.next("std_ready"))
                chain(ve.reciprocal(rstd[:], std[:]))
                for t in range(KT):
                    chain(ve.scalar_tensor_tensor(tmp[:, t % 2, :], src[:, t, :],
                                                  vec2[:, w0 + t:w0 + t + 1], rstd[:],
                                                  ALU.mult, ALU.mult))
                    ve.tensor_tensor(x[:, t, :], x[:, t, :], tmp[:, t % 2, :], ALU.add).then_inc(x_ready, v.tick("x_ready"))
                    dve.wait_ge(x_ready, v.own("x_ready"))

            def topk_round(m):
                t = m // 16 + 1
                s0, n = (0, 256, 640)[t - 1], P * (t + 1)
                sc = selm[:, s0:s0 + n]
                if m % 16 == 0:
                    chain(ve.tensor_tensor(sc[:, n - P:n], sc[:, n - P:n], caus[:], ALU.add))
                chain(ve.max(top8[:], sc))
                chain(ve.match_replace(sc, top8[:], sc, TAKEN))
                if m % 16 == 15:
                    chain(ve.tensor_scalar(sc, sc, TAKEN, NEG, ALU.not_equal, ALU.mult))

            def bias_tables(h):
                a0 = relt[:]
                for k in range(3):
                    o = 16 - 8 * k
                    ins = ve.tensor_tensor(
                        comb[:, h % 2, k, :].rearrange("p (j i) -> p j i", i=ROWS),
                        bass.AP(tensor=a0.tensor, offset=a0.offset + 384 * h + 383 - o,
                                ap=[list(a0.ap[0]), [-1, 32], [-48, 8]]), namask[:, k, :].rearrange("p (j i) -> p j i", i=ROWS),
                        ALU.add)
                chain(ins)

            def attend(units, p, sb, obuf):
                for i in range(len(units) + 3):
                    if i < len(units):
                        u = units[i]
                        n = u["n"]
                        if units is na_units and i % TT == 0:
                            bias_tables(u["head"])
                        dve.wait_ge(s_full, v.count("s_full", i + 1))
                        src = ps[:, B_S + i % 2, 0:n]
                        if u["bias"] is not None:
                            chain(ve.tensor_tensor(sb[:, i % 2, 0:n], src, u["bias"], ALU.add))
                            src = sb[:, i % 2, 0:n]
                        if u["sel"] is not None:
                            chain(ve.tensor_tensor(src, src, u["sel"], ALU.add))
                        ve.tensor_reduce(nmax[:, i % 3, :], src, AX.X, ALU.max, negate=True).then_inc(max_ready, v.tick("max_ready"))
                        dve.wait_ge(max_ready, v.own("max_ready"))
                    if 1 <= i <= len(units):
                        w = i - 1
                        n = units[w]["n"]
                        dve.wait_ge(exp_done, v.count("exp_done", w + 1))
                        chain(ve.reciprocal(rinv[:, w % 3, :], rsum[:, w % 3, :]))
                        ve.tensor_scalar(p[:, w % 3, 0:n], p[:, w % 3, 0:n],
                                                  rinv[:, w % 3, :], None, ALU.mult).then_inc(p_ready, v.tick("p_ready"))
                        dve.wait_ge(p_ready, v.own("p_ready"))
                    w = i - 3
                    if w >= 0 and w % 8 == 7:
                        dve.wait_ge(pv_done, v.count("pv_done", w + 1))
                        if units is b2_units:
                            dve.wait_ge(o_hi, v.next("o_hi"))
                            t = (6, 7, 4, 5)[w // 8]
                            low(act_lo[:, t, :], ps[:, B_O, :], act_hi[:, t, :], "o_copied")
                        else:
                            ve.tensor_copy(obuf[:, w // 8, :], ps[:, B_O, :]).then_inc(o_copied, v.tick("o_copied"))
                            dve.wait_ge(o_copied, v.own("o_copied"))
                    if units is b2_units and i < 16:
                        for m in range(3 * i, 3 * i + 3):
                            topk_round(m)
                v.skip("s_full", len(units))
                v.skip("exp_done", len(units))
                v.skip("pv_done", len(units))

            ve.memset(eps[:], EPS)
            dve.wait_ge(c_sig, v.next("c_sig"))
            ve.tensor_tensor(cact[:], cT[:], csig[:], ALU.mult).then_inc(cact_ready, v.tick("cact_ready"))
            dve.wait_ge(cact_ready, v.own("cact_ready"))
            dve.wait_ge(pos_in, v.next("pos_in", 1, 16))
            dve.wait_ge(consts_in, v.next("consts_in", 8, 16))
            chain(ve.tensor_copy(kk[:, 0, :].rearrange("p (c r) -> p c r", r=ROWS),
                                 posi[:].rearrange("p (r c) -> p c r", r=ROWS)))
            chain(ve.tensor_scalar(ang[:, 0, :], kk[:, 0, :], invf[:, 0:1], None, ALU.mult))
            big = 12582912.0
            chain(ve.tensor_scalar(kk[:, 0, :], ang[:, 0, :], 0.5 / np.pi, 0.0, ALU.mult, ALU.add))
            chain(ve.tensor_scalar(kk[:, 1, :], ang[:, 0, :], 0.5 / np.pi, 0.25, ALU.mult, ALU.add))
            chain(ve.tensor_scalar(kk[:], kk[:], big, None, ALU.add))
            chain(ve.tensor_scalar(kk[:], kk[:], big, None, ALU.subtract))
            c1 = 6.28125
            c2 = float(np.float32(np.round((2 * np.pi - c1) * 2 ** 20) / 2 ** 20))
            c3 = float(2 * np.pi - c1 - c2)
            chain(ve.tensor_copy(ang[:, 1, :], ang[:, 0, :]))
            for c in (c1, c2, c3):
                chain(ve.scalar_tensor_tensor(ang[:], kk[:], -c, ang[:], ALU.mult, ALU.add))
            chain(ve.tensor_scalar(ang[:, 1, :], ang[:, 1, :], float(np.pi / 2), None, ALU.add))
            chain(ve.tensor_scalar(ang[:], ang[:], -3.1415925, 3.1415925, ALU.max, ALU.min))
            ve.tensor_scalar(ang[:, 0, :], ang[:, 0, :], invf[:, 1:2], None, ALU.mult).then_inc(ang_ready, v.tick("ang_ready"))
            dve.wait_ge(ang_ready, v.own("ang_ready"))
            dve.wait_ge(ada_done, v.next("ada_done"))
            chain(ve.tensor_tensor(mod[:].rearrange("p l m -> p (l m)"), ps[:, B_N, 0:96], bada[:],
                                   ALU.add))

            with v.layers():
                ve.tensor_copy(cur[:, 0:NV1], vec1[:, bass.ds(v.l, 1), :].rearrange("p o m -> p (o m)"))
                chain(ve.tensor_copy(cur[:, NV1:NV1 + 48],
                                     mod[:, bass.ds(v.l, 1), :].rearrange("p o m -> p (o m)")))
                ve.scalar_tensor_tensor(scl[:, 0, :], cur[:, M_SCA:M_SCA + 8], 1.0,
                                        cur[:, V_GMIX:V_GMIX + 8], ALU.add, ALU.mult)
                ins = ve.scalar_tensor_tensor(scl[:, 1, :], cur[:, M_SCM:M_SCM + 8], 1.0,
                                              cur[:, V_GMLP:V_GMLP + 8], ALU.add, ALU.mult)
                ins.then_inc(vec_ready, v.tick("vec_ready"))
                dve.wait_ge(vec_ready, v.own("vec_ready"))
                dve.wait_ge(vec_ready, v.next("vec_ready"))
                norm(KT, lambda t: x[:, t, :], lambda t: scl[:, 0, t:t + 1],
                     lambda t: act_hi[:, t, :], lambda t: act_lo[:, t, :],
                     lambda t: cur[:, M_SHA + t:M_SHA + t + 1])
                dve.wait_ge(bias_in, v.next("bias_in", NAH, 16))
                v.skip("lin_out", 16)
                attend(na_units, p_sb, s_sb, o_na)
                dve.wait_ge(lin_out, v.next("lin_out", 4))
                ve.tensor_tensor(rmul[0:32, 0, :], rraw[0:32, 2, :], cosT[0:32, :], ALU.mult)
                chain(ve.tensor_tensor(rmul[0:32, 1, :], rraw[32:64, 2, :], sinT[32:64, :], ALU.mult))
                for h in range(MLAH):
                    ins = ve.tensor_tensor(kT[64:96, h, :], rmul[0:32, 0, :], rmul[0:32, 1, :], ALU.add)
                ins.then_inc(rope_done, v.tick("rope_done"))
                dve.wait_ge(rope_done, v.own("rope_done"))
                for t0, k, c in ((0, 2, V_GQ), (2, 1, V_GKV)):
                    norm(k, lambda t: craw[:, t0 + t, :], lambda t: cur[:, c + t:c + t + 1],
                         lambda t: cn_hi[:, t0 + t, :], lambda t: cn_lo[:, t0 + t, :])
                dve.wait_ge(lin_out, v.next("lin_out", 8))
                for w in range(2):
                    ve.tensor_tensor(rmul[:, 0, :], rraw[:, w, :], cosT[:], ALU.mult)
                    chain(ve.tensor_tensor(rmul[:, 1, :], rraw[:, 2 + w, :], sinT[:], ALU.mult))
                    for h in range(4):
                        r = slice(32 * h, 32 * h + 32)
                        ins = ve.tensor_tensor(qT[64:96, 4 * w + h, :], rmul[r, 0, :], rmul[r, 1, :],
                                               ALU.add)
                    if w == 0:
                        chain(ins)
                ins.then_inc(rope_done, v.tick("rope_done"))
                dve.wait_ge(rope_done, v.own("rope_done"))
                v.skip("lin_out", 8)
                attend(mla_units, p_sb, s_sb, o_mla)
                for br in range(2):
                    o = (o_na, o_mla)[br]
                    dve.wait_ge(lin_out, v.count("lin_out", 0))
                    for t in range(4):
                        dve.wait_ge(osplit_hi, v.next("osplit_hi"))
                        low(os_lo[:, t, :], o[:, t, :], os_hi[:, t, :], "osplit_ready")
                    v.skip("lin_out", 8)
                    for t in range(KT):
                        dve.wait_ge(lin_out, v.next("lin_out"))
                        if br == 0:
                            ins = ve.tensor_tensor(merged[:, t, :], ybuf[:, t % 2, :], gsig[:, t, :],
                                                   ALU.mult)
                        else:
                            chain(ve.tensor_tensor(gsig[:, t, :], ybuf[:, t % 2, :], gsig[:, t, :],
                                                   ALU.mult))
                            ins = ve.tensor_tensor(merged[:, t, :], merged[:, t, :], gsig[:, t, :],
                                                   ALU.add)
                        ins.then_inc(merged_ready, v.tick("merged_ready"))
                        dve.wait_ge(merged_ready, v.own("merged_ready"))
                for t in range(KT):
                    dve.wait_ge(hi_ready, v.next("hi_ready"))
                    low(act_lo[:, t, :], merged[:, t, :], act_hi[:, t, :], "act_ready")

                def residual():
                    for t in range(KT):
                        dve.wait_ge(lin_out, v.next("lin_out"))
                        ve.tensor_tensor(x[:, t, :], x[:, t, :], ybuf[:, t % 2, :], ALU.add).then_inc(x_ready, v.tick("x_ready"))
                        dve.wait_ge(x_ready, v.own("x_ready"))

                residual()
                norm(KT, lambda t: x[:, t, :], lambda t: scl[:, 1, t:t + 1],
                     lambda t: act_hi[:, t, :], lambda t: act_lo[:, t, :],
                     lambda t: cur[:, M_SHM + t:M_SHM + t + 1])
                with v.ff():
                    for t in range(KT + 1):
                        if t < KT:
                            dve.wait_ge(lin_out, v.next("lin_out"))
                            ve.tensor_tensor(squ[:, t % 2, :], rel_u[:, t % 2, :],
                                                      rel_u[:, t % 2, :], ALU.mult).then_inc(square_ready, v.tick("square_ready"))
                            dve.wait_ge(square_ready, v.own("square_ready"))
                        if t:
                            dve.wait_ge(hi_ready, v.next("hi_ready"))
                            low(hid_lo[:, t - 1, :], squ[:, (t - 1) % 2, :], hid_hi[:, t - 1, :],
                                "act_ready")
                    residual()

            dve.wait_ge(std_ready, v.next("std_ready"))
            chain(ve.reciprocal(rstd[:], std[:]))
            for t in range(KT):
                if t >= 2:
                    dve.wait_ge(permuted, v.next("permuted"))
                ve.scalar_tensor_tensor(tmp[:, t % 2, :], x[:, t, :],
                                                 vec2[:, W_GF + t:W_GF + t + 1], rstd[:],
                                                 ALU.mult, ALU.mult).then_inc(scaled_ready, v.tick("scaled_ready"))
                dve.wait_ge(scaled_ready, v.own("scaled_ready"))
            dve.wait_ge(permuted, v.next("permuted", 2))
            ve.memset(relrow[0:8, 0:P - 1], NEG).then_inc(rel_ready, v.tick("rel_ready"))
            dve.wait_ge(rel_ready, v.own("rel_ready"))
            norm(KT, lambda t: x[:, t, :], lambda t: vec2[:, W_PRE + t:W_PRE + t + 1],
                 lambda t: act_hi[:, t, :], lambda t: act_lo[:, t, :])
            dve.wait_ge(small2_in, v.next("small2_in", 5, 16))
            dve.wait_ge(lin_out, v.next("lin_out", 1 + 16))
            for t in range(2):
                cw = lambda k: vec2[:, W_CW + 2 * k + t:W_CW + 2 * k + t + 1]
                chain(ve.tensor_tensor(ct[:, 0, :], zc[:, t, :], zc[:, 2 + t, :], ALU.mult))
                chain(ve.tensor_scalar(ct[:, 1, :], ct[:, 0, :], cw(2), None, ALU.mult))
                for k in (1, 0):
                    d = 2 - k
                    chain(ve.scalar_tensor_tensor(ct[:, 1, d:S], ct[:, 0, 0:S - d], cw(k),
                                                  ct[:, 1, d:S], ALU.mult, ALU.add))
                ve.tensor_tensor(zc[:, t, :], ct[:, 1, :], zc[:, 4 + t, :], ALU.mult).then_inc(ya_ready, v.tick("ya_ready"))
                dve.wait_ge(ya_ready, v.own("ya_ready"))
            for t in range(2):
                src, wins = zc[:, 6 + t, :], []
                for k in range(4 if t else 2):
                    d, dst = 2 ** k, ct[:, k % 3, :]
                    ve.tensor_copy(dst[:, 0:d], src[:, 0:d])
                    chain(ve.tensor_tensor(dst[:, d:S], src[:, d:S], src[:, 0:S - d], ALU.add))
                    src = dst
                    wins.append(dst)
                for k, r in enumerate((slice(0, 64), slice(64, P))):
                    win = wins[2 * t + k]
                    chain(ve.tensor_tensor(win[r], win[r], pcnt[r, t, :], ALU.mult))
                    ins = ve.tensor_tensor(zc[r, 6 + t, :], win[r], zc[r, 6 + t, :], ALU.subtract)
                ins.then_inc(pool_d, v.tick("pool_d"))
                dve.wait_ge(pool_d, v.own("pool_d"))
            dve.wait_ge(pool_d, v.next("pool_d", 2))
            dve.wait_ge(lin_out, v.next("lin_out", 14))
            for t in range(2):
                dve.wait_ge(hi_ready, v.next("hi_ready"))
                low(act_lo[:, t, :], zc[:, t, :], act_hi[:, t, :], "act_ready")
            dve.wait_ge(lin_out, v.next("lin_out", 2))
            for t in range(2):
                dve.wait_ge(hi_ready, v.next("hi_ready"))
                low(act_lo[:, 2 + t, :], zc[:, 6 + t, :], act_hi[:, 2 + t, :], "act_ready")
            for m in range(24):
                t, h = m // 8 + 1, m % 8
                s0, n = (0, 256, 640)[t - 1], P * (t + 1)
                sc = selm[:, s0:s0 + n]
                dve.wait_ge(ix_relu, v.next("ix_relu"))
                if h == 0:
                    ins = ve.tensor_scalar(sc, ixr[:, m % 2, 0:n], iw[:, t, 0:1], None, ALU.mult)
                else:
                    ins = ve.scalar_tensor_tensor(sc, ixr[:, m % 2, 0:n], iw[:, t, h:h + 1], sc,
                                                  ALU.mult, ALU.add)
                ins.then_inc(ix_used, v.tick("ix_used"))
                dve.wait_ge(ix_used, v.own("ix_used"))
                dve.wait_ge(ix_used, v.next("ix_used"))
            dve.wait_ge(wide_in, v.next("wide_in", 8, 16))
            attend(b2_units, p2_sb, s2_sb, None)
            v.skip("lin_out", KT)
            norm_add(mixr, W_MPOST)
            norm(KT, lambda t: x[:, t, :], lambda t: vec2[:, W_FPRE + t:W_FPRE + t + 1],
                 lambda t: act_hi[:, t, :], lambda t: act_lo[:, t, :])
            for c in range(H2T):
                dve.wait_ge(lin_out, v.next("lin_out", 2))
                chain(ve.tensor_tensor(tmp[:, c % 2, :], sq[:, 0, :], std[:], ALU.mult))
                ve.tensor_tensor(tmp[:, c % 2, :], tmp[:, c % 2, :], sq[:, 1, :], ALU.mult).then_inc(prod_ready, v.tick("prod_ready"))
                dve.wait_ge(prod_ready, v.own("prod_ready"))
                dve.wait_ge(hi_ready, v.next("hi_ready"))
                low(h2_lo[:, c, :], tmp[:, c % 2, :], h2_hi[:, c, :], "act_ready")
            v.skip("lin_out", KT)
            norm_add(fraw, W_FPOST)
            norm(KT, lambda t: x[:, t, :], lambda t: vec2[:, W_PLE + t:W_PLE + t + 1],
                 lambda t: act_hi[:, t, :], lambda t: act_lo[:, t, :])
            v.skip("lin_out", 2)
            for t in range(2):
                dve.wait_ge(hi_ready, v.next("hi_ready"))
                low(pT_lo[:, t, :], pT[:, t, :], pT_hi[:, t, :], "act_ready")
            v.skip("lin_out", KT)
            for t in range(KT):
                dve.wait_ge(lin_out, v.next("lin_out"))
                chain(ve.tensor_tensor(pg[:, t, :], pg[:, t, :], ybuf[:, t % 2, :], ALU.mult))
                ve.tensor_tensor(x[:, t, :], x[:, t, :], pg[:, t, :], ALU.add).then_inc(x_ready, v.tick("x_ready"))
                dve.wait_ge(x_ready, v.own("x_ready"))

        @block.tensor
        def _(pe):
            v = View(pe, made, per, mlp_entered)
            te = nc.tensor

            def bank(n):
                if v.n["lin_out"] >= 1:
                    pe.wait_ge(lin_out, v.count("lin_out", -1))
                v.skip("lin_out")
                return ps[:, n % 2, :]

            def chunk(c):
                n = v.l * C_LAYER + (c + 1)
                if v.j is not None:
                    n = n + v.j * 8
                pe.wait_ge(w_split, n)
                return whi[:, c % 2, :], wlo[:, c % 2, :]

            def three(out, w, a, start, stop, swap=False):
                (wh, wl), (ah, al) = w, a
                if swap:
                    (wh, wl), (ah, al) = a, w
                te.matmul(out, wh, ah, start=start, stop=False)
                te.matmul(out, wh, al, start=False, stop=False)
                return te.matmul(out, wl, ah, start=False, stop=stop)

            def linear(n, c, tiles, kts, cols, src, wait=None, each=None):
                wh, wl = chunk(c)
                for i in range(tiles):
                    b = bank(n + i)
                    for k in range(kts):
                        if i == 0 and wait is not None:
                            pe.wait_ge(sems[wait], v.next(wait))
                        o = k * cols + P * i
                        ins = three(b, (wh[:, o:o + P], wl[:, o:o + P]), src(k), k == 0, k == kts - 1)
                    ins.then_inc(lin_full, v.tick("lin_full"))
                return n + tiles

            def by_token(n, c, kts, cols, src, width):
                wh, wl = chunk(c)
                for t in range(TT):
                    b = bank(n + t)
                    for k in range(kts):
                        o = k * cols + (cols - width)
                        ah, al = src(k)
                        ins = three(b[:, 0:width], (wh[:, o:o + width], wl[:, o:o + width]),
                                    (ah[:, P * t:P * t + P], al[:, P * t:P * t + P]),
                                    k == 0, k == kts - 1, swap=True)
                    ins.then_inc(lin_full, v.tick("lin_full"))
                return n + TT

            def norm(n_tiles):
                for t in range(n_tiles):
                    pe.wait_ge(sq_ready, v.next("sq_ready"))
                    te.matmul(ps[:, B_N, :], ones[:], sq[:, t % 2, :], start=(t == 0),
                                       stop=(t == n_tiles - 1)).then_inc(sq_used, v.tick("sq_used"))

            def attend(units, p, pt):
                for i in range(len(units) + 3):
                    if i < len(units):
                        u = units[i]
                        if i >= 2:
                            pe.wait_ge(exp_done, v.count("exp_done", i - 1))
                        te.matmul(ps[:, B_S + i % 2, 0:u["n"]], u["q"], u["k"],
                                           start=True, stop=True).then_inc(s_full, v.tick("s_full"))
                    w = i - 2
                    if 0 <= w < len(units):
                        pe.wait_ge(p_ready, v.count("p_ready", w + 1))
                        if w >= 2:
                            pe.wait_ge(pt_copied, v.count("pt_copied", w - 1))
                        for b in range(units[w]["n"] // P):
                            ins = te.transpose(ps[:, B_T + w % 2, P * b:P * b + P],
                                               p[:, w % 3, P * b:P * b + P], ident[:])
                        ins.then_inc(pt_full, v.tick("pt_full"))
                    w = i - 3
                    if w >= 0:
                        u = units[w]
                        if w % 8 == 0 and w:
                            pe.wait_ge(o_copied, v.count("o_copied", w // 8))
                        pe.wait_ge(pt_copied, v.count("pt_copied", w + 1))
                        r = 64 * (u["head"] % 2)
                        o = ps[r:r + 64, B_O, P * u["t"]:P * u["t"] + P]
                        nb = u["n"] // P
                        for b in range(nb):
                            ins = te.matmul(o, u["v"][b], pt[:, w % 2, P * b:P * b + P],
                                            start=(b == 0), stop=(b == nb - 1))
                        ins.then_inc(pv_done, v.tick("pv_done"))
                for s in ("exp_done", "p_ready", "pt_copied"):
                    v.skip(s, len(units))
                pe.wait_ge(o_copied, v.next("o_copied", len(units) // 8))

            pe.wait_ge(consts_in, v.next("consts_in", 8, 16))
            pe.wait_ge(x_in, v.next("x_in", TT, 16))
            for t in range(KT):
                b = bank(t)
                for k in range(TT):
                    ins = te.transpose(b[:, P * k:P * k + P], xin[:, k, P * t:P * t + P], ident[:])
                ins.then_inc(lin_full, v.tick("lin_full"))
            pe.wait_ge(cact_ready, v.next("cact_ready"))
            with pe.Fori(0, 12) as i:
                for k in range(4):
                    pe.wait_ge(ada_landed[k], 16 * i + 16)
                    for m in range(2):
                        for kt in range(KT):
                            ins = te.matmul(ps[:, B_N, bass.ds(8 * i + (2 * k + m), 1)],
                                            ada[:, k, 256 * kt + P * m:256 * kt + P * m + P],
                                            cact[:, kt:kt + 1], start=(kt == 0), stop=(kt == KT - 1))
                    ins.then_inc(ada_used, 1)
            pe.wait_ge(ada_used, 48)
            pe.nop().then_inc(ada_done, v.tick("ada_done"))

            h = lambda k: (act_hi[:, k, :], act_lo[:, k, :])
            with v.layers():
                norm(KT)
                n = linear(0, C_Q, 2, KT, 256, h, wait="act_ready")
                for c in range(C_Q + 1, C_V):
                    n = linear(n, c, 2, KT, 256, h)
                for c in (C_V, C_V + 1):
                    n = by_token(n, c, KT, 256, h, 256)
                pe.wait_ge(lin_out, v.count("lin_out", 0))
                pe.wait_ge(vodd_in, v.next("vodd_in", 6, 16))
                attend(na_units, p_sb, pt_sb)
                n = linear(n, C_CQ, 2, KT, 256, h)
                n = linear(n, C_CKV, 2, KT, 256, h)
                norm(2)
                norm(1)
                cn = lambda k: (cn_hi[:, k, :], cn_lo[:, k, :])
                n = linear(n, C_UQ, 8, 2, 1024, cn, wait="act_ready")
                pe.wait_ge(act_ready, v.next("act_ready"))
                ckv = lambda k: (cn_hi[:, 2, :], cn_lo[:, 2, :])
                n = linear(n, C_UKV, 4, 1, 1024, ckv)
                n = by_token(n, C_UKV, 1, 1024, ckv, 512)
                pe.wait_ge(lin_out, v.count("lin_out", 0))
                pe.wait_ge(rope_done, v.next("rope_done", 2))
                attend(mla_units, p_sb, pt_sb)
                os = lambda k: (os_hi[:, k, :], os_lo[:, k, :])
                for br in range(2):
                    for c in range(4):
                        n = linear(n, (C_GNA, C_GMLA)[br] + c, 2, KT, 256, h)
                    for c in range(2):
                        n = linear(n, (C_BNA, C_BMLA)[br] + c, 4, 4, 512, os,
                                   wait="osplit_ready" if c == 0 else None)
                for c in range(4):
                    n = linear(n, C_OUT + c, 2, KT, 256, h, wait="act_ready" if c == 0 else None)
                norm(KT)
                pe.wait_ge(act_ready, v.next("act_ready", KT))
                hid = lambda k: (hid_hi[:, k, :], hid_lo[:, k, :])
                with v.ff():
                    for c in range(4):
                        n = linear(n, C_FF + c, 2, KT, 256, h)
                    for c in range(4, 8):
                        n = linear(n, C_FF + c, 2, KT, 256, hid, wait="act_ready" if c == 4 else None)

            norm(KT)
            pe.wait_ge(small2_in, v.next("small2_in", 5, 16))
            v.skip("lin_out")
            te.matmul(ps[0:8, 0, :], relT[0:32, :], onehot[0:32, 0:S], start=True, stop=True).then_inc(lin_full, v.tick("lin_full"))
            norm(KT)
            n = 1
            for c in range(10):
                n = linear(n, c, 2, KT, 256, h, wait="act_ready" if c == 0 else None)
            n = linear(n, C2_VI, 1, KT, 256, h)
            wh, wl = chunk(C2_VI)
            b = bank(n)
            for t in range(TT):
                for k in range(KT):
                    o = 256 * k + P
                    ins = three(b[:, 8 * t:8 * t + 8], (wh[:, o:o + 8], wl[:, o:o + 8]),
                                (act_hi[:, k, P * t:P * t + P], act_lo[:, k, P * t:P * t + P]),
                                k == 0, k == KT - 1, swap=True)
            ins.then_inc(lin_full, v.tick("lin_full"))
            n += 1
            for c in (1, 2):
                n = by_token(n, C2_VI + c, KT, 256, h, 256)
            pe.wait_ge(pool_d, v.next("pool_d", 2))
            for t in range(2):
                b = bank(n)
                te.matmul(b, poolw[:, t, :], zc[:, 6 + t, :], start=True, stop=True).then_inc(lin_full, v.tick("lin_full"))
                n += 1
            pe.wait_ge(lin_out, v.count("lin_out", 0))
            for m in range(24):
                t, hh = m // 8 + 1, m % 8
                r = slice(64 * (hh % 2), 64 * (hh % 2) + 64)
                if m >= 2:
                    pe.wait_ge(ix_relu, v.next("ix_relu"))
                te.matmul(ps[:, B_S + m % 2, 0:P * (t + 1)], iq[r, hh // 2, P * t:P * t + P],
                                   ik[r, 0:P * (t + 1)], start=True, stop=True).then_inc(ix_full, v.tick("ix_full"))
            pe.wait_ge(ix_relu, v.next("ix_relu", 2))
            attend(b2_units, p2_sb, pt2_sb)
            pe.wait_ge(act_ready, v.next("act_ready", 4))
            for c in range(4):
                n = linear(n, C2_OUT + c, 2, KT, 256, h)
            norm(KT)
            norm(KT)
            for c in range(H2T):
                n = linear(n, C2_GU + c, 2, KT, 256, h, wait="act_ready" if c == 0 else None)
            for t in range(KT):
                b = bank(n)
                for half in range(2):
                    wh, wl = chunk(C2_DOWN + 2 * t + half)
                    for k in range(11):
                        kk_ = 11 * half + k
                        if t == 0:
                            pe.wait_ge(act_ready, v.next("act_ready"))
                        ins = three(b, (wh[:, P * k:P * k + P], wl[:, P * k:P * k + P]),
                                    (h2_hi[:, kk_, :], h2_lo[:, kk_, :]), kk_ == 0, kk_ == H2T - 1)
                ins.then_inc(lin_full, v.tick("lin_full"))
                n += 1
            norm(KT)
            norm(KT)
            pe.wait_ge(p_in, v.next("p_in", 1, 16))
            for t in range(2):
                b = bank(n)
                for k in range(TT):
                    ins = te.transpose(b[:, P * k:P * k + P], pin[:, k, P * t:P * t + P], ident[:])
                ins.then_inc(lin_full, v.tick("lin_full"))
                n += 1
            for c in range(4):
                n = linear(n, C2_PG + c, 2, KT, 256, h, wait="act_ready" if c == 0 else None)
            n = linear(n, C2_PP, KT, 2, 1024, lambda k: (pT_hi[:, k, :], pT_lo[:, k, :]),
                       wait="act_ready")
            pe.wait_ge(x_ready, v.next("x_ready", 3 * KT))
            for t in range(TT):
                for k in range(2):
                    b = bank(n)
                    for f in range(4):
                        ins = te.transpose(b[:, P * f:P * f + P], x[:, 4 * k + f, P * t:P * t + P],
                                           ident[:])
                    ins.then_inc(lin_full, v.tick("lin_full"))
                    n += 1

    return made


def host_constants():
    p = np.arange(P)
    f32 = np.float32
    ident = np.eye(P, dtype=f32)
    ones = np.ones((P, P), f32)
    namask = np.full((P, 3, 32, 8), NEG, f32)
    for kind, (tile, c0) in enumerate(((0, 0), (1, 8), (3, 32))):
        col = 16 * tile + p // 8
        start = np.clip(col - 8, 0, COLS - 16)
        j = c0 + np.arange(32)
        ok = (j[None] >= start[:, None]) & (j[None] < start[:, None] + 16)
        namask[:, kind][ok] = 0.0
    invf = np.empty((P, 2), f32)
    invf[:, 0] = f32(1.0) / np.power(f32(10000.0), (np.arange(0, 32, 2, dtype=f32) / f32(32)))[p % 16]
    invf[:, 1] = np.where(p % 32 < 16, -1.0, 1.0)
    dist = np.arange(S)
    n = np.maximum(dist, 0)
    nf = np.maximum(n, 1).astype(f32)
    large = 16 + (np.log(nf / f32(16)) / f32(np.log(8.0)) * f32(16)).astype(np.int32)
    bucket = np.where(n < 16, n, np.minimum(large, 31))
    onehot = (np.arange(32)[:, None] == bucket[None]).astype(f32)
    pcnt = np.empty((P, 2, S), f32)
    for t in range(2):
        for k in range(2):
            pcnt[64 * k:64 * k + 64, t] = 1.0 / np.minimum(np.arange(S) + 1, 2 ** (2 * t + k + 1))
    caus = np.where(p[None] > p[:, None], NEG, 0.0).astype(f32)
    return dict(ident=ident, ones=ones, namask=namask.reshape(P, 3, 256), invf=invf, onehot=onehot,
                pcnt=pcnt, caus=caus)


def chunks(w, cols):
    k, n = w.shape
    c = w.reshape(k // P, P, n // cols, cols).transpose(2, 1, 0, 3).reshape(n // cols, P, -1)
    return np.pad(c, ((0, 0), (0, 0), (0, CH - c.shape[2])))


def columns(v):
    return v.reshape(-1, P).T


def kernel(**inputs):
    import concourse.bacc as bacc
    from concourse.bass_utils import run_bass_kernel_spmd

    i = {k: np.asarray(v) for k, v in inputs.items()}
    stream, ada, vec1 = [], [], []
    for l in range(DEPTH):
        w = i["w_in"][l]
        kr = w[:, 1920:1952]
        stream += [chunks(w[:, 0:512], 256), chunks(w[:, 512:1024], 256), chunks(w[:, 1024:1536], 256),
                   chunks(w[:, 1536:1792], 256),
                   chunks(np.concatenate([w[:, 1792:1920], kr, kr[:, 16:], kr[:, :16],
                                          np.zeros((D, 64), w.dtype)], 1), 256)]
        uq = i["w_uq"][l].reshape(256, 8, 96)
        stream.append(chunks(np.concatenate([
            uq[:, :, :64].reshape(256, 512), uq[:, :, 64:].reshape(256, 256),
            np.concatenate([uq[:, :, 80:], uq[:, :, 64:80]], 2).reshape(256, 256)], 1), 1024))
        ukv = i["w_ukv"][l].reshape(P, 8, 128)
        stream.append(chunks(np.concatenate([ukv[:, :, :64].reshape(P, 512),
                                             ukv[:, :, 64:].reshape(P, 512)], 1), 1024))
        for k, br in enumerate(("w_br_na", "w_br_mla")):
            stream += [chunks(w[:, 1952 + D * k:1952 + D * k + D], 256), chunks(i[br][l], 512)]
        stream.append(chunks(i["w_out"][l], 256))
        for j in range(FFJ):
            stream += [chunks(i["w_ff1"][l][:, D * j:D * j + D], 256),
                       chunks(i["w_ff2"][l][D * j:D * j + D], 256)]
        ada.append(chunks(i["w_ada"][l], 256))
        vec1.append(np.concatenate([columns(i[k][l]) for k in ("g_mix", "g_mlp", "b_gate", "g_q", "g_kv")], 1))
    w = i["w_in_2"][0]
    o = np.cumsum([0] + [256] * 7 + [512, 64, 8, 256, 256, 256])
    part = lambda k: w[:, o[k]:o[k + 1]]
    for k in (0, 1, 2, 3, 4, 5, 10, 11, 7):
        stream.append(chunks(part(k), 256))
    stream.append(chunks(np.concatenate([part(8), part(8), part(9), np.zeros((D, 120), w.dtype)], 1), 256))
    stream += [chunks(part(6), 256), chunks(part(12), 256), chunks(i["w_out_2"][0], 256)]
    gu = i["w_gate_up_2"][0].reshape(D, 2, H2T, P).transpose(0, 2, 1, 3).reshape(D, -1)
    stream.append(chunks(gu, 256))
    down = chunks_down(i["w_down_2"][0])
    stream += [down, chunks(i["w_ple_gate_2"][0], 256), chunks(i["w_ple_proj_2"][0], 1024)]
    stream = np.concatenate(stream)
    assert stream.shape == (N_CHUNK, P, CH)

    rpb = np.zeros((DEPTH, NAH, 16, 48), np.float32)
    rpb[:, :, :15, 16:47] = i["rpb"]
    rpb = rpb.reshape(DEPTH, NAH, -1)[:, :, ::-1]
    poolw = np.zeros((P, 2, P), np.float32)
    for k in range(4):
        r = slice(64 * (k % 2), 64 * (k % 2) + 64)
        poolw[r, k // 2, r] = i["pool_w_2"][0, k]
    vec2 = np.concatenate([columns(v) for v in (
        i["g_final"], i["g_mix_pre_2"][0], i["pool_scale_2"][0], i["conv_w_2"][0].reshape(-1),
        i["g_mix_post_2"][0], i["g_ffn_pre_2"][0], i["g_ffn_post_2"][0], i["g_ple_2"][0])], 1)
    arrays = dict(
        x=i["x"], positions=i["positions"], w_stream=stream, w_ada=np.concatenate(ada),
        vec1=np.stack(vec1, 1), vec2=vec2,
        bada=np.concatenate([columns(i["b_ada"][l]) for l in range(DEPTH)], 1), cT=columns(i["c"]),
        rpb_rev=rpb, relT=i["rel_bias_2"].T, poolw=poolw, p_2=i["p_2"], **host_constants())
    arrays = {k: np.ascontiguousarray(v) for k, v in arrays.items()}

    counts = {}
    for final in (False, True):
        nc = bacc.Bacc("TRN2", target_bir_lowering=False, num_devices=1)
        aps = {k: nc.dram_tensor("in_" + k, v.shape, mybir.dt.from_np(v.dtype), kind="ExternalInput").ap()
               for k, v in arrays.items()}
        out = nc.dram_tensor("out", (1, S, D), F32, kind="ExternalOutput").ap()
        made = build(nc, counts, aps, out)
        counts = {k: (m[0], m[1], m[2]) for k, m in made.items()}
    r = run_bass_kernel_spmd(nc, [{"in_" + k: v for k, v in arrays.items()}], core_ids=[0])
    return r.results[0]["out"]


def chunks_down(w):
    c = w.reshape(2, 11, P, KT, P).transpose(3, 0, 2, 1, 4).reshape(2 * KT, P, 11 * P)
    return np.pad(c, ((0, 0), (0, 0), (0, CH - 11 * P)))
```

```python
from collections import Counter
from contextlib import ExitStack, contextmanager

import numpy as np

import concourse.bass as bass
from concourse import mybir

F32 = mybir.dt.float32
F32R = mybir.dt.float32r
I32 = mybir.dt.int32
ALU = mybir.AluOpType
ACT = mybir.ActivationFunctionType
AX = mybir.AxisListType

P = 128
D = 1024
S = 512
KT = D // P
TT = S // P
DEPTH = 2
CH = 2048
NEG = -1.0e30
TAKEN = -3.0e38
EPS = 1e-6
ROWS, COLS = 8, 64
NAH = MLAH = 8
HD = 64
C_Q, C_K, C_V, C_CQ, C_CKV, C_UQ, C_UKV = 0, 2, 4, 6, 7, 8, 9
C_GNA, C_BNA, C_GMLA, C_BMLA, C_OUT, C_FF = 10, 14, 16, 20, 22, 26
FFJ = 4
C_LAYER = C_FF + 8 * FFJ
C2_Z, C2_VI, C2_OUT, C2_GU, C2_DOWN, C2_PG, C2_PP, C2_END = 0, 10, 13, 17, 39, 55, 59, 60
H2T = 22
N_CHUNK = DEPTH * C_LAYER + C2_END
ADA_PRO = 4
ADA_LAY = 4
V_GMIX, V_GMLP, V_BG, V_GQ, V_GKV, NV1 = 0, 8, 16, 32, 34, 35
W_GF, W_PRE, W_PS, W_CW, W_MPOST, W_FPRE, W_FPOST, W_PLE, NV2 = 0, 8, 16, 18, 24, 32, 40, 48, 56
M_SHA, M_SCA, M_GA, M_SHM, M_SCM, M_GM = (NV1 + 8 * i for i in range(6))


class View:

    def __init__(self, eng, made, per, entered):
        self.eng, self.made, self.per, self.entered = eng, made, per, entered
        self.n = Counter()
        self.p = Counter()
        self.l = None
        self.j = None
        self.last = False

    def value(self, name, n):
        prologue, layer, ff = self.per.get(name, (0, 0, 0))
        if self.l is not None:
            n = self.l * (layer + FFJ * ff) + (prologue + n)
        if self.j is not None:
            n = n + self.j * ff
        return n

    def next(self, name, k=1, unit=1):
        self.n[name] += k * unit
        return self.value(name, self.n[name])

    def count(self, name, k):
        return self.value(name, self.n[name] + k)

    def skip(self, name, k=1):
        self.n[name] += k

    def own(self, name):
        return self.value(name, self.p[name])

    def tick(self, name, unit=1):
        frame = 0 if self.l is None else 3 if self.last else 2 if self.j is not None else 1
        self.made[name][frame] += unit
        self.p[name] += unit
        return unit

    @contextmanager
    def layers(self):
        self.n, self.p = Counter(), Counter()
        with self.eng.Fori(0, DEPTH) as l:
            self.l = l
            yield
        self.n, self.p = Counter(), Counter()
        self.l = DEPTH
        self.last = True

    @contextmanager
    def ff(self):
        n0, p0 = Counter(self.n), Counter(self.p)
        self.eng.sem_inc(self.entered)
        with self.eng.Fori(0, FFJ) as j:
            self.j = j
            yield
        self.j = None
        self.n, self.p = n0, p0
        for name, (_, _, ff) in self.per.items():
            self.n[name] += FFJ * ff
            self.p[name] += FFJ * ff


SIGNALS = """
x_in consts_in pos_in c_sig ang_ready sin_done vec_ready lin_full lin_out sq_ready sq_used
std_ready scaled_ready hi_ready act_ready x_ready vodd_in bias_in s_full max_ready exp_done
p_ready pt_full pt_copied pv_done o_copied permuted rope_done osplit_hi osplit_ready merged_ready
square_ready small2_in rel_ready rel_out wide_in ix_full ix_relu ix_used ya_ready pool_d o_hi
prod_ready p_in dve_chain fin_out sum_step ada2_used acc_ready vec2_ready half_used bias_step
""".split()


def build(nc, per, a, out):
    made = {n: [0, 0, 0, 0] for n in SIGNALS}
    with ExitStack() as ctx:
        def sem(name):
            return ctx.enter_context(nc.semaphore(name))

        x_in = sem("x_in")
        consts_in = sem("consts_in")
        pos_in = sem("pos_in")
        c_sig = sem("c_sig")
        ang_ready = sem("ang_ready")
        sin_done = sem("sin_done")
        vec_ready = sem("vec_ready")
        lin_full = sem("lin_full")
        lin_out = sem("lin_out")
        sq_ready = sem("sq_ready")
        sq_used = sem("sq_used")
        std_ready = sem("std_ready")
        scaled_ready = sem("scaled_ready")
        hi_ready = sem("hi_ready")
        act_ready = sem("act_ready")
        x_ready = sem("x_ready")
        vodd_in = sem("vodd_in")
        bias_in = sem("bias_in")
        s_full = sem("s_full")
        max_ready = sem("max_ready")
        exp_done = sem("exp_done")
        p_ready = sem("p_ready")
        pt_full = sem("pt_full")
        pt_copied = sem("pt_copied")
        pv_done = sem("pv_done")
        o_copied = sem("o_copied")
        permuted = sem("permuted")
        rope_done = sem("rope_done")
        osplit_hi = sem("osplit_hi")
        osplit_ready = sem("osplit_ready")
        merged_ready = sem("merged_ready")
        square_ready = sem("square_ready")
        small2_in = sem("small2_in")
        rel_ready = sem("rel_ready")
        rel_out = sem("rel_out")
        wide_in = sem("wide_in")
        ix_full = sem("ix_full")
        ix_relu = sem("ix_relu")
        ix_used = sem("ix_used")
        ya_ready = sem("ya_ready")
        pool_d = sem("pool_d")
        o_hi = sem("o_hi")
        prod_ready = sem("prod_ready")
        p_in = sem("p_in")
        dve_chain = sem("dve_chain")
        fin_out = sem("fin_out")
        sems = dict(osplit_ready=osplit_ready, act_ready=act_ready, o_copied=o_copied)
        raw_landed = [sem(f"raw_landed{k}") for k in range(2)]
        ada_landed = [sem(f"ada_landed{k}") for k in range(KT)]
        ada2_landed = [sem(f"ada2_landed{k}") for k in range(2)]
        ada_used = sem("ada_used")
        ada_sum = sem("ada_sum")
        ada_full = sem("ada_full")
        ada_taken = sem("ada_taken")
        cact_ready = sem("cact_ready")
        sum_step = sem("sum_step")
        ada2_used = sem("ada2_used")
        acc_ready = sem("acc_ready")
        vec2_ready = sem("vec2_ready")
        bias_step = sem("bias_step")
        half_used = sem("half_used")
        w_hi = sem("w_hi")
        w_split = sem("w_split")
        mlp_entered = sem("mlp_entered")

        top = [nc.sbuf_base + (-nc.sbuf_base) % 64]

        def fixed(name, shape, dt=F32):
            t = nc.alloc_sbuf_tensor_at(name, [P] + shape, dt, offset=top[0])
            top[0] += (4 * int(np.prod(shape)) + 31) // 32 * 32
            return t

        x = fixed("x", [KT, S])
        act_hi = fixed("act_hi", [KT, S], F32R)
        act_lo = fixed("act_lo", [KT, S], F32R)
        raw = fixed("raw", [2, CH])
        whi = fixed("whi", [2, CH], F32R)
        wlo = fixed("wlo", [2, CH], F32R)
        ident = fixed("ident", [P])
        ones = fixed("ones", [P])
        sq = fixed("sq", [2, S])
        std = fixed("std", [S])
        rstd = fixed("rstd", [S])
        ssum = fixed("ssum", [S])
        tmp = fixed("tmp", [2, S])
        cur = fixed("cur", [NV1 + 48])
        scl = fixed("scl", [2, KT])
        vec1 = fixed("vec1", [DEPTH, NV1])
        vec2 = fixed("vec2", [NV2])
        mod = fixed("mod", [DEPTH, 48])
        modf = mod[:].rearrange("p l m -> p (l m)")
        nmax = fixed("nmax", [4, 1])
        rsum = fixed("rsum", [4, 1])
        rinv = fixed("rinv", [4, 1])
        cact = fixed("cact", [KT])
        modraw = fixed("modraw", [32])
        eps = fixed("eps", [1])
        iw = fixed("iw", [TT, 8])
        top8 = fixed("top8", [8])
        cosT = fixed("cosT", [S])
        sinT = fixed("sinT", [S])
        namask = fixed("namask", [3, 256])
        arena0 = top[0]
        arena_end = nc.sbuf_usable_end

        def at(name, kb, shape, dt=F32):
            off = arena0 + int(kb * 1024)
            assert off + 4 * int(np.prod(shape)) <= arena_end, (name, kb, arena0, arena_end)
            return nc.alloc_sbuf_tensor_at(name, [P] + shape, dt, offset=off)

        ada = at("ada", 0, [KT, D])
        acc = at("acc", 62, [2, D])
        xin = at("xin", 32, [TT, D])
        cT = at("cT", 49, [KT])
        csig = at("csig", 49.5, [KT])
        posi = at("posi", 50, [S], I32)
        ang = at("ang", 52, [2, S])
        kk = at("kk", 56, [2, S])
        invf = at("invf", 60, [2])
        o_na = at("o_na", 0, [4, S])
        o_mla = at("o_mla", 8, [4, S])
        QT = at("QT", 16, [4, S])
        KTn = at("KTn", 24, [4, S])
        Ve = at("Ve", 32, [TT, S])
        Vo = at("Vo", 40, [3, S])
        relt = at("relt", 46, [NAH, 384])
        comb = at("comb", 58, [2, 3, 256])
        p_sb = at("p_sb", 64, [4, S])
        pt_sb = at("pt_sb", 72, [2, S])
        s_sb = at("s_sb", 76, [2, S])
        ada2 = at("ada2", 80, [2, D])
        acc_na = at("acc_na", 8, [D])
        acc_mla = at("acc_mla", 56, [D])
        qT = at("qT", 16, [MLAH, S])
        kT = at("kT", 32, [MLAH, S])
        Vm = at("Vm", 48, [TT, S])
        craw = at("craw", 56, [3, S])
        cn_hi = at("cn_hi", 62, [3, S], F32R)
        cn_lo = at("cn_lo", 68, [3, S], F32R)
        rraw = at("rraw", 8, [4, S])
        rmul = at("rmul", 74, [2, S])
        gsig = at("gsig", 16, [KT, S])
        os_hi = at("os_hi", 32, [4, S], F32R)
        os_lo = at("os_lo", 40, [4, S], F32R)
        merged = at("merged", 48, [KT, S])
        ybuf = at("ybuf", 64, [2, S])
        hid_hi = at("hid_hi", 16, [KT, S], F32R)
        hid_lo = at("hid_lo", 32, [KT, S], F32R)
        rel_u = at("rel_u", 68, [2, S])
        squ = at("squ", 72, [2, S])
        zc = at("zc", 0, [8, S])
        zq = at("zq", 16, [8, S])
        iq = at("iq", 32, [4, S])
        ik = at("ik", 40, [S])
        V2 = at("V2", 42, [TT, S])
        wide = at("wide", 50, [8, S])
        selm = at("selm", 66, [1152])
        ixr = at("ixr", 70.5, [2, S])
        p2_sb = at("p2_sb", 0, [4, S])
        pt2_sb = at("pt2_sb", 8, [2, S])
        s2_sb = at("s2_sb", 12, [2, S])
        relT = at("relT", 16, [8])
        onehot = at("onehot", 17, [S])
        relrow = at("relrow", 20, [640])
        caus = at("caus", 85, [P])
        poolw = at("poolw", 70.5, [2, P])
        pcnt = at("pcnt", 74.5, [2, S])
        ct = at("ct", 78.5, [3, S])
        mixr = at("mixr", 0, [KT, S])
        h2_hi = at("h2_hi", 0, [H2T, S], F32R)
        h2_lo = at("h2_lo", 44, [H2T, S], F32R)
        fraw = nc.alloc_sbuf_tensor_at("fraw", [P, KT, S], F32, offset=nc.sbuf_base + (-nc.sbuf_base) % 64 + 16384)
        pin = at("pin", 0, [TT, 256])
        pT = at("pT", 4, [2, S])
        pT_hi = at("pT_hi", 8, [2, S], F32R)
        pT_lo = at("pT_lo", 12, [2, S], F32R)
        pg = at("pg", 16, [KT, S])
        outb = at("outb", 32, [TT, D])

        ps = ctx.enter_context(nc.psum_tensor("ps", [P, 8, 512], F32))
        B_S, B_T, B_O, B_N = 2, 4, 6, 7
        relscr = nc.dram_tensor("relscr", (8, 640), F32).ap()

        def backward(t, o, n):
            a0 = t[:]
            return bass.AP(tensor=a0.tensor, offset=a0.offset + o, ap=[list(a0.ap[0]), [-1, n]])

        na_units, mla_units, b2_units = [], [], []
        for h in range(NAH):
            r0 = 64 * (h % 2)
            for q in range(TT):
                c0 = (0, 8, 24, 32)[q]
                vs = []
                for b in range(2):
                    c = c0 + 16 * b
                    vs.append((Ve if c % 16 == 0 else Vo)[:, c // 16, h * HD:(h + 1) * HD])
                na_units.append(dict(
                    q=QT[r0:r0 + 64, h // 2, q * P:(q + 1) * P],
                    k=KTn[r0:r0 + 64, h // 2, 8 * c0:8 * c0 + 256],
                    n=256, bias=comb[:, h % 2, (0, 1, 1, 2)[q], :], sel=None, v=vs, head=h, t=q))
        for h in range(MLAH):
            for q in range(TT):
                mla_units.append(dict(
                    q=qT[0:96, h, q * P:(q + 1) * P], k=kT[0:96, h, :], n=S, bias=None, sel=None,
                    v=[Vm[:, b, h * HD:(h + 1) * HD] for b in range(TT)], head=h, t=q))
        for h in [4, 5, 6, 7, 0, 1, 2, 3]:
            r0 = 64 * (h % 2)
            zt = (0 if h < 4 else 4) + (h % 4) // 2
            for q in range(TT):
                n = P * (q + 1)
                s0 = (0, 0, 256, 640)[q]
                b2_units.append(dict(
                    q=zq[r0:r0 + 64, zt, q * P:(q + 1) * P], k=zq[r0:r0 + 64, zt + 2, 0:n], n=n,
                    bias=backward(wide, h * S + n - 1, n), sel=selm[:, s0:s0 + n] if h < 4 and q else None,
                    v=[V2[:, b, h * HD:(h + 1) * HD] for b in range(q + 1)], head=h, t=q))

        def rpb_rows(l, h):
            o = a["rpb_rev"][bass.ds(l, 1), h]
            return bass.AP(tensor=o.tensor, offset=o.offset + 33, ap=[[1, 16], [48, 8], [1, 384]])

        def rel_wide(h):
            return bass.AP(tensor=relscr.tensor, offset=640 * h, ap=[[1, P], [1, S]])

        block = ctx.enter_context(nc.Block())

        @block.sync
        def _(sp):
            v = View(sp, made, per, mlp_entered)
            xv = a["x"].rearrange("o (r c) d -> (o c) r d", r=ROWS)
            for t in range(TT):
                sp.dma_start(xin[:, t, :], xv[16 * t:16 * t + 16]).then_inc(x_in, v.tick("x_in", 16))
            for dst, src in ((ident, "ident"), (ones, "ones"), (namask, "namask"), (vec1, "vec1"),
                             (vec2, "vec2"), (modf, "bada"), (cT, "cT"), (invf, "invf")):
                sp.dma_start(dst if dst is modf else dst[:], a[src]).then_inc(consts_in, v.tick("consts_in", 16))
            sp.dma_start(posi[:], a["positions"].broadcast_to((P, S))).then_inc(pos_in, v.tick("pos_in", 16))
            for k in range(KT):
                sp.dma_start(ada[:, k, :], a["w_ada"][k]).then_inc(ada_landed[k], 16)
            for k in range(2):
                sp.dma_start(raw[:, k, :], a["w_stream"][k]).then_inc(raw_landed[k], 16)
            with sp.Fori(1, ADA_PRO) as i:
                for k in range(KT):
                    sp.wait_ge(ada_used, KT * i + (k + 1 - KT))
                    sp.dma_start(ada[:, k, :], a["w_ada"][bass.ds(KT * i + k, 1)]
                                 .rearrange("o p f -> (o p) f")).then_inc(ada_landed[k], 16)
            with sp.Fori(1, N_CHUNK // 2) as i:
                for k in range(2):
                    sp.wait_ge(w_split, 2 * i + (k - 1))
                    sp.dma_start(raw[:, k, :], a["w_stream"][bass.ds(2 * i + k, 1)]
                                 .rearrange("o p f -> (o p) f")).then_inc(raw_landed[k], 16)

        @block.gpsimd
        def _(pool):
            with pool.Fori(0, N_CHUNK // 2) as i:
                for k in range(2):
                    pool.wait_ge(w_hi, 2 * i + (k + 1))
                    nc.gpsimd.tensor_tensor(wlo[:, k, :], raw[:, k, :], whi[:, k, :].bitcast(F32),
                                            ALU.subtract).then_inc(w_split, 1)

        @block.scalar
        def _(act):
            v = View(act, made, per, mlp_entered)
            sc = nc.scalar

            def split_hi(c):
                k = c % 2
                if v.l is None:
                    n = 16 * (c // 2 + 1)
                else:
                    if v.last and c >= C2_END:
                        return
                    n = v.l * (8 * C_LAYER) + 16 * (c // 2 + 1)
                    if v.j is not None:
                        n = n + v.j * 64
                act.wait_ge(raw_landed[k], n)
                sc.activation(whi[:, k, :], raw[:, k, :], ACT.Copy).then_inc(w_hi, 1)

            def evac(i, dst, func=ACT.Copy, rows=slice(0, P), cols=S, **kw):
                act.wait_ge(lin_full, v.next("lin_full"))
                sc.activation(dst, ps[rows, i % 2, 0:cols], func, **kw).then_inc(lin_out, v.tick("lin_out"))
                act.wait_ge(lin_out, v.own("lin_out"))
                v.skip("lin_out")

            def square(t, src):
                if t >= 2:
                    act.wait_ge(sum_step, v.next("sum_step"))
                sc.activation(sq[:, t % 2, :], src, ACT.Square).then_inc(sq_ready, v.tick("sq_ready"))
                if t == KT - 1:
                    act.wait_ge(sum_step, v.next("sum_step", 2))

            def norm(n_tiles, dim, src=None, hi=None, shift=None):
                for t in range(n_tiles if src else 0):
                    if t >= 2:
                        act.wait_ge(sq_used, v.next("sq_used"))
                    sc.activation(sq[:, t % 2, :], src(t), ACT.Square).then_inc(sq_ready, v.tick("sq_ready"))
                act.wait_ge(sq_used, v.next("sq_used", min(2, n_tiles) if src else 1))
                sc.activation(std[:], ps[:, B_N, :], ACT.Sqrt, bias=eps[:, 0:1],
                              scale=1.0 / dim).then_inc(std_ready, v.tick("std_ready"))
                act.wait_ge(std_ready, v.own("std_ready"))
                for t in range(n_tiles if hi else 0):
                    act.wait_ge(scaled_ready, v.next("scaled_ready"))
                    if shift is None:
                        ins = sc.activation(hi(t), tmp[:, t % 2, :], ACT.Copy)
                    else:
                        ins = sc.activation(hi(t), tmp[:, t % 2, :], ACT.Identity, bias=shift(t))
                    ins.then_inc(hi_ready, v.tick("hi_ready"))

            def load_ada(h):
                act.dma_start(ada2[:, h % 2, :],
                              a["w_ada"][bass.ds(v.l * (KT * ADA_LAY) + (KT * ADA_PRO + h), 1)]
                              .rearrange("o p f -> (o p) f")).then_inc(ada2_landed[h % 2], 16)

            def attend(units, p, pt, sb, n=0, ada0=None):
                for i in range(len(units) + 4):
                    if i < len(units):
                        w = units[i]["n"]
                        biased = units[i]["bias"] is not None
                        act.wait_ge(max_ready, v.count("max_ready", i + 1))
                        src = sb[:, i % 2, 0:w] if biased else ps[:, B_S + i % 2, 0:w]
                        sc.activation(p[:, i % 4, 0:w], src, ACT.Exp, bias=nmax[:, i % 4, :],
                                      scale=-1.0 if biased else 1.0,
                                      accum_out=rsum[:, i % 4, :]).then_inc(exp_done, v.tick("exp_done"))
                    u = i - 3
                    if 0 <= u < len(units):
                        w = units[u]["n"]
                        act.wait_ge(pt_full, v.count("pt_full", u + 1))
                        if u >= 2:
                            act.wait_ge(pv_done, v.count("pv_done", u - 1))
                        sc.activation(pt[:, u % 2, 0:w], ps[:, B_T + u % 2, 0:w],
                                      ACT.Copy).then_inc(pt_copied, v.tick("pt_copied"))
                    u = i - 4
                    if units is b2_units and u >= 0 and u % 8 == 7:
                        act.wait_ge(pv_done, v.count("pv_done", u + 1))
                        sc.activation(act_hi[:, (6, 7, 4, 5)[u // 8], :], ps[:, B_O, :],
                                      ACT.Copy).then_inc(o_hi, v.tick("o_hi"))
                    if ada0 is not None and i % 2 and i < len(units):
                        h = ada0 + i // 2
                        act.wait_ge(ada2_used, v.next("ada2_used"))
                        if h + 2 < KT * ADA_LAY:
                            load_ada(h + 2)
                    if ada0 is not None and i in (17, len(units) + 3):
                        w = (ada0 // KT) + (i > 17)
                        evac(n + (i > 17), modraw[:, 8 * w:8 * w + 8], cols=8)
                act.wait_ge(pt_copied, v.own("pt_copied"))
                v.skip("max_ready", len(units))
                v.skip("pt_full", len(units))
                v.skip("pv_done", len(units))
                act.wait_ge(o_copied, v.next("o_copied", len(units) // 8))

            act.wait_ge(consts_in, v.next("consts_in", 8, 16))
            sc.activation(csig[:], cT[:], ACT.Sigmoid).then_inc(c_sig, v.tick("c_sig"))
            act.wait_ge(c_sig, v.own("c_sig"))
            act.wait_ge(ang_ready, v.next("ang_ready"))
            sc.activation(sinT[:], ang[:, 0, :], ACT.Sin)
            sc.activation(cosT[:], ang[:, 1, :], ACT.Sin).then_inc(sin_done, v.tick("sin_done"))
            act.wait_ge(sin_done, v.own("sin_done"))
            for t in range(KT):
                evac(t, x[:, t, :])
                square(t, x[:, t, :])
            for c in range(2):
                split_hi(c)

            with v.layers():
                act.wait_ge(vec_ready, v.next("vec_ready"))
                for h in range(NAH):
                    act.dma_start(relt[:, h, :], rpb_rows(v.l, h)).then_inc(bias_in, v.tick("bias_in", 16))
                for h in range(2):
                    load_ada(h)
                norm(KT, D, hi=lambda t: act_hi[:, t, :],
                     shift=lambda t: cur[:, M_SHA + t:M_SHA + t + 1])
                n = 0
                for c in range(C_Q, C_V):
                    for i in range(2):
                        evac(n, (QT if c < C_K else KTn)[:, 2 * (c % 2) + i, :],
                             scale=HD ** -0.5 if c < C_K else 1.0)
                        n += 1
                    split_hi(c + 2)
                for c in range(C_V, C_CQ):
                    for t in range(TT):
                        evac(n, Ve[:, t, 256 * (c - C_V):256 * (c - C_V) + 256], cols=256)
                        n += 1
                    split_hi(c + 2)
                for o in range(3):
                    act.dma_start(Vo[0:64, o, :], Ve[64:128, o, :]).then_inc(vodd_in, v.tick("vodd_in", 16))
                    act.dma_start(Vo[64:128, o, :], Ve[0:64, o + 1, :]).then_inc(vodd_in, v.tick("vodd_in", 16))
                attend(na_units, p_sb, pt_sb, s_sb, n, 0)
                n += 2
                for i in range(4):
                    if i < 3:
                        evac(n, craw[:, i, :])
                    else:
                        evac(n, rraw[0:64, 2, :], rows=slice(0, 64))
                    n += 1
                    if i % 2:
                        split_hi(C_CQ + i // 2 + 2)
                norm(2, 256, src=lambda t: craw[:, t, :], hi=lambda t: cn_hi[:, t, :])
                norm(1, 128, src=lambda t: craw[:, 2, :], hi=lambda t: cn_hi[:, 2, :])
                for t in range(4):
                    act.wait_ge(lin_full, v.next("lin_full"))
                    b = ps[:, n % 2, :]
                    sc.activation(qT[0:64, 2 * t, :], b[0:64, :], ACT.Copy, scale=96 ** -0.5)
                    sc.activation(qT[0:64, 2 * t + 1, :], b[64:128, :], ACT.Copy,
                                           scale=96 ** -0.5).then_inc(lin_out, v.tick("lin_out"))
                    act.wait_ge(lin_out, v.own("lin_out"))
                    v.skip("lin_out")
                    n += 1
                act.wait_ge(rope_done, v.next("rope_done"))
                for t in range(4):
                    evac(n, rraw[:, t, :], scale=96 ** -0.5)
                    n += 1
                split_hi(C_UQ + 2)
                for t in range(4):
                    act.wait_ge(lin_full, v.next("lin_full"))
                    b = ps[:, n % 2, :]
                    sc.activation(kT[0:64, 2 * t, :], b[0:64, :], ACT.Copy)
                    sc.activation(kT[0:64, 2 * t + 1, :], b[64:128, :], ACT.Copy).then_inc(lin_out, v.tick("lin_out"))
                    act.wait_ge(lin_out, v.own("lin_out"))
                    v.skip("lin_out")
                    n += 1
                for t in range(TT):
                    evac(n, Vm[:, t, :])
                    n += 1
                split_hi(C_UKV + 2)
                act.wait_ge(rope_done, v.next("rope_done"))
                attend(mla_units, p_sb, pt_sb, s_sb, n, KT * ADA_LAY // 2)
                n += 2
                for br in range(2):
                    for t in range(4):
                        sc.activation(os_hi[:, t, :], (o_na, o_mla)[br][:, t, :], ACT.Copy).then_inc(osplit_hi, v.tick("osplit_hi"))
                        act.wait_ge(osplit_hi, v.own("osplit_hi"))
                    for c in range(4):
                        for i in range(2):
                            t = 2 * c + i
                            k = V_BG + 8 * br + t
                            evac(n, gsig[:, t, :], ACT.Sigmoid, bias=cur[:, k:k + 1])
                            n += 1
                        split_hi((C_GNA, C_GMLA)[br] + c + 2)
                    for c in range(2):
                        for i in range(4):
                            t = 4 * c + i
                            if t >= 2:
                                act.wait_ge(merged_ready, v.next("merged_ready"))
                            evac(n, ybuf[:, t % 2, :])
                            n += 1
                        split_hi((C_BNA, C_BMLA)[br] + c + 2)
                    act.wait_ge(merged_ready, v.next("merged_ready", 2))
                for t in range(KT):
                    sc.activation(act_hi[:, t, :], merged[:, t, :], ACT.Copy).then_inc(hi_ready, v.tick("hi_ready"))
                    act.wait_ge(hi_ready, v.own("hi_ready"))

                def residual(n, c0, gate):
                    for t in range(KT + 1):
                        if t < KT:
                            evac(n + t, ybuf[:, t % 2, :], scale=cur[:, gate + t:gate + t + 1])
                            if t % 2:
                                split_hi(c0 + t // 2 + 2)
                        if t:
                            act.wait_ge(x_ready, v.next("x_ready"))
                            square(t - 1, x[:, t - 1, :])

                act.wait_ge(vec2_ready, v.next("vec2_ready"))
                residual(n, C_OUT, M_GA)
                n += KT
                norm(KT, D, hi=lambda t: act_hi[:, t, :],
                     shift=lambda t: cur[:, M_SHM + t:M_SHM + t + 1])
                with v.ff():
                    for c in range(4):
                        for i in range(2):
                            t = 2 * c + i
                            evac(n + t, rel_u[:, t % 2, :], ACT.Relu)
                            if t:
                                act.wait_ge(square_ready, v.next("square_ready"))
                                sc.activation(hid_hi[:, t - 1, :], squ[:, (t - 1) % 2, :],
                                                       ACT.Copy).then_inc(hi_ready, v.tick("hi_ready"))
                                act.wait_ge(hi_ready, v.own("hi_ready"))
                        split_hi(C_FF + c + 2)
                    act.wait_ge(square_ready, v.next("square_ready"))
                    sc.activation(hid_hi[:, 7, :], squ[:, 1, :], ACT.Copy).then_inc(hi_ready, v.tick("hi_ready"))
                    act.wait_ge(hi_ready, v.own("hi_ready"))
                    residual(n + KT, C_FF + 4, M_GM)

            for dst, src in ((relT, "relT"), (onehot, "onehot"), (poolw, "poolw"), (pcnt, "pcnt"),
                             (caus, "caus")):
                d = dst[0:32] if dst is relT or dst is onehot else dst[:]
                act.dma_start(d, a[src]).then_inc(small2_in, v.tick("small2_in", 16))
            norm(KT, D)
            for t in range(KT):
                act.wait_ge(scaled_ready, v.next("scaled_ready"))
                sc.activation(x[:, t, :].rearrange("p (r c) -> p r c", r=ROWS),
                                       tmp[:, t % 2, :].rearrange("p (c r) -> p r c", r=ROWS),
                                       ACT.Copy).then_inc(permuted, v.tick("permuted"))
                act.wait_ge(permuted, v.own("permuted"))
            for t in range(KT):
                square(t, x[:, t, :])
            act.wait_ge(rel_ready, v.next("rel_ready"))
            act.wait_ge(lin_full, v.next("lin_full"))
            sc.activation(relrow[0:8, P - 1:P - 1 + S], ps[0:8, 0, :], ACT.Copy).then_inc(lin_out, v.tick("lin_out"))
            act.wait_ge(lin_out, v.own("lin_out"))
            act.wait_ge(lin_out, v.next("lin_out"))
            act.dma_start(relscr[:, 0:P - 1 + S], relrow[0:8, 0:P - 1 + S]).then_inc(rel_out, v.tick("rel_out", 16))
            act.wait_ge(rel_out, v.next("rel_out", 1, 16))
            for h in range(8):
                act.dma_start(wide[:, h, :], rel_wide(h)).then_inc(wide_in, v.tick("wide_in", 16))
            norm(KT, D, hi=lambda t: act_hi[:, t, :])
            n = 1
            for c in range(10):
                for i in range(2):
                    dst = zc[:, 2 * c + i, :] if c < 4 else zq[:, 2 * c - 8 + i, :] if c < 8 \
                        else iq[:, 2 * c - 16 + i, :]
                    evac(n, dst, scale=HD ** -0.5 if c in (4, 6) else 1.0)
                    n += 1
                split_hi(c + 2)
            evac(n, ik[:])
            n += 1
            evac(n, iw[:].rearrange("p t h -> p (t h)"), cols=32, scale=8 ** -0.5 * 64 ** -0.5)
            n += 1
            split_hi(C2_VI + 2)
            for c in range(2):
                for t in range(TT):
                    evac(n, V2[:, t, 256 * c:256 * c + 256], cols=256)
                    n += 1
                split_hi(C2_VI + c + 3)
            for t in range(2):
                act.wait_ge(ya_ready, v.next("ya_ready"))
                sc.activation(act_hi[:, t, :], zc[:, t, :], ACT.Copy).then_inc(hi_ready, v.tick("hi_ready"))
                act.wait_ge(hi_ready, v.own("hi_ready"))
            for t in range(2):
                evac(n, zc[:, 6 + t, :], scale=vec2[:, W_PS + t:W_PS + t + 1])
                n += 1
            for t in range(2):
                sc.activation(act_hi[:, 2 + t, :], zc[:, 6 + t, :], ACT.Copy).then_inc(hi_ready, v.tick("hi_ready"))
                act.wait_ge(hi_ready, v.own("hi_ready"))
            for m in range(24):
                t = m // 8 + 1
                act.wait_ge(ix_full, v.next("ix_full"))
                if m >= 2:
                    act.wait_ge(ix_used, v.next("ix_used"))
                sc.activation(ixr[:, m % 2, 0:P * (t + 1)], ps[:, B_S + m % 2, 0:P * (t + 1)],
                                       ACT.Relu).then_inc(ix_relu, v.tick("ix_relu"))
                act.wait_ge(ix_relu, v.own("ix_relu"))
            act.wait_ge(ix_used, v.next("ix_used", 2))
            attend(b2_units, p2_sb, pt2_sb, s2_sb)

            def added():
                for t in range(KT):
                    act.wait_ge(x_ready, v.next("x_ready"))
                    square(t, x[:, t, :])
                norm(KT, D, hi=lambda t: act_hi[:, t, :])

            for t in range(KT):
                evac(n, mixr[:, t, :])
                n += 1
                if t % 2:
                    split_hi(C2_OUT + t // 2 + 2)
                square(t, mixr[:, t, :])
            norm(KT, D)
            added()
            for c in range(H2T):
                act.wait_ge(lin_full, v.next("lin_full"))
                sc.activation(std[:], ps[:, n % 2, :], ACT.Sigmoid)
                sc.activation(sq[:, 0, :], ps[:, n % 2, :], ACT.Copy).then_inc(lin_out, v.tick("lin_out"))
                act.wait_ge(lin_out, v.own("lin_out"))
                v.skip("lin_out")
                evac(n + 1, sq[:, 1, :])
                n += 2
                split_hi(C2_GU + c + 2)
                act.wait_ge(prod_ready, v.next("prod_ready"))
                sc.activation(h2_hi[:, c, :], tmp[:, c % 2, :], ACT.Copy).then_inc(hi_ready, v.tick("hi_ready"))
                act.wait_ge(hi_ready, v.own("hi_ready"))
            for t in range(KT):
                act.wait_ge(half_used, v.next("half_used"))
                split_hi(C2_DOWN + 2 * t + 2)
                act.wait_ge(lin_full, v.next("lin_full"))
                sc.activation(fraw[:, t, :], ps[:, n % 2, :], ACT.Copy).then_inc(lin_out, v.tick("lin_out"))
                act.wait_ge(lin_out, v.own("lin_out"))
                v.skip("lin_out")
                n += 1
                split_hi(C2_DOWN + 2 * t + 3)
                square(t, fraw[:, t, :])
            act.dma_start(pin[:], a["p_2"].rearrange("a o (t p) d -> p (a o t) d", p=P)).then_inc(p_in, v.tick("p_in", 16))
            norm(KT, D)
            added()
            for t in range(2):
                evac(n, pT[:, t, :])
                n += 1
            for t in range(2):
                sc.activation(pT_hi[:, t, :], pT[:, t, :], ACT.Copy).then_inc(hi_ready, v.tick("hi_ready"))
                act.wait_ge(hi_ready, v.own("hi_ready"))
            for c in range(4):
                for i in range(2):
                    evac(n, pg[:, 2 * c + i, :], ACT.Sigmoid)
                    n += 1
                split_hi(C2_PG + c + 2)
            for t in range(KT):
                if t >= 2:
                    act.wait_ge(x_ready, v.next("x_ready"))
                evac(n, ybuf[:, t % 2, :])
                n += 1
            act.wait_ge(x_ready, v.next("x_ready", 2))
            for t in range(TT):
                for k in range(2):
                    evac(n, outb[:, t, S * k:S * k + S])
                    n += 1
                act.dma_start(out.rearrange("o (t p) d -> t (o p) d", p=P)[t], outb[:, t, :]).then_inc(fin_out, v.tick("fin_out", 16))
            act.wait_ge(fin_out, v.next("fin_out", TT, 16))

        @block.vector
        def _(dve):
            v = View(dve, made, per, mlp_entered)
            ve = nc.vector

            def chain(ins):
                ins.then_inc(dve_chain, v.tick("dve_chain"))
                dve.wait_ge(dve_chain, v.own("dve_chain"))

            def low(dst, src, hi, done):
                ve.tensor_tensor(dst, src, hi.bitcast(F32), ALU.subtract).then_inc(sems[done], v.tick(done))
                dve.wait_ge(sems[done], v.own(done))

            def norm(n_tiles, src, scale, hi, lo, shift=None):
                dve.wait_ge(std_ready, v.next("std_ready"))
                chain(ve.reciprocal(rstd[:], std[:]))
                for t in range(n_tiles + 1):
                    if t < n_tiles:
                        ve.scalar_tensor_tensor(tmp[:, t % 2, :], src(t), scale(t), rstd[:],
                                                         ALU.mult, ALU.mult).then_inc(scaled_ready, v.tick("scaled_ready"))
                        dve.wait_ge(scaled_ready, v.own("scaled_ready"))
                    if t:
                        dve.wait_ge(hi_ready, v.next("hi_ready"))
                        h = hi(t - 1).bitcast(F32)
                        if shift is None:
                            ins = ve.tensor_tensor(lo(t - 1), tmp[:, (t - 1) % 2, :], h, ALU.subtract)
                        else:
                            ins = ve.scalar_tensor_tensor(lo(t - 1), tmp[:, (t - 1) % 2, :],
                                                          shift(t - 1), h, ALU.add, ALU.subtract)
                        ins.then_inc(act_ready, v.tick("act_ready"))
                        dve.wait_ge(act_ready, v.own("act_ready"))

            def add_square(t):
                dve.wait_ge(sq_ready, v.next("sq_ready"))
                if t == 0:
                    ins = ve.tensor_copy(ssum[:], sq[:, 0, :])
                else:
                    ins = ve.tensor_tensor(ssum[:], ssum[:], sq[:, t % 2, :], ALU.add)
                ins.then_inc(sum_step, v.tick("sum_step"))
                dve.wait_ge(sum_step, v.own("sum_step"))

            def norm_add(src, w0):
                dve.wait_ge(std_ready, v.next("std_ready"))
                chain(ve.reciprocal(rstd[:], std[:]))
                for t in range(KT):
                    chain(ve.scalar_tensor_tensor(tmp[:, t % 2, :], src[:, t, :],
                                                  vec2[:, w0 + t:w0 + t + 1], rstd[:],
                                                  ALU.mult, ALU.mult))
                    ve.tensor_tensor(x[:, t, :], x[:, t, :], tmp[:, t % 2, :],
                                     ALU.add).then_inc(x_ready, v.tick("x_ready"))
                    dve.wait_ge(x_ready, v.own("x_ready"))
                    if t:
                        add_square(t - 1)
                add_square(KT - 1)

            def topk_round(m):
                t = m // 16 + 1
                s0, n = (0, 256, 640)[t - 1], P * (t + 1)
                sc = selm[:, s0:s0 + n]
                if m % 16 == 0:
                    chain(ve.tensor_tensor(sc[:, n - P:n], sc[:, n - P:n], caus[:], ALU.add))
                chain(ve.max(top8[:], sc))
                chain(ve.match_replace(sc, top8[:], sc, TAKEN))
                if m % 16 == 15:
                    chain(ve.tensor_scalar(sc, sc, TAKEN, NEG, ALU.not_equal, ALU.mult))

            def bias_tables(h):
                a0 = relt[:]
                for k in range(3):
                    o = 16 - 8 * k
                    ins = ve.tensor_tensor(
                        comb[:, h % 2, k, :].rearrange("p (j i) -> p j i", i=ROWS),
                        bass.AP(tensor=a0.tensor, offset=a0.offset + 384 * h + 383 - o,
                                ap=[list(a0.ap[0]), [-1, 32], [-48, 8]]), namask[:, k, :].rearrange("p (j i) -> p j i", i=ROWS),
                        ALU.add)
                chain(ins)

            def modulation(summed, h):
                k = h % KT
                dve.wait_ge(ada2_landed[h % 2], v.l * (8 * KT * ADA_LAY) + 16 * (h // 2 + 1))
                if k == 0:
                    if h % (2 * KT):
                        dve.wait_ge(lin_full, v.next("lin_full"))
                    ins = ve.tensor_scalar(summed[:], ada2[:, h % 2, :], cact[:, 0:1], None, ALU.mult)
                else:
                    ins = ve.scalar_tensor_tensor(summed[:], ada2[:, h % 2, :], cact[:, k:k + 1],
                                                  summed[:], ALU.mult, ALU.add)
                ins.then_inc(ada2_used, v.tick("ada2_used"))
                dve.wait_ge(ada2_used, v.own("ada2_used"))
                if k == KT - 1:
                    dve.sem_inc(acc_ready, v.tick("acc_ready"))

            def attend(units, p, sb, obuf, summed=None, h0=0):
                for i in range(len(units) + 4):
                    if i < len(units):
                        u = units[i]
                        n = u["n"]
                        if units is na_units and i % TT == 0:
                            bias_tables(u["head"])
                        dve.wait_ge(s_full, v.count("s_full", i + 1))
                        src = ps[:, B_S + i % 2, 0:n]
                        if u["sel"] is not None:
                            chain(ve.tensor_tensor(sb[:, i % 2, 0:n], src, u["sel"], ALU.add))
                            src = sb[:, i % 2, 0:n]
                        if u["bias"] is not None:
                            dve.sem_inc(bias_step, v.tick("bias_step"))
                            ins = ve.tensor_tensor_reduce(
                                out=sb[:, i % 2, 0:n], in0=src, in1=u["bias"], scale=-1.0,
                                scalar=-TAKEN, op0=ALU.add, op1=ALU.min, accum_out=nmax[:, i % 4, :])
                        else:
                            ins = ve.tensor_reduce(nmax[:, i % 4, :], src, AX.X, ALU.max, negate=True)
                        ins.then_inc(max_ready, v.tick("max_ready"))
                    if summed is not None and i % 2 == 0 and i < len(units):
                        modulation(summed, h0 + i // 2)
                    w = i - 2
                    if 0 <= w < len(units):
                        n = units[w]["n"]
                        dve.wait_ge(exp_done, v.count("exp_done", w + 1))
                        chain(ve.reciprocal(rinv[:, w % 4, :], rsum[:, w % 4, :]))
                        ve.tensor_scalar(p[:, w % 4, 0:n], p[:, w % 4, 0:n], rinv[:, w % 4, :], None,
                                         ALU.mult).then_inc(p_ready, v.tick("p_ready"))
                    w = i - 4
                    if w >= 0 and w % 8 == 7:
                        dve.wait_ge(pv_done, v.count("pv_done", w + 1))
                        if units is b2_units:
                            dve.wait_ge(o_hi, v.next("o_hi"))
                            t = (6, 7, 4, 5)[w // 8]
                            low(act_lo[:, t, :], ps[:, B_O, :], act_hi[:, t, :], "o_copied")
                        else:
                            ve.tensor_copy(obuf[:, w // 8, :], ps[:, B_O, :]).then_inc(
                                o_copied, v.tick("o_copied"))
                    if units is b2_units and i < 16:
                        for m in range(3 * i, 3 * i + 3):
                            topk_round(m)
                dve.wait_ge(o_copied, v.own("o_copied"))
                v.skip("s_full", len(units))
                v.skip("exp_done", len(units))
                v.skip("pv_done", len(units))

            ve.memset(eps[:], EPS)
            dve.wait_ge(c_sig, v.next("c_sig"))
            ve.tensor_tensor(cact[:], cT[:], csig[:], ALU.mult).then_inc(cact_ready, 1)
            dve.wait_ge(cact_ready, 1)
            dve.wait_ge(pos_in, v.next("pos_in", 1, 16))
            dve.wait_ge(consts_in, v.next("consts_in", 8, 16))
            chain(ve.tensor_copy(kk[:, 0, :].rearrange("p (c r) -> p c r", r=ROWS),
                                 posi[:].rearrange("p (r c) -> p c r", r=ROWS)))
            chain(ve.tensor_scalar(ang[:, 0, :], kk[:, 0, :], invf[:, 0:1], None, ALU.mult))
            big = 12582912.0
            chain(ve.tensor_scalar(kk[:, 0, :], ang[:, 0, :], 0.5 / np.pi, 0.0, ALU.mult, ALU.add))
            chain(ve.tensor_scalar(kk[:, 1, :], ang[:, 0, :], 0.5 / np.pi, 0.25, ALU.mult, ALU.add))
            chain(ve.tensor_scalar(kk[:], kk[:], big, None, ALU.add))
            chain(ve.tensor_scalar(kk[:], kk[:], big, None, ALU.subtract))
            c1 = 6.28125
            c2 = float(np.float32(np.round((2 * np.pi - c1) * 2 ** 20) / 2 ** 20))
            c3 = float(2 * np.pi - c1 - c2)
            chain(ve.tensor_copy(ang[:, 1, :], ang[:, 0, :]))
            for c in (c1, c2, c3):
                chain(ve.scalar_tensor_tensor(ang[:], kk[:], -c, ang[:], ALU.mult, ALU.add))
            chain(ve.tensor_scalar(ang[:, 1, :], ang[:, 1, :], float(np.pi / 2), None, ALU.add))
            chain(ve.tensor_scalar(ang[:], ang[:], -3.1415925, 3.1415925, ALU.max, ALU.min))
            ve.tensor_scalar(ang[:, 0, :], ang[:, 0, :], invf[:, 1:2], None, ALU.mult).then_inc(ang_ready, v.tick("ang_ready"))
            dve.wait_ge(ang_ready, v.own("ang_ready"))
            for t in range(KT):
                add_square(t)
            with dve.Fori(0, ADA_PRO // 2) as i:
                for m in range(2):
                    for k in range(KT):
                        dve.wait_ge(ada_landed[k], 32 * i + (16 * m + 16))
                        if k == 0:
                            ins = ve.tensor_scalar(acc[:, m, :], ada[:, k, :], cact[:, 0:1], None,
                                                   ALU.mult)
                        else:
                            ins = ve.scalar_tensor_tensor(acc[:, m, :], ada[:, k, :],
                                                          cact[:, k:k + 1], acc[:, m, :],
                                                          ALU.mult, ALU.add)
                        ins.then_inc(ada_used, 1)
                        dve.wait_ge(ada_used, 2 * KT * i + (KT * m + k + 1))
                    dve.sem_inc(ada_sum, 1)
                dve.wait_ge(ada_full, 2 * i + 2)
                ve.tensor_tensor(modf[:, bass.ds(16 * i, 16)], ps[:, B_N, 0:16],
                                 modf[:, bass.ds(16 * i, 16)], ALU.add).then_inc(ada_taken, 1)
            dve.wait_ge(ada_taken, ADA_PRO // 2)

            with v.layers():
                ve.tensor_copy(cur[:, 0:NV1], vec1[:, bass.ds(v.l, 1), :].rearrange("p o m -> p (o m)"))
                chain(ve.tensor_copy(cur[:, NV1:NV1 + 16],
                                     mod[:, bass.ds(v.l, 1), 0:16].rearrange("p o m -> p (o m)")))
                ins = ve.scalar_tensor_tensor(scl[:, 0, :], cur[:, M_SCA:M_SCA + 8], 1.0,
                                              cur[:, V_GMIX:V_GMIX + 8], ALU.add, ALU.mult)
                ins.then_inc(vec_ready, v.tick("vec_ready"))
                dve.wait_ge(vec_ready, v.own("vec_ready"))
                dve.wait_ge(vec_ready, v.next("vec_ready"))
                norm(KT, lambda t: x[:, t, :], lambda t: scl[:, 0, t:t + 1],
                     lambda t: act_hi[:, t, :], lambda t: act_lo[:, t, :],
                     lambda t: cur[:, M_SHA + t:M_SHA + t + 1])
                dve.wait_ge(bias_in, v.next("bias_in", NAH, 16))
                v.skip("lin_out", 16)
                v.skip("lin_full", 16)
                attend(na_units, p_sb, s_sb, o_na, acc_na, 0)
                v.skip("lin_out", 2)
                dve.wait_ge(lin_out, v.next("lin_out", 4))
                ve.tensor_tensor(rmul[0:32, 0, :], rraw[0:32, 2, :], cosT[0:32, :], ALU.mult)
                chain(ve.tensor_tensor(rmul[0:32, 1, :], rraw[32:64, 2, :], sinT[32:64, :], ALU.mult))
                for h in range(MLAH):
                    ins = ve.tensor_tensor(kT[64:96, h, :], rmul[0:32, 0, :], rmul[0:32, 1, :], ALU.add)
                ins.then_inc(rope_done, v.tick("rope_done"))
                dve.wait_ge(rope_done, v.own("rope_done"))
                for t0, k, c in ((0, 2, V_GQ), (2, 1, V_GKV)):
                    norm(k, lambda t: craw[:, t0 + t, :], lambda t: cur[:, c + t:c + t + 1],
                         lambda t: cn_hi[:, t0 + t, :], lambda t: cn_lo[:, t0 + t, :])
                v.skip("sq_ready", 3)
                dve.wait_ge(lin_out, v.next("lin_out", 8))
                for w in range(2):
                    ve.tensor_tensor(rmul[:, 0, :], rraw[:, w, :], cosT[:], ALU.mult)
                    chain(ve.tensor_tensor(rmul[:, 1, :], rraw[:, 2 + w, :], sinT[:], ALU.mult))
                    for h in range(4):
                        r = slice(32 * h, 32 * h + 32)
                        ins = ve.tensor_tensor(qT[64:96, 4 * w + h, :], rmul[r, 0, :], rmul[r, 1, :],
                                               ALU.add)
                    if w == 0:
                        chain(ins)
                ins.then_inc(rope_done, v.tick("rope_done"))
                dve.wait_ge(rope_done, v.own("rope_done"))
                v.skip("lin_out", 8)
                v.skip("lin_full", 1 + 4 + 8 + 8)
                attend(mla_units, p_sb, s_sb, o_mla, acc_mla, 2 * KT)
                dve.wait_ge(lin_out, v.next("lin_out", 2))
                chain(ve.tensor_tensor(modf[:, bass.ds(32 * v.l + 32, 32)], modraw[:],
                                       modf[:, bass.ds(32 * v.l + 32, 32)], ALU.add))
                chain(ve.tensor_copy(cur[:, NV1 + 16:NV1 + 48],
                                     mod[:, bass.ds(v.l, 1), 16:48].rearrange("p o m -> p (o m)")))
                ve.scalar_tensor_tensor(scl[:, 1, :], cur[:, M_SCM:M_SCM + 8], 1.0,
                                        cur[:, V_GMLP:V_GMLP + 8], ALU.add,
                                        ALU.mult).then_inc(vec2_ready, v.tick("vec2_ready"))
                dve.wait_ge(vec2_ready, v.own("vec2_ready"))
                for br in range(2):
                    o = (o_na, o_mla)[br]
                    dve.wait_ge(lin_out, v.count("lin_out", 0))
                    for t in range(4):
                        dve.wait_ge(osplit_hi, v.next("osplit_hi"))
                        low(os_lo[:, t, :], o[:, t, :], os_hi[:, t, :], "osplit_ready")
                    v.skip("lin_out", 8)
                    for t in range(KT):
                        dve.wait_ge(lin_out, v.next("lin_out"))
                        if br == 0:
                            ins = ve.tensor_tensor(merged[:, t, :], ybuf[:, t % 2, :], gsig[:, t, :],
                                                   ALU.mult)
                        else:
                            chain(ve.tensor_tensor(gsig[:, t, :], ybuf[:, t % 2, :], gsig[:, t, :],
                                                   ALU.mult))
                            ins = ve.tensor_tensor(merged[:, t, :], merged[:, t, :], gsig[:, t, :],
                                                   ALU.add)
                        ins.then_inc(merged_ready, v.tick("merged_ready"))
                        dve.wait_ge(merged_ready, v.own("merged_ready"))
                for t in range(KT):
                    dve.wait_ge(hi_ready, v.next("hi_ready"))
                    low(act_lo[:, t, :], merged[:, t, :], act_hi[:, t, :], "act_ready")

                def residual():
                    for t in range(KT + 1):
                        if t < KT:
                            dve.wait_ge(lin_out, v.next("lin_out"))
                            ve.tensor_tensor(x[:, t, :], x[:, t, :], ybuf[:, t % 2, :],
                                             ALU.add).then_inc(x_ready, v.tick("x_ready"))
                            dve.wait_ge(x_ready, v.own("x_ready"))
                        if t:
                            add_square(t - 1)

                residual()
                norm(KT, lambda t: x[:, t, :], lambda t: scl[:, 1, t:t + 1],
                     lambda t: act_hi[:, t, :], lambda t: act_lo[:, t, :],
                     lambda t: cur[:, M_SHM + t:M_SHM + t + 1])
                with v.ff():
                    for t in range(KT + 1):
                        if t < KT:
                            dve.wait_ge(lin_out, v.next("lin_out"))
                            ve.tensor_tensor(squ[:, t % 2, :], rel_u[:, t % 2, :],
                                                      rel_u[:, t % 2, :], ALU.mult).then_inc(square_ready, v.tick("square_ready"))
                            dve.wait_ge(square_ready, v.own("square_ready"))
                        if t:
                            dve.wait_ge(hi_ready, v.next("hi_ready"))
                            low(hid_lo[:, t - 1, :], squ[:, (t - 1) % 2, :], hid_hi[:, t - 1, :],
                                "act_ready")
                    residual()

            dve.wait_ge(std_ready, v.next("std_ready"))
            chain(ve.reciprocal(rstd[:], std[:]))
            for t in range(KT):
                if t >= 2:
                    dve.wait_ge(permuted, v.next("permuted"))
                ve.scalar_tensor_tensor(tmp[:, t % 2, :], x[:, t, :],
                                                 vec2[:, W_GF + t:W_GF + t + 1], rstd[:],
                                                 ALU.mult, ALU.mult).then_inc(scaled_ready, v.tick("scaled_ready"))
                dve.wait_ge(scaled_ready, v.own("scaled_ready"))
            dve.wait_ge(permuted, v.next("permuted", 2))
            for t in range(KT):
                add_square(t)
            ve.memset(relrow[0:8, 0:P - 1], NEG).then_inc(rel_ready, v.tick("rel_ready"))
            dve.wait_ge(rel_ready, v.own("rel_ready"))
            norm(KT, lambda t: x[:, t, :], lambda t: vec2[:, W_PRE + t:W_PRE + t + 1],
                 lambda t: act_hi[:, t, :], lambda t: act_lo[:, t, :])
            dve.wait_ge(small2_in, v.next("small2_in", 5, 16))
            dve.wait_ge(lin_out, v.next("lin_out", 1 + 16))
            for t in range(2):
                cw = lambda k: vec2[:, W_CW + 2 * k + t:W_CW + 2 * k + t + 1]
                chain(ve.tensor_tensor(ct[:, 0, :], zc[:, t, :], zc[:, 2 + t, :], ALU.mult))
                chain(ve.tensor_scalar(ct[:, 1, :], ct[:, 0, :], cw(2), None, ALU.mult))
                for k in (1, 0):
                    d = 2 - k
                    chain(ve.scalar_tensor_tensor(ct[:, 1, d:S], ct[:, 0, 0:S - d], cw(k),
                                                  ct[:, 1, d:S], ALU.mult, ALU.add))
                ve.tensor_tensor(zc[:, t, :], ct[:, 1, :], zc[:, 4 + t, :], ALU.mult).then_inc(ya_ready, v.tick("ya_ready"))
                dve.wait_ge(ya_ready, v.own("ya_ready"))
            for t in range(2):
                src, wins = zc[:, 6 + t, :], []
                for k in range(4 if t else 2):
                    d, dst = 2 ** k, ct[:, k % 3, :]
                    ve.tensor_copy(dst[:, 0:d], src[:, 0:d])
                    chain(ve.tensor_tensor(dst[:, d:S], src[:, d:S], src[:, 0:S - d], ALU.add))
                    src = dst
                    wins.append(dst)
                for k, r in enumerate((slice(0, 64), slice(64, P))):
                    win = wins[2 * t + k]
                    chain(ve.tensor_tensor(win[r], win[r], pcnt[r, t, :], ALU.mult))
                    ins = ve.tensor_tensor(zc[r, 6 + t, :], win[r], zc[r, 6 + t, :], ALU.subtract)
                ins.then_inc(pool_d, v.tick("pool_d"))
                dve.wait_ge(pool_d, v.own("pool_d"))
            dve.wait_ge(pool_d, v.next("pool_d", 2))
            dve.wait_ge(lin_out, v.next("lin_out", 14))
            for t in range(2):
                dve.wait_ge(hi_ready, v.next("hi_ready"))
                low(act_lo[:, t, :], zc[:, t, :], act_hi[:, t, :], "act_ready")
            dve.wait_ge(lin_out, v.next("lin_out", 2))
            for t in range(2):
                dve.wait_ge(hi_ready, v.next("hi_ready"))
                low(act_lo[:, 2 + t, :], zc[:, 6 + t, :], act_hi[:, 2 + t, :], "act_ready")
            for m in range(24):
                t, h = m // 8 + 1, m % 8
                s0, n = (0, 256, 640)[t - 1], P * (t + 1)
                sc = selm[:, s0:s0 + n]
                dve.wait_ge(ix_relu, v.next("ix_relu"))
                if h == 0:
                    ins = ve.tensor_scalar(sc, ixr[:, m % 2, 0:n], iw[:, t, 0:1], None, ALU.mult)
                else:
                    ins = ve.scalar_tensor_tensor(sc, ixr[:, m % 2, 0:n], iw[:, t, h:h + 1], sc,
                                                  ALU.mult, ALU.add)
                ins.then_inc(ix_used, v.tick("ix_used"))
                dve.wait_ge(ix_used, v.own("ix_used"))
                dve.wait_ge(ix_used, v.next("ix_used"))
            dve.wait_ge(wide_in, v.next("wide_in", 8, 16))
            attend(b2_units, p2_sb, s2_sb, None)
            v.skip("lin_out", KT)
            for t in range(KT):
                add_square(t)
            norm_add(mixr, W_MPOST)
            norm(KT, lambda t: x[:, t, :], lambda t: vec2[:, W_FPRE + t:W_FPRE + t + 1],
                 lambda t: act_hi[:, t, :], lambda t: act_lo[:, t, :])
            for c in range(H2T):
                dve.wait_ge(lin_out, v.next("lin_out", 2))
                chain(ve.tensor_tensor(tmp[:, c % 2, :], sq[:, 0, :], std[:], ALU.mult))
                ve.tensor_tensor(tmp[:, c % 2, :], tmp[:, c % 2, :], sq[:, 1, :], ALU.mult).then_inc(prod_ready, v.tick("prod_ready"))
                dve.wait_ge(prod_ready, v.own("prod_ready"))
                dve.wait_ge(hi_ready, v.next("hi_ready"))
                low(h2_lo[:, c, :], tmp[:, c % 2, :], h2_hi[:, c, :], "act_ready")
            v.skip("lin_out", KT)
            for t in range(KT):
                add_square(t)
            norm_add(fraw, W_FPOST)
            norm(KT, lambda t: x[:, t, :], lambda t: vec2[:, W_PLE + t:W_PLE + t + 1],
                 lambda t: act_hi[:, t, :], lambda t: act_lo[:, t, :])
            v.skip("lin_out", 2)
            for t in range(2):
                dve.wait_ge(hi_ready, v.next("hi_ready"))
                low(pT_lo[:, t, :], pT[:, t, :], pT_hi[:, t, :], "act_ready")
            v.skip("lin_out", KT)
            for t in range(KT):
                dve.wait_ge(lin_out, v.next("lin_out"))
                chain(ve.tensor_tensor(pg[:, t, :], pg[:, t, :], ybuf[:, t % 2, :], ALU.mult))
                ve.tensor_tensor(x[:, t, :], x[:, t, :], pg[:, t, :], ALU.add).then_inc(x_ready, v.tick("x_ready"))
                dve.wait_ge(x_ready, v.own("x_ready"))

        @block.tensor
        def _(pe):
            v = View(pe, made, per, mlp_entered)
            te = nc.tensor

            def bank(n):
                if v.n["lin_out"] >= 1:
                    pe.wait_ge(lin_out, v.count("lin_out", -1))
                v.skip("lin_out")
                return ps[:, n % 2, :]

            def chunk(c):
                n = v.l * C_LAYER + (c + 1)
                if v.j is not None:
                    n = n + v.j * 8
                pe.wait_ge(w_split, n)
                return whi[:, c % 2, :], wlo[:, c % 2, :]

            def three(out, w, a, start, stop, swap=False):
                (wh, wl), (ah, al) = w, a
                if swap:
                    (wh, wl), (ah, al) = a, w
                te.matmul(out, wh, ah, start=start, stop=False)
                te.matmul(out, wh, al, start=False, stop=False)
                return te.matmul(out, wl, ah, start=False, stop=stop)

            def linear(n, c, tiles, kts, cols, src, wait=None, each=None):
                wh, wl = chunk(c)

                def part(b, i, k):
                    o = k * cols + P * i
                    return three(b, (wh[:, o:o + P], wl[:, o:o + P]), src(k), k == 0, k == kts - 1)

                if wait is not None and tiles == 2:
                    b = [bank(n), bank(n + 1)]
                    for k in range(kts):
                        pe.wait_ge(sems[wait], v.next(wait))
                        for i in range(2):
                            ins = part(b[i], i, k)
                            if k == kts - 1:
                                ins.then_inc(lin_full, v.tick("lin_full"))
                    return n + tiles
                for i in range(tiles):
                    b = bank(n + i)
                    for k in range(kts):
                        if i == 0 and wait is not None:
                            pe.wait_ge(sems[wait], v.next(wait))
                        ins = part(b, i, k)
                    ins.then_inc(lin_full, v.tick("lin_full"))
                return n + tiles

            def by_token(n, c, kts, cols, src, width):
                wh, wl = chunk(c)
                for t in range(TT):
                    b = bank(n + t)
                    for k in range(kts):
                        o = k * cols + (cols - width)
                        ah, al = src(k)
                        ins = three(b[:, 0:width], (wh[:, o:o + width], wl[:, o:o + width]),
                                    (ah[:, P * t:P * t + P], al[:, P * t:P * t + P]),
                                    k == 0, k == kts - 1, swap=True)
                    ins.then_inc(lin_full, v.tick("lin_full"))
                return n + TT

            def norm(n_tiles):
                for t in range(n_tiles):
                    pe.wait_ge(sq_ready, v.next("sq_ready"))
                    te.matmul(ps[:, B_N, :], ones[:], sq[:, t % 2, :], start=(t == 0),
                              stop=(t == n_tiles - 1)).then_inc(sq_used, v.tick("sq_used"))

            def norm_x(steps=KT):
                pe.wait_ge(sum_step, v.next("sum_step", steps))
                v.skip("sq_ready", steps)
                te.matmul(ps[:, B_N, :], ones[:], ssum[:], start=True,
                          stop=True).then_inc(sq_used, v.tick("sq_used"))

            def attend(units, p, pt, n=0, acc=None):
                for i in range(len(units) + 4):
                    if i < len(units):
                        u = units[i]
                        if i >= 2:
                            pe.wait_ge(exp_done, v.count("exp_done", i - 1))
                        te.matmul(ps[:, B_S + i % 2, 0:u["n"]], u["q"], u["k"], start=True,
                                  stop=True).then_inc(s_full, v.tick("s_full"))
                    if acc is not None and i in (15, len(units) + 2):
                        w = i > 15
                        b = bank(n + w)
                        pe.wait_ge(acc_ready, v.next("acc_ready"))
                        for k in range(KT):
                            ins = te.matmul(b[:, k:k + 1], acc[:, P * k:P * k + P], ones[:, 0:1],
                                            start=True, stop=True)
                        ins.then_inc(lin_full, v.tick("lin_full"))
                    w = i - 3
                    if 0 <= w < len(units):
                        pe.wait_ge(p_ready, v.count("p_ready", w + 1))
                        if w >= 2:
                            pe.wait_ge(pt_copied, v.count("pt_copied", w - 1))
                        for b_ in range(units[w]["n"] // P):
                            ins = te.transpose(ps[:, B_T + w % 2, P * b_:P * b_ + P],
                                               p[:, w % 4, P * b_:P * b_ + P], ident[:])
                        ins.then_inc(pt_full, v.tick("pt_full"))
                    w = i - 4
                    if w >= 0:
                        u = units[w]
                        if w % 8 == 0 and w:
                            pe.wait_ge(o_copied, v.count("o_copied", w // 8))
                        pe.wait_ge(pt_copied, v.count("pt_copied", w + 1))
                        r = 64 * (u["head"] % 2)
                        o = ps[r:r + 64, B_O, P * u["t"]:P * u["t"] + P]
                        nb = u["n"] // P
                        for b_ in range(nb):
                            ins = te.matmul(o, u["v"][b_], pt[:, w % 2, P * b_:P * b_ + P],
                                            start=(b_ == 0), stop=(b_ == nb - 1))
                        ins.then_inc(pv_done, v.tick("pv_done"))
                for name in ("exp_done", "p_ready", "pt_copied"):
                    v.skip(name, len(units))
                pe.wait_ge(o_copied, v.next("o_copied", len(units) // 8))

            pe.wait_ge(consts_in, v.next("consts_in", 8, 16))
            pe.wait_ge(x_in, v.next("x_in", TT, 16))
            for t in range(KT):
                b = bank(t)
                for k in range(TT):
                    ins = te.transpose(b[:, P * k:P * k + P], xin[:, k, P * t:P * t + P], ident[:])
                ins.then_inc(lin_full, v.tick("lin_full"))
            with pe.Fori(0, ADA_PRO // 2) as i:
                for m in range(2):
                    pe.wait_ge(ada_sum, 2 * i + (m + 1))
                    for k in range(KT):
                        ins = te.matmul(ps[:, B_N, KT * m + k:KT * m + k + 1],
                                        acc[:, m, P * k:P * k + P], ones[:, 0:1],
                                        start=True, stop=True)
                    ins.then_inc(ada_full, 1)
            pe.wait_ge(ada_taken, ADA_PRO // 2)

            h = lambda k: (act_hi[:, k, :], act_lo[:, k, :])
            with v.layers():
                norm_x(0)
                n = linear(0, C_Q, 2, KT, 256, h, wait="act_ready")
                for c in range(C_Q + 1, C_V):
                    n = linear(n, c, 2, KT, 256, h)
                for c in (C_V, C_V + 1):
                    n = by_token(n, c, KT, 256, h, 256)
                pe.wait_ge(lin_out, v.count("lin_out", 0))
                pe.wait_ge(vodd_in, v.next("vodd_in", 6, 16))
                attend(na_units, p_sb, pt_sb, n, acc_na)
                n += 2
                n = linear(n, C_CQ, 2, KT, 256, h)
                n = linear(n, C_CKV, 2, KT, 256, h)
                norm(2)
                norm(1)
                cn = lambda k: (cn_hi[:, k, :], cn_lo[:, k, :])
                n = linear(n, C_UQ, 8, 2, 1024, cn, wait="act_ready")
                pe.wait_ge(act_ready, v.next("act_ready"))
                ckv = lambda k: (cn_hi[:, 2, :], cn_lo[:, 2, :])
                n = linear(n, C_UKV, 4, 1, 1024, ckv)
                n = by_token(n, C_UKV, 1, 1024, ckv, 512)
                pe.wait_ge(lin_out, v.count("lin_out", 0))
                pe.wait_ge(rope_done, v.next("rope_done", 2))
                attend(mla_units, p_sb, pt_sb, n, acc_mla)
                n += 2
                os = lambda k: (os_hi[:, k, :], os_lo[:, k, :])
                for br in range(2):
                    for c in range(4):
                        n = linear(n, (C_GNA, C_GMLA)[br] + c, 2, KT, 256, h)
                    for c in range(2):
                        n = linear(n, (C_BNA, C_BMLA)[br] + c, 4, 4, 512, os,
                                   wait="osplit_ready" if c == 0 else None)
                for c in range(4):
                    n = linear(n, C_OUT + c, 2, KT, 256, h, wait="act_ready" if c == 0 else None)
                norm_x()
                pe.wait_ge(act_ready, v.next("act_ready", KT))
                hid = lambda k: (hid_hi[:, k, :], hid_lo[:, k, :])
                with v.ff():
                    for c in range(4):
                        n = linear(n, C_FF + c, 2, KT, 256, h)
                    for c in range(4, 8):
                        n = linear(n, C_FF + c, 2, KT, 256, hid, wait="act_ready" if c == 4 else None)

            norm_x(0)
            pe.wait_ge(small2_in, v.next("small2_in", 5, 16))
            v.skip("lin_out")
            te.matmul(ps[0:8, 0, :], relT[0:32, :], onehot[0:32, 0:S], start=True, stop=True).then_inc(lin_full, v.tick("lin_full"))
            norm_x()
            n = 1
            for c in range(10):
                n = linear(n, c, 2, KT, 256, h, wait="act_ready" if c == 0 else None)
            n = linear(n, C2_VI, 1, KT, 256, h)
            wh, wl = chunk(C2_VI)
            b = bank(n)
            for t in range(TT):
                for k in range(KT):
                    o = 256 * k + P
                    ins = three(b[:, 8 * t:8 * t + 8], (wh[:, o:o + 8], wl[:, o:o + 8]),
                                (act_hi[:, k, P * t:P * t + P], act_lo[:, k, P * t:P * t + P]),
                                k == 0, k == KT - 1, swap=True)
            ins.then_inc(lin_full, v.tick("lin_full"))
            n += 1
            for c in (1, 2):
                n = by_token(n, C2_VI + c, KT, 256, h, 256)
            pe.wait_ge(pool_d, v.next("pool_d", 2))
            for t in range(2):
                b = bank(n)
                te.matmul(b, poolw[:, t, :], zc[:, 6 + t, :], start=True, stop=True).then_inc(lin_full, v.tick("lin_full"))
                n += 1
            pe.wait_ge(lin_out, v.count("lin_out", 0))
            for m in range(24):
                t, hh = m // 8 + 1, m % 8
                r = slice(64 * (hh % 2), 64 * (hh % 2) + 64)
                if m >= 2:
                    pe.wait_ge(ix_relu, v.next("ix_relu"))
                te.matmul(ps[:, B_S + m % 2, 0:P * (t + 1)], iq[r, hh // 2, P * t:P * t + P],
                                   ik[r, 0:P * (t + 1)], start=True, stop=True).then_inc(ix_full, v.tick("ix_full"))
            pe.wait_ge(ix_relu, v.next("ix_relu", 2))
            attend(b2_units, p2_sb, pt2_sb)
            pe.wait_ge(act_ready, v.next("act_ready", 4))
            for c in range(4):
                n = linear(n, C2_OUT + c, 2, KT, 256, h)
            norm_x()
            norm_x()
            for c in range(H2T):
                n = linear(n, C2_GU + c, 2, KT, 256, h, wait="act_ready" if c == 0 else None)
            for t in range(KT):
                b = bank(n)
                for half in range(2):
                    wh, wl = chunk(C2_DOWN + 2 * t + half)
                    for k in range(11):
                        kk_ = 11 * half + k
                        if t == 0:
                            pe.wait_ge(act_ready, v.next("act_ready"))
                        ins = three(b, (wh[:, P * k:P * k + P], wl[:, P * k:P * k + P]),
                                    (h2_hi[:, kk_, :], h2_lo[:, kk_, :]), kk_ == 0, kk_ == H2T - 1)
                    if half == 0:
                        ins.then_inc(half_used, v.tick("half_used"))
                ins.then_inc(lin_full, v.tick("lin_full"))
                n += 1
            norm_x()
            norm_x()
            pe.wait_ge(p_in, v.next("p_in", 1, 16))
            for t in range(2):
                b = bank(n)
                for k in range(TT):
                    ins = te.transpose(b[:, P * k:P * k + P], pin[:, k, P * t:P * t + P], ident[:])
                ins.then_inc(lin_full, v.tick("lin_full"))
                n += 1
            for c in range(4):
                n = linear(n, C2_PG + c, 2, KT, 256, h, wait="act_ready" if c == 0 else None)
            n = linear(n, C2_PP, KT, 2, 1024, lambda k: (pT_hi[:, k, :], pT_lo[:, k, :]),
                       wait="act_ready")
            pe.wait_ge(x_ready, v.next("x_ready", 3 * KT))
            for t in range(TT):
                for k in range(2):
                    b = bank(n)
                    for f in range(4):
                        ins = te.transpose(b[:, P * f:P * f + P], x[:, 4 * k + f, P * t:P * t + P],
                                           ident[:])
                    ins.then_inc(lin_full, v.tick("lin_full"))
                    n += 1

    return made


def host_constants():
    p = np.arange(P)
    f32 = np.float32
    ident = np.eye(P, dtype=f32)
    ones = np.ones((P, P), f32)
    namask = np.full((P, 3, 32, 8), NEG, f32)
    for kind, (tile, c0) in enumerate(((0, 0), (1, 8), (3, 32))):
        col = 16 * tile + p // 8
        start = np.clip(col - 8, 0, COLS - 16)
        j = c0 + np.arange(32)
        ok = (j[None] >= start[:, None]) & (j[None] < start[:, None] + 16)
        namask[:, kind][ok] = 0.0
    invf = np.empty((P, 2), f32)
    invf[:, 0] = f32(1.0) / np.power(f32(10000.0), (np.arange(0, 32, 2, dtype=f32) / f32(32)))[p % 16]
    invf[:, 1] = np.where(p % 32 < 16, -1.0, 1.0)
    dist = np.arange(S)
    n = np.maximum(dist, 0)
    nf = np.maximum(n, 1).astype(f32)
    large = 16 + (np.log(nf / f32(16)) / f32(np.log(8.0)) * f32(16)).astype(np.int32)
    bucket = np.where(n < 16, n, np.minimum(large, 31))
    onehot = (np.arange(32)[:, None] == bucket[None]).astype(f32)
    pcnt = np.empty((P, 2, S), f32)
    for t in range(2):
        for k in range(2):
            pcnt[64 * k:64 * k + 64, t] = 1.0 / np.minimum(np.arange(S) + 1, 2 ** (2 * t + k + 1))
    caus = np.where(p[None] > p[:, None], NEG, 0.0).astype(f32)
    return dict(ident=ident, ones=ones, namask=namask.reshape(P, 3, 256), invf=invf, onehot=onehot,
                pcnt=pcnt, caus=caus)


def chunks(w, cols):
    k, n = w.shape
    c = w.reshape(k // P, P, n // cols, cols).transpose(2, 1, 0, 3).reshape(n // cols, P, -1)
    return np.pad(c, ((0, 0), (0, 0), (0, CH - c.shape[2])))


def columns(v):
    return v.reshape(-1, P).T


def kernel(**inputs):
    import concourse.bacc as bacc
    from concourse.bass_utils import run_bass_kernel_spmd

    i = {k: np.asarray(v) for k, v in inputs.items()}
    stream, vec1 = [], []
    for l in range(DEPTH):
        w = i["w_in"][l]
        kr = w[:, 1920:1952]
        stream += [chunks(w[:, 0:512], 256), chunks(w[:, 512:1024], 256), chunks(w[:, 1024:1536], 256),
                   chunks(w[:, 1536:1792], 256),
                   chunks(np.concatenate([w[:, 1792:1920], kr, kr[:, 16:], kr[:, :16],
                                          np.zeros((D, 64), w.dtype)], 1), 256)]
        uq = i["w_uq"][l].reshape(256, 8, 96)
        stream.append(chunks(np.concatenate([
            uq[:, :, :64].reshape(256, 512), uq[:, :, 64:].reshape(256, 256),
            np.concatenate([uq[:, :, 80:], uq[:, :, 64:80]], 2).reshape(256, 256)], 1), 1024))
        ukv = i["w_ukv"][l].reshape(P, 8, 128)
        stream.append(chunks(np.concatenate([ukv[:, :, :64].reshape(P, 512),
                                             ukv[:, :, 64:].reshape(P, 512)], 1), 1024))
        for k, br in enumerate(("w_br_na", "w_br_mla")):
            stream += [chunks(w[:, 1952 + D * k:1952 + D * k + D], 256), chunks(i[br][l], 512)]
        stream.append(chunks(i["w_out"][l], 256))
        for j in range(FFJ):
            stream += [chunks(i["w_ff1"][l][:, D * j:D * j + D], 256),
                       chunks(i["w_ff2"][l][D * j:D * j + D], 256)]
        vec1.append(np.concatenate([columns(i[k][l]) for k in ("g_mix", "g_mlp", "b_gate", "g_q", "g_kv")], 1))
    w = i["w_in_2"][0]
    o = np.cumsum([0] + [256] * 7 + [512, 64, 8, 256, 256, 256])
    part = lambda k: w[:, o[k]:o[k + 1]]
    for k in (0, 1, 2, 3, 4, 5, 10, 11, 7):
        stream.append(chunks(part(k), 256))
    stream.append(chunks(np.concatenate([part(8), part(8), part(9), np.zeros((D, 120), w.dtype)], 1), 256))
    stream += [chunks(part(6), 256), chunks(part(12), 256), chunks(i["w_out_2"][0], 256)]
    gu = i["w_gate_up_2"][0].reshape(D, 2, H2T, P).transpose(0, 2, 1, 3).reshape(D, -1)
    stream.append(chunks(gu, 256))
    down = chunks_down(i["w_down_2"][0])
    stream += [down, chunks(i["w_ple_gate_2"][0], 256), chunks(i["w_ple_proj_2"][0], 1024)]
    stream = np.concatenate(stream)
    assert stream.shape == (N_CHUNK, P, CH)

    ada = i["w_ada"].reshape(DEPTH, KT, P, 6, D).transpose(0, 3, 1, 2, 4).reshape(-1, P, D)
    rpb = np.zeros((DEPTH, NAH, 16, 48), np.float32)
    rpb[:, :, :15, 16:47] = i["rpb"]
    rpb = rpb.reshape(DEPTH, NAH, -1)[:, :, ::-1]
    poolw = np.zeros((P, 2, P), np.float32)
    for k in range(4):
        r = slice(64 * (k % 2), 64 * (k % 2) + 64)
        poolw[r, k // 2, r] = i["pool_w_2"][0, k]
    vec2 = np.concatenate([columns(v) for v in (
        i["g_final"], i["g_mix_pre_2"][0], i["pool_scale_2"][0], i["conv_w_2"][0].reshape(-1),
        i["g_mix_post_2"][0], i["g_ffn_pre_2"][0], i["g_ffn_post_2"][0], i["g_ple_2"][0])], 1)
    arrays = dict(
        x=i["x"], positions=i["positions"], w_stream=stream, w_ada=ada,
        vec1=np.stack(vec1, 1), vec2=vec2,
        bada=np.concatenate([columns(i["b_ada"][l]) for l in range(DEPTH)], 1), cT=columns(i["c"]),
        rpb_rev=rpb, relT=i["rel_bias_2"].T, poolw=poolw, p_2=i["p_2"], **host_constants())
    arrays = {k: np.ascontiguousarray(v) for k, v in arrays.items()}

    counts = {}
    for final in (False, True):
        nc = bacc.Bacc("TRN2", target_bir_lowering=False, num_devices=1)
        aps = {k: nc.dram_tensor("in_" + k, v.shape, mybir.dt.from_np(v.dtype), kind="ExternalInput").ap()
               for k, v in arrays.items()}
        out = nc.dram_tensor("out", (1, S, D), F32, kind="ExternalOutput").ap()
        made = build(nc, counts, aps, out)
        counts = {k: (m[0], m[1], m[2]) for k, m in made.items()}
    r = run_bass_kernel_spmd(nc, [{"in_" + k: v for k, v in arrays.items()}], core_ids=[0])
    return r.results[0]["out"]


def chunks_down(w):
    c = w.reshape(2, 11, P, KT, P).transpose(3, 0, 2, 1, 4).reshape(2 * KT, P, 11 * P)
    return np.pad(c, ((0, 0), (0, 0), (0, CH - 11 * P)))
```

```python
from collections import Counter
from contextlib import ExitStack, contextmanager

import numpy as np

import concourse.bass as bass
from concourse import mybir

F32 = mybir.dt.float32
F32R = mybir.dt.float32r
I32 = mybir.dt.int32
ALU = mybir.AluOpType
ACT = mybir.ActivationFunctionType
AX = mybir.AxisListType

P = 128
D = 1024
S = 512
KT = D // P
TT = S // P
DEPTH = 2
CH = 2048
NEG = -1.0e30
TAKEN = -3.0e38
EPS = 1e-6
ROWS, COLS = 8, 64
NAH = MLAH = 8
HD = 64
C_Q, C_K, C_V, C_CQ, C_CKV, C_UQ, C_UKV = 0, 2, 4, 6, 7, 8, 9
C_GNA, C_BNA, C_GMLA, C_BMLA, C_OUT, C_FF = 10, 14, 16, 20, 22, 26
FFJ = 4
C_LAYER = C_FF + 8 * FFJ
C2_IX, C2_Z, C2_V, C2_OUT, C2_GU, C2_DOWN, C2_PP, C2_PG, C2_END = 0, 3, 11, 13, 17, 39, 55, 56, 60
H2T = 22
N_CHUNK = DEPTH * C_LAYER + C2_END
ADA_PRO = 4
ADA_LAY = 4
V_GMIX, V_GMLP, V_BG, V_GQ, V_GKV, NV1 = 0, 8, 16, 32, 34, 35
W_GF, W_PRE, W_PS, W_CW, W_MPOST, W_FPRE, W_FPOST, W_PLE, NV2 = 0, 8, 16, 18, 24, 32, 40, 48, 56
M_SHA, M_SCA, M_GA, M_SHM, M_SCM, M_GM = (NV1 + 8 * i for i in range(6))


class View:

    def __init__(self, eng, made, per, entered):
        self.eng, self.made, self.per, self.entered = eng, made, per, entered
        self.n = Counter()
        self.p = Counter()
        self.l = None
        self.j = None
        self.last = False

    def value(self, name, n):
        prologue, layer, ff = self.per.get(name, (0, 0, 0))
        if self.l is not None:
            n = self.l * (layer + FFJ * ff) + (prologue + n)
        if self.j is not None:
            n = n + self.j * ff
        return n

    def next(self, name, k=1, unit=1):
        self.n[name] += k * unit
        return self.value(name, self.n[name])

    def count(self, name, k):
        return self.value(name, self.n[name] + k)

    def skip(self, name, k=1):
        self.n[name] += k

    def own(self, name):
        return self.value(name, self.p[name])

    def tick(self, name, unit=1):
        frame = 0 if self.l is None else 3 if self.last else 2 if self.j is not None else 1
        self.made[name][frame] += unit
        self.p[name] += unit
        return unit

    @contextmanager
    def layers(self):
        self.n, self.p = Counter(), Counter()
        with self.eng.Fori(0, DEPTH) as l:
            self.l = l
            yield
        self.enter_block2()

    def enter_block2(self):
        self.n, self.p = Counter(), Counter()
        self.l = DEPTH
        self.last = True

    @contextmanager
    def ff(self):
        n0, p0 = Counter(self.n), Counter(self.p)
        self.eng.sem_inc(self.entered)
        with self.eng.Fori(0, FFJ) as j:
            self.j = j
            yield
        self.j = None
        self.n, self.p = n0, p0
        for name, (_, _, ff) in self.per.items():
            self.n[name] += FFJ * ff
            self.p[name] += FFJ * ff


SIGNALS = """
x_in consts_in pos_in c_sig ang_ready sin_done pool_step x_added add_ready vec_ready lin_full
lin_out sq_ready sq_used std_ready scaled_ready hi_ready act_ready x_ready vodd_in bias_in s_full
max_ready exp_done p_ready pt_full pt_copied pv_done o_copied permuted rope_done osplit_hi
osplit_ready merged_ready square_ready small2_in rel_ready rel_out wide_in ix_full ix_relu ix_used
ya_ready pool_d o_hi prod_ready p_in dve_chain fin_out sum_step ada2_used acc_ready diag_ready
rstd_full p_full vec2_ready half_used bias_step
""".split()


def build(nc, per, a, out):
    made = {n: [0, 0, 0, 0] for n in SIGNALS}
    with ExitStack() as ctx:
        def sem(name):
            return ctx.enter_context(nc.semaphore(name))

        x_in = sem("x_in")
        consts_in = sem("consts_in")
        pos_in = sem("pos_in")
        c_sig = sem("c_sig")
        ang_ready = sem("ang_ready")
        pool_step = sem("pool_step")
        add_ready = sem("add_ready")
        x_added = sem("x_added")
        sin_done = sem("sin_done")
        vec_ready = sem("vec_ready")
        lin_full = sem("lin_full")
        lin_out = sem("lin_out")
        sq_ready = sem("sq_ready")
        sq_used = sem("sq_used")
        std_ready = sem("std_ready")
        scaled_ready = sem("scaled_ready")
        hi_ready = sem("hi_ready")
        act_ready = sem("act_ready")
        x_ready = sem("x_ready")
        vodd_in = sem("vodd_in")
        bias_in = sem("bias_in")
        s_full = sem("s_full")
        max_ready = sem("max_ready")
        exp_done = sem("exp_done")
        p_ready = sem("p_ready")
        pt_full = sem("pt_full")
        pt_copied = sem("pt_copied")
        pv_done = sem("pv_done")
        o_copied = sem("o_copied")
        permuted = sem("permuted")
        rope_done = sem("rope_done")
        osplit_hi = sem("osplit_hi")
        osplit_ready = sem("osplit_ready")
        merged_ready = sem("merged_ready")
        square_ready = sem("square_ready")
        small2_in = sem("small2_in")
        rel_ready = sem("rel_ready")
        rel_out = sem("rel_out")
        wide_in = sem("wide_in")
        ix_full = sem("ix_full")
        ix_relu = sem("ix_relu")
        ix_used = sem("ix_used")
        ya_ready = sem("ya_ready")
        pool_d = sem("pool_d")
        o_hi = sem("o_hi")
        prod_ready = sem("prod_ready")
        p_in = sem("p_in")
        dve_chain = sem("dve_chain")
        fin_out = sem("fin_out")
        sems = dict(osplit_ready=osplit_ready, act_ready=act_ready, o_copied=o_copied)
        raw_landed = [sem(f"raw_landed{k}") for k in range(2)]
        ada_landed = [sem(f"ada_landed{k}") for k in range(KT)]
        ada2_landed = [sem(f"ada2_landed{k}") for k in range(2)]
        ada_used = sem("ada_used")
        ada_sum = sem("ada_sum")
        ada_full = sem("ada_full")
        ada_taken = sem("ada_taken")
        cact_ready = sem("cact_ready")
        sum_step = sem("sum_step")
        ada2_used = sem("ada2_used")
        acc_ready = sem("acc_ready")
        diag_ready = sem("diag_ready")
        rstd_full = sem("rstd_full")
        p_full = sem("p_full")
        vec2_ready = sem("vec2_ready")
        bias_step = sem("bias_step")
        half_used = sem("half_used")
        w_hi = sem("w_hi")
        w_split = sem("w_split")
        mlp_entered = sem("mlp_entered")

        top = [nc.sbuf_base + (-nc.sbuf_base) % 64]

        def fixed(name, shape, dt=F32):
            t = nc.alloc_sbuf_tensor_at(name, [P] + shape, dt, offset=top[0])
            top[0] += (4 * int(np.prod(shape)) + 31) // 32 * 32
            return t

        x = fixed("x", [KT, S])
        act0 = top[0]
        act_hi = fixed("act_hi", [KT, S], F32R)
        act_lo = fixed("act_lo", [KT, S], F32R)
        raw = fixed("raw", [2, CH])
        whi = fixed("whi", [2, CH], F32R)
        wlo = fixed("wlo", [2, CH], F32R)
        ident = fixed("ident", [P])
        ones = fixed("ones", [P])
        sq = fixed("sq", [2, S])
        std = fixed("std", [S])
        diag = fixed("diag", [TT, P])
        rms = fixed("rms", [2, TT])
        ssum = fixed("ssum", [S])
        tmp = fixed("tmp", [2, S])
        cur = fixed("cur", [NV1 + 48])
        scl = fixed("scl", [2, KT])
        vec1 = fixed("vec1", [DEPTH, NV1])
        vec2 = fixed("vec2", [NV2])
        mod = fixed("mod", [DEPTH, 48])
        modf = mod[:].rearrange("p l m -> p (l m)")
        nmax = fixed("nmax", [4, 1])
        rsum = fixed("rsum", [4, 1])
        rinv = fixed("rinv", [4, 1])
        cact = fixed("cact", [KT])
        modraw = fixed("modraw", [32])
        eps = fixed("eps", [1])
        iw = fixed("iw", [TT, 8])
        top8 = fixed("top8", [8])
        rope0 = top[0]
        cosT = fixed("cosT", [S])
        sinT = fixed("sinT", [S])
        namask = fixed("namask", [3, 256])
        arena0 = top[0]
        arena_end = nc.sbuf_usable_end

        def at(name, kb, shape, dt=F32):
            off = arena0 + int(kb * 1024)
            assert off + 4 * int(np.prod(shape)) <= arena_end, (name, kb, arena0, arena_end)
            return nc.alloc_sbuf_tensor_at(name, [P] + shape, dt, offset=off)

        ada = at("ada", 0, [KT, D])
        acc = at("acc", 62, [2, D])
        xin = at("xin", 32, [TT, D])
        cT = at("cT", 49, [KT])
        csig = at("csig", 49.5, [KT])
        posi = at("posi", 50, [S], I32)
        ang = at("ang", 52, [2, S])
        kk = at("kk", 56, [2, S])
        invf = at("invf", 60, [2])
        prod = at("prod", 70, [2, S])
        o_na = at("o_na", 0, [4, S])
        o_mla = at("o_mla", 8, [4, S])
        QT = at("QT", 16, [4, S])
        KTn = at("KTn", 24, [4, S])
        Ve = at("Ve", 32, [TT, S])
        Vo = at("Vo", 40, [3, S])
        relt = at("relt", 46, [NAH, 384])
        comb = at("comb", 58, [2, 3, 256])
        p_sb = at("p_sb", 64, [4, S])
        pt_sb = at("pt_sb", 72, [2, S])
        s_sb = at("s_sb", 76, [2, S])
        ada2 = at("ada2", 80, [2, D])
        acc_na = at("acc_na", 8, [D])
        acc_mla = at("acc_mla", 56, [D])
        qT = at("qT", 16, [MLAH, S])
        kT = at("kT", 32, [MLAH, S])
        Vm = at("Vm", 48, [TT, S])
        craw = at("craw", 56, [3, S])
        cn_hi = at("cn_hi", 62, [3, S], F32R)
        cn_lo = at("cn_lo", 68, [3, S], F32R)
        rraw = at("rraw", 8, [4, S])
        rmul = at("rmul", 74, [2, S])
        gsig = at("gsig", 16, [KT, S])
        os_hi = at("os_hi", 32, [4, S], F32R)
        os_lo = at("os_lo", 40, [4, S], F32R)
        merged = at("merged", 48, [KT, S])
        ybuf = at("ybuf", 64, [2, S])
        hid_hi = at("hid_hi", 16, [KT, S], F32R)
        hid_lo = at("hid_lo", 32, [KT, S], F32R)
        rel_u = at("rel_u", 68, [2, S])
        squ = at("squ", 72, [2, S])
        zc = at("zc", 0, [8, S])
        zq = at("zq", 16, [8, S])
        iq = at("iq", 32, [4, S])
        ik = at("ik", 40, [S])
        V2 = at("V2", 42, [TT, S])
        wide = at("wide", 50, [8, S])
        selm = at("selm", 66, [1152])
        ixr = at("ixr", 70.5, [2, S])
        p2_sb = at("p2_sb", 0, [4, S])
        pt2_sb = at("pt2_sb", 8, [2, S])
        s2_sb = at("s2_sb", 12, [2, S])
        relT = at("relT", 16, [8])
        iwT = at("iwT", 42, [S])
        onehot = at("onehot", 17, [S])
        relrow = at("relrow", 20, [640])
        caus = at("caus", 85, [P])
        poolw = at("poolw", 86, [2, P])
        pcnt = at("pcnt", 74.5, [2, S])
        ct = at("ct", 78.5, [3, S])
        mixr = at("mixr", 0, [KT, S])
        h2_hi = at("h2_hi", 0, [H2T, S], F32R)
        h2_lo = at("h2_lo", 44, [H2T, S], F32R)
        fraw = nc.alloc_sbuf_tensor_at("fraw", [P, KT, S], F32, offset=act0)
        pin = tmp[:].rearrange("p a (b c) -> p (a b) c", b=2)
        pT_hi = nc.alloc_sbuf_tensor_at("pT_hi", [P, 2, S], F32R, offset=rope0)
        pT_lo = at("pT_lo", 12, [2, S], F32R)
        pj = at("pj", 48, [KT, S])
        pg = at("pg", 16, [KT, S])
        outb = at("outb", 32, [TT, D])

        ps = ctx.enter_context(nc.psum_tensor("ps", [P, 8, 512], F32))
        B_S, B_T, B_O, B_N = 2, 4, 6, 7
        rstd = ps[:, B_N, :]
        relscr = nc.dram_tensor("relscr", (8, 640), F32).ap()

        def backward(t, o, n):
            a0 = t[:]
            return bass.AP(tensor=a0.tensor, offset=a0.offset + o, ap=[list(a0.ap[0]), [-1, n]])

        na_units, mla_units, b2_units = [], [], []
        for h in range(NAH):
            r0 = 64 * (h % 2)
            for q in range(TT):
                c0 = (0, 8, 24, 32)[q]
                vs = []
                for b in range(2):
                    c = c0 + 16 * b
                    vs.append((Ve if c % 16 == 0 else Vo)[:, c // 16, h * HD:(h + 1) * HD])
                na_units.append(dict(
                    q=QT[r0:r0 + 64, h // 2, q * P:(q + 1) * P],
                    k=KTn[r0:r0 + 64, h // 2, 8 * c0:8 * c0 + 256],
                    n=256, bias=comb[:, h % 2, (0, 1, 1, 2)[q], :], sel=None, v=vs, head=h, t=q))
        for h in range(MLAH):
            for q in range(TT):
                mla_units.append(dict(
                    q=qT[0:96, h, q * P:(q + 1) * P], k=kT[0:96, h, :], n=S, bias=None, sel=None,
                    v=[Vm[:, b, h * HD:(h + 1) * HD] for b in range(TT)], head=h, t=q))
        for h in [4, 5, 6, 7, 0, 1, 2, 3]:
            r0 = 64 * (h % 2)
            zt = (0 if h < 4 else 4) + (h % 4) // 2
            for q in range(TT):
                n = P * (q + 1)
                s0 = (0, 0, 256, 640)[q]
                b2_units.append(dict(
                    q=zq[r0:r0 + 64, zt, q * P:(q + 1) * P], k=zq[r0:r0 + 64, zt + 2, 0:n], n=n,
                    bias=backward(wide, h * S + n - 1, n), sel=selm[:, s0:s0 + n] if h < 4 and q else None,
                    v=[V2[:, b, h * HD:(h + 1) * HD] for b in range(q + 1)], head=h, t=q))

        def rpb_rows(l, h):
            o = a["rpb_rev"][bass.ds(l, 1), h]
            return bass.AP(tensor=o.tensor, offset=o.offset + 33, ap=[[1, 16], [48, 8], [1, 384]])

        def rel_wide(h):
            return bass.AP(tensor=relscr.tensor, offset=640 * h, ap=[[1, P], [1, S]])

        block = ctx.enter_context(nc.Block())

        @block.sync
        def _(sp):
            v = View(sp, made, per, mlp_entered)
            xv = a["x"].rearrange("o (r c) d -> (o c) r d", r=ROWS)
            for t in range(TT):
                sp.dma_start(xin[:, t, :], xv[16 * t:16 * t + 16]).then_inc(x_in, v.tick("x_in", 16))
            for dst, src in ((ident, "ident"), (ones, "ones"), (namask, "namask"), (vec1, "vec1"),
                             (vec2, "vec2"), (modf, "bada"), (cT, "cT"), (invf, "invf")):
                sp.dma_start(dst if dst is modf else dst[:], a[src]).then_inc(consts_in, v.tick("consts_in", 16))
            sp.dma_start(posi[:], a["positions"].broadcast_to((P, S))).then_inc(pos_in, v.tick("pos_in", 16))
            for k in range(KT):
                sp.dma_start(ada[:, k, :], a["w_ada"][k]).then_inc(ada_landed[k], 16)
            for k in range(2):
                sp.dma_start(raw[:, k, :], a["w_stream"][k]).then_inc(raw_landed[k], 16)
            with sp.Fori(1, ADA_PRO) as i:
                for k in range(KT):
                    sp.wait_ge(ada_used, KT * i + (k + 1 - KT))
                    sp.dma_start(ada[:, k, :], a["w_ada"][bass.ds(KT * i + k, 1)]
                                 .rearrange("o p f -> (o p) f")).then_inc(ada_landed[k], 16)
            with sp.Fori(1, N_CHUNK // 2) as i:
                for k in range(2):
                    sp.wait_ge(w_split, 2 * i + (k - 1))
                    sp.dma_start(raw[:, k, :], a["w_stream"][bass.ds(2 * i + k, 1)]
                                 .rearrange("o p f -> (o p) f")).then_inc(raw_landed[k], 16)

        @block.gpsimd
        def _(pool):
            v = View(pool, made, per, mlp_entered)
            gp = nc.gpsimd

            def step(ins):
                ins.then_inc(pool_step, v.tick("pool_step"))
                pool.wait_ge(pool_step, v.own("pool_step"))

            def split_lo(k, n):
                pool.wait_ge(w_hi, n)
                gp.tensor_tensor(wlo[:, k, :], raw[:, k, :], whi[:, k, :].bitcast(F32),
                                 ALU.subtract).then_inc(w_split, 1)

            def split_pairs(first, last):
                with pool.Fori(first // 2, last // 2) as i:
                    for k in range(2):
                        split_lo(k, 2 * i + (k + 1))

            def add_to_x():
                for t in range(KT):
                    pool.wait_ge(add_ready, v.next("add_ready"))
                    gp.tensor_tensor(x[:, t, :], x[:, t, :], tmp[:, t % 2, :],
                                     ALU.add).then_inc(x_added, v.tick("x_added"))

            pool.wait_ge(pos_in, v.next("pos_in", 1, 16))
            pool.wait_ge(consts_in, v.next("consts_in", 8, 16))
            step(gp.tensor_copy(kk[:, 0, :].rearrange("p (c r) -> p c r", r=ROWS),
                                posi[:].rearrange("p (r c) -> p c r", r=ROWS)))
            step(gp.tensor_scalar(ang[:, 0, :], kk[:, 0, :], invf[:, 0:1], None, ALU.mult))
            big = 12582912.0
            step(gp.tensor_scalar(kk[:, 0, :], ang[:, 0, :], 0.5 / np.pi, 0.0, ALU.mult, ALU.add))
            step(gp.tensor_scalar(kk[:, 1, :], ang[:, 0, :], 0.5 / np.pi, 0.25, ALU.mult, ALU.add))
            step(gp.tensor_scalar(kk[:], kk[:], big, None, ALU.add))
            step(gp.tensor_scalar(kk[:], kk[:], big, None, ALU.subtract))
            c1 = 6.28125
            c2 = float(np.float32(np.round((2 * np.pi - c1) * 2 ** 20) / 2 ** 20))
            c3 = float(2 * np.pi - c1 - c2)
            step(gp.tensor_copy(ang[:, 1, :], ang[:, 0, :]))
            for c in (c1, c2, c3):
                step(gp.tensor_scalar(prod[:], kk[:], c, None, ALU.mult))
                step(gp.tensor_tensor(ang[:], ang[:], prod[:], ALU.subtract))
            step(gp.tensor_scalar(ang[:, 1, :], ang[:, 1, :], float(np.pi / 2), None, ALU.add))
            step(gp.tensor_scalar(ang[:], ang[:], -3.1415925, 3.1415925, ALU.max, ALU.min))
            gp.tensor_scalar(ang[:, 0, :], ang[:, 0, :], invf[:, 1:2], None,
                             ALU.mult).then_inc(ang_ready, v.tick("ang_ready"))

            v.enter_block2()
            first = DEPTH * C_LAYER
            mixed, fed = first + C2_GU + 2, first + C2_PP + 2
            split_pairs(0, mixed - 1)
            split_lo(0, mixed)
            add_to_x()
            split_lo(1, mixed + 1)
            split_pairs(mixed + 1, fed - 1)
            split_lo(0, fed)
            add_to_x()
            for c in range(fed, N_CHUNK):
                split_lo(c % 2, c + 1)

        @block.scalar
        def _(act):
            v = View(act, made, per, mlp_entered)
            sc = nc.scalar

            def split_hi(c):
                k = c % 2
                if v.l is None:
                    n = 16 * (c // 2 + 1)
                else:
                    if v.last and c >= C2_END:
                        return
                    n = v.l * (8 * C_LAYER) + 16 * (c // 2 + 1)
                    if v.j is not None:
                        n = n + v.j * 64
                act.wait_ge(raw_landed[k], n)
                sc.activation(whi[:, k, :], raw[:, k, :], ACT.Copy).then_inc(w_hi, 1)

            def evac(i, dst, func=ACT.Copy, rows=slice(0, P), cols=S, **kw):
                act.wait_ge(lin_full, v.next("lin_full"))
                sc.activation(dst, ps[rows, i % 2, 0:cols], func, **kw).then_inc(lin_out, v.tick("lin_out"))
                act.wait_ge(lin_out, v.own("lin_out"))
                v.skip("lin_out")

            def square(t, src):
                if t >= 2:
                    act.wait_ge(sum_step, v.next("sum_step"))
                sc.activation(sq[:, t % 2, :], src, ACT.Square).then_inc(sq_ready, v.tick("sq_ready"))
                if t == KT - 1:
                    act.wait_ge(sum_step, v.next("sum_step", 2))

            def norm(n_tiles, dim, src=None, hi=None, shift=None):
                for t in range(n_tiles if src else 0):
                    sc.activation(sq[:, t % 2, :], src(t), ACT.Square).then_inc(sq_ready, v.tick("sq_ready"))
                act.wait_ge(sq_used, v.next("sq_used"))
                sc.activation(rms[:, 0, :], ps[:, B_N, 0:TT], ACT.Sqrt, bias=eps[:, 0:1],
                              scale=1.0 / dim).then_inc(std_ready, v.tick("std_ready"))
                act.wait_ge(std_ready, v.own("std_ready"))
                for t in range(n_tiles if hi else 0):
                    act.wait_ge(scaled_ready, v.next("scaled_ready"))
                    if shift is None:
                        ins = sc.activation(hi(t), tmp[:, t % 2, :], ACT.Copy)
                    else:
                        ins = sc.activation(hi(t), tmp[:, t % 2, :], ACT.Identity, bias=shift(t))
                    ins.then_inc(hi_ready, v.tick("hi_ready"))

            def load_ada(h):
                act.dma_start(ada2[:, h % 2, :],
                              a["w_ada"][bass.ds(v.l * (KT * ADA_LAY) + (KT * ADA_PRO + h), 1)]
                              .rearrange("o p f -> (o p) f")).then_inc(ada2_landed[h % 2], 16)

            def attend(units, p, pt, sb, n=0, ada0=None):
                for i in range(len(units) + 4):
                    u = i - 3
                    if 0 <= u < len(units):
                        w = units[u]["n"]
                        act.wait_ge(pt_full, v.count("pt_full", u + 1))
                        if u >= 2:
                            act.wait_ge(pv_done, v.count("pv_done", u - 1))
                        sc.activation(pt[:, u % 2, 0:w], ps[:, B_T + u % 2, 0:w],
                                      ACT.Copy).then_inc(pt_copied, v.tick("pt_copied"))
                    if i < len(units):
                        w = units[i]["n"]
                        biased = units[i]["bias"] is not None
                        act.wait_ge(max_ready, v.count("max_ready", i + 1))
                        src = sb[:, i % 2, 0:w] if biased else ps[:, B_S + i % 2, 0:w]
                        sc.activation(p[:, i % 4, 0:w], src, ACT.Exp, bias=nmax[:, i % 4, :],
                                      scale=-1.0 if biased else 1.0,
                                      accum_out=rsum[:, i % 4, :]).then_inc(exp_done, v.tick("exp_done"))
                    u = i - 4
                    if units is b2_units and u >= 0 and u % 8 == 7:
                        act.wait_ge(pv_done, v.count("pv_done", u + 1))
                        sc.activation(act_hi[:, (6, 7, 4, 5)[u // 8], :], ps[:, B_O, :],
                                      ACT.Copy).then_inc(o_hi, v.tick("o_hi"))
                    if ada0 is not None and i % 2 and i < len(units):
                        h = ada0 + i // 2
                        act.wait_ge(ada2_used, v.next("ada2_used"))
                        if h + 2 < KT * ADA_LAY:
                            load_ada(h + 2)
                    if ada0 is not None and i in (17, len(units) + 3):
                        w = (ada0 // KT) + (i > 17)
                        evac(n + (i > 17), modraw[:, 8 * w:8 * w + 8], cols=8)
                act.wait_ge(pt_copied, v.own("pt_copied"))
                v.skip("max_ready", len(units))
                v.skip("pt_full", len(units))
                v.skip("pv_done", len(units))
                act.wait_ge(o_copied, v.next("o_copied", len(units) // 8))

            act.wait_ge(consts_in, v.next("consts_in", 8, 16))
            sc.activation(csig[:], cT[:], ACT.Sigmoid).then_inc(c_sig, v.tick("c_sig"))
            act.wait_ge(c_sig, v.own("c_sig"))
            for t in range(KT):
                evac(t, x[:, t, :])
                square(t, x[:, t, :])
            for c in range(2):
                split_hi(c)
            act.wait_ge(ang_ready, v.next("ang_ready"))
            sc.activation(sinT[:], ang[:, 0, :], ACT.Sin)
            sc.activation(cosT[:], ang[:, 1, :], ACT.Sin).then_inc(sin_done, v.tick("sin_done"))
            act.wait_ge(sin_done, v.own("sin_done"))

            with v.layers():
                act.wait_ge(vec_ready, v.next("vec_ready"))
                norm(KT, D, hi=lambda t: act_hi[:, t, :],
                     shift=lambda t: cur[:, M_SHA + t:M_SHA + t + 1])
                for h in range(2):
                    load_ada(h)
                for h in range(NAH):
                    act.dma_start(relt[:, h, :], rpb_rows(v.l, h)).then_inc(bias_in, v.tick("bias_in", 16))
                n = 0
                for c in range(C_Q, C_V):
                    for i in range(2):
                        evac(n, (QT if c < C_K else KTn)[:, 2 * (c % 2) + i, :],
                             scale=HD ** -0.5 if c < C_K else 1.0)
                        n += 1
                    split_hi(c + 2)
                for c in range(C_V, C_CQ):
                    for t in range(TT):
                        evac(n, Ve[:, t, 256 * (c - C_V):256 * (c - C_V) + 256], cols=256)
                        n += 1
                    split_hi(c + 2)
                for o in range(3):
                    act.dma_start(Vo[0:64, o, :], Ve[64:128, o, :]).then_inc(vodd_in, v.tick("vodd_in", 16))
                    act.dma_start(Vo[64:128, o, :], Ve[0:64, o + 1, :]).then_inc(vodd_in, v.tick("vodd_in", 16))
                attend(na_units, p_sb, pt_sb, s_sb, n, 0)
                n += 2
                for i in range(4):
                    if i == 2:
                        norm(2, 256, src=lambda t: craw[:, t, :], hi=lambda t: cn_hi[:, t, :])
                    if i < 3:
                        evac(n, craw[:, i, :])
                    else:
                        evac(n, rraw[0:64, 2, :], rows=slice(0, 64))
                    n += 1
                    if i % 2:
                        split_hi(C_CQ + i // 2 + 2)
                norm(1, 128, src=lambda t: craw[:, 2, :], hi=lambda t: cn_hi[:, 2, :])
                for t in range(4):
                    act.wait_ge(lin_full, v.next("lin_full"))
                    b = ps[:, n % 2, :]
                    sc.activation(qT[0:64, 2 * t, :], b[0:64, :], ACT.Copy, scale=96 ** -0.5)
                    sc.activation(qT[0:64, 2 * t + 1, :], b[64:128, :], ACT.Copy,
                                           scale=96 ** -0.5).then_inc(lin_out, v.tick("lin_out"))
                    act.wait_ge(lin_out, v.own("lin_out"))
                    v.skip("lin_out")
                    n += 1
                act.wait_ge(rope_done, v.next("rope_done"))
                for t in range(4):
                    evac(n, rraw[:, t, :], scale=96 ** -0.5)
                    n += 1
                split_hi(C_UQ + 2)
                for t in range(4):
                    act.wait_ge(lin_full, v.next("lin_full"))
                    b = ps[:, n % 2, :]
                    sc.activation(kT[0:64, 2 * t, :], b[0:64, :], ACT.Copy)
                    sc.activation(kT[0:64, 2 * t + 1, :], b[64:128, :], ACT.Copy).then_inc(lin_out, v.tick("lin_out"))
                    act.wait_ge(lin_out, v.own("lin_out"))
                    v.skip("lin_out")
                    n += 1
                for t in range(TT):
                    evac(n, Vm[:, t, :])
                    n += 1
                split_hi(C_UKV + 2)
                act.wait_ge(rope_done, v.next("rope_done"))
                attend(mla_units, p_sb, pt_sb, s_sb, n, KT * ADA_LAY // 2)
                n += 2
                for br in range(2):
                    for t in range(4):
                        sc.activation(os_hi[:, t, :], (o_na, o_mla)[br][:, t, :], ACT.Copy).then_inc(osplit_hi, v.tick("osplit_hi"))
                        act.wait_ge(osplit_hi, v.own("osplit_hi"))
                    for c in range(4):
                        for i in range(2):
                            t = 2 * c + i
                            k = V_BG + 8 * br + t
                            evac(n, gsig[:, t, :], ACT.Sigmoid, bias=cur[:, k:k + 1])
                            n += 1
                        split_hi((C_GNA, C_GMLA)[br] + c + 2)
                    for c in range(2):
                        for i in range(4):
                            t = 4 * c + i
                            if t >= 2:
                                act.wait_ge(merged_ready, v.next("merged_ready"))
                            evac(n, ybuf[:, t % 2, :])
                            n += 1
                        split_hi((C_BNA, C_BMLA)[br] + c + 2)
                    act.wait_ge(merged_ready, v.next("merged_ready", 2))
                for t in range(KT):
                    sc.activation(act_hi[:, t, :], merged[:, t, :], ACT.Copy).then_inc(hi_ready, v.tick("hi_ready"))
                    act.wait_ge(hi_ready, v.own("hi_ready"))

                def residual(n, c0, gate):
                    for t in range(KT + 1):
                        if t < KT:
                            evac(n + t, ybuf[:, t % 2, :], scale=cur[:, gate + t:gate + t + 1])
                            if t % 2 and t < KT - 1:
                                split_hi(c0 + t // 2 + 2)
                        if t:
                            act.wait_ge(x_ready, v.next("x_ready"))
                            square(t - 1, x[:, t - 1, :])
                    split_hi(c0 + 5)

                act.wait_ge(vec2_ready, v.next("vec2_ready"))
                residual(n, C_OUT, M_GA)
                n += KT
                norm(KT, D, hi=lambda t: act_hi[:, t, :],
                     shift=lambda t: cur[:, M_SHM + t:M_SHM + t + 1])
                with v.ff():
                    for c in range(4):
                        for i in range(2):
                            t = 2 * c + i
                            evac(n + t, rel_u[:, t % 2, :], ACT.Relu)
                            if t:
                                act.wait_ge(square_ready, v.next("square_ready"))
                                sc.activation(hid_hi[:, t - 1, :], squ[:, (t - 1) % 2, :],
                                                       ACT.Copy).then_inc(hi_ready, v.tick("hi_ready"))
                                act.wait_ge(hi_ready, v.own("hi_ready"))
                        split_hi(C_FF + c + 2)
                    act.wait_ge(square_ready, v.next("square_ready"))
                    sc.activation(hid_hi[:, 7, :], squ[:, 1, :], ACT.Copy).then_inc(hi_ready, v.tick("hi_ready"))
                    act.wait_ge(hi_ready, v.own("hi_ready"))
                    residual(n + KT, C_FF + 4, M_GM)

            for dst, src in ((relT, "relT"), (onehot, "onehot"), (poolw, "poolw"), (pcnt, "pcnt"),
                             (caus, "caus")):
                d = dst[0:32] if dst is relT or dst is onehot else dst[:]
                act.dma_start(d, a[src]).then_inc(small2_in, v.tick("small2_in", 16))
            norm(KT, D)
            for t in range(KT):
                act.wait_ge(scaled_ready, v.next("scaled_ready"))
                sc.activation(x[:, t, :].rearrange("p (r c) -> p r c", r=ROWS),
                                       tmp[:, t % 2, :].rearrange("p (c r) -> p r c", r=ROWS),
                                       ACT.Copy).then_inc(permuted, v.tick("permuted"))
                act.wait_ge(permuted, v.own("permuted"))
            for t in range(KT):
                square(t, x[:, t, :])
            act.wait_ge(rel_ready, v.next("rel_ready"))
            act.wait_ge(lin_full, v.next("lin_full"))
            sc.activation(relrow[0:8, P - 1:P - 1 + S], ps[0:8, 0, :], ACT.Copy).then_inc(lin_out, v.tick("lin_out"))
            act.wait_ge(lin_out, v.own("lin_out"))
            act.wait_ge(lin_out, v.next("lin_out"))
            norm(KT, D, hi=lambda t: act_hi[:, t, :])
            act.dma_start(relscr[:, 0:P - 1 + S], relrow[0:8, 0:P - 1 + S]).then_inc(rel_out, v.tick("rel_out", 16))
            act.wait_ge(rel_out, v.next("rel_out", 1, 16))
            for h in range(8):
                act.dma_start(wide[:, h, :], rel_wide(h)).then_inc(wide_in, v.tick("wide_in", 16))
            n = 1
            for c in range(2):
                for i in range(2):
                    evac(n, iq[:, 2 * c + i, :])
                    n += 1
                split_hi(c + 2)
            act.wait_ge(lin_full, v.next("lin_full"))
            b = ps[:, n % 2, :]
            sc.activation(ik[0:64, :], b[0:64, :], ACT.Copy)
            sc.activation(ik[64:P, :], b[0:64, :], ACT.Copy)
            sc.activation(iwT[0:8, :], b[64:72, :], ACT.Copy,
                          scale=8 ** -0.5 * 64 ** -0.5).then_inc(lin_out, v.tick("lin_out"))
            act.wait_ge(lin_out, v.own("lin_out"))
            v.skip("lin_out")
            n += 1
            split_hi(C2_Z + 1)

            def index_relu(m):
                t = m // 8 + 1
                act.wait_ge(ix_full, v.next("ix_full"))
                if m >= 2:
                    act.wait_ge(ix_used, v.next("ix_used"))
                sc.activation(ixr[:, m % 2, 0:P * (t + 1)], ps[:, B_S + m % 2, 0:P * (t + 1)],
                              ACT.Relu).then_inc(ix_relu, v.tick("ix_relu"))

            for c in range(8):
                for i in range(2):
                    dst = zc[:, 2 * c + i, :] if c < 4 else zq[:, 2 * c - 8 + i, :]
                    evac(n, dst, scale=HD ** -0.5 if c in (4, 6) else 1.0)
                    n += 1
                    index_relu(2 * c + i)
                if c == 0:
                    evac(n, iw[:].rearrange("p t h -> p (t h)"), cols=32)
                    n += 1
                split_hi(C2_Z + c + 2)
            for t in range(2):
                evac(n, zc[:, 6 + t, :], scale=vec2[:, W_PS + t:W_PS + t + 1])
                n += 1
            for c in range(2):
                for t in range(TT):
                    evac(n, V2[:, t, 256 * c:256 * c + 256], cols=256)
                    n += 1
                    index_relu(16 + TT * c + t)
                split_hi(C2_V + c + 2)
            act.wait_ge(ya_ready, v.next("ya_ready", 2))
            for t in range(4):
                sc.activation(act_hi[:, t, :], zc[:, t if t < 2 else 4 + t, :],
                              ACT.Copy).then_inc(hi_ready, v.tick("hi_ready"))
            act.wait_ge(ix_used, v.next("ix_used", 2))
            attend(b2_units, p2_sb, pt2_sb, s2_sb)

            def added():
                for t in range(KT):
                    act.wait_ge(x_added, v.next("x_added"))
                    square(t, x[:, t, :])
                norm(KT, D, hi=lambda t: act_hi[:, t, :])

            for t in range(KT):
                evac(n, mixr[:, t, :])
                n += 1
                square(t, mixr[:, t, :])
                if t % 2:
                    split_hi(C2_OUT + t // 2 + 2)
            norm(KT, D)
            added()
            for c in range(H2T):
                act.wait_ge(lin_full, v.next("lin_full"))
                sc.activation(std[:], ps[:, n % 2, :], ACT.Sigmoid)
                sc.activation(sq[:, 0, :], ps[:, n % 2, :], ACT.Copy).then_inc(lin_out, v.tick("lin_out"))
                act.wait_ge(lin_out, v.own("lin_out"))
                v.skip("lin_out")
                evac(n + 1, sq[:, 1, :])
                n += 2
                split_hi(C2_GU + c + 2)
                act.wait_ge(prod_ready, v.next("prod_ready"))
                sc.activation(h2_hi[:, c, :], tmp[:, c % 2, :], ACT.Copy).then_inc(hi_ready, v.tick("hi_ready"))
                act.wait_ge(hi_ready, v.own("hi_ready"))
            act.wait_ge(act_ready, v.next("act_ready", KT + 4 + KT + H2T))
            act.dma_start(pin, a["p_2"].rearrange("a o (t p) d -> p (a o t) d", p=P)).then_inc(p_in, v.tick("p_in", 16))
            for t in range(KT):
                if t == 2:
                    act.wait_ge(p_full, v.next("p_full"))
                    for k in range(2):
                        sc.activation(pT_hi[:, k, :], ps[:, B_S + k, :],
                                      ACT.Copy).then_inc(hi_ready, v.tick("hi_ready"))
                act.wait_ge(half_used, v.next("half_used"))
                split_hi(C2_DOWN + 2 * t + 2)
                act.wait_ge(lin_full, v.next("lin_full"))
                sc.activation(fraw[:, t, :], ps[:, n % 2, :], ACT.Copy).then_inc(lin_out, v.tick("lin_out"))
                act.wait_ge(lin_out, v.own("lin_out"))
                v.skip("lin_out")
                n += 1
                if t < KT - 1:
                    split_hi(C2_DOWN + 2 * t + 3)
                square(t, fraw[:, t, :])
            split_hi(C2_DOWN + 2 * KT + 1)
            for t in range(2):
                evac(n, pj[:, t, :])
                n += 1
            norm(KT, D)
            for t in range(KT):
                if t + 2 < KT:
                    evac(n, pj[:, t + 2, :])
                    n += 1
                if t == KT - 2:
                    split_hi(C2_PP + 2)
                act.wait_ge(x_added, v.next("x_added"))
                square(t, x[:, t, :])
            norm(KT, D, hi=lambda t: act_hi[:, t, :])
            for c in range(4):
                for i in range(2):
                    evac(n, pg[:, 2 * c + i, :], ACT.Sigmoid)
                    n += 1
                split_hi(C2_PG + c + 2)
            for t in range(TT):
                for k in range(2):
                    evac(n, outb[:, t, S * k:S * k + S])
                    n += 1
                act.dma_start(out.rearrange("o (t p) d -> t (o p) d", p=P)[t], outb[:, t, :]).then_inc(fin_out, v.tick("fin_out", 16))
            act.wait_ge(fin_out, v.next("fin_out", TT, 16))

        @block.vector
        def _(dve):
            v = View(dve, made, per, mlp_entered)
            ve = nc.vector

            def chain(ins):
                ins.then_inc(dve_chain, v.tick("dve_chain"))
                dve.wait_ge(dve_chain, v.own("dve_chain"))

            def low(dst, src, hi, done):
                ve.tensor_tensor(dst, src, hi.bitcast(F32), ALU.subtract).then_inc(sems[done], v.tick(done))
                dve.wait_ge(sems[done], v.own(done))

            def inverse_rms():
                dve.wait_ge(std_ready, v.next("std_ready"))
                chain(ve.reciprocal(rms[:, 1, :], rms[:, 0, :]))
                ve.tensor_tensor(diag[:], ident[:].rearrange("p (o q) -> p o q", o=1).broadcast_to((P, TT, P)),
                                 rms[:, 1, :].rearrange("p (t o) -> p t o", o=1).broadcast_to((P, TT, P)),
                                 ALU.mult).then_inc(diag_ready, v.tick("diag_ready"))
                dve.wait_ge(rstd_full, v.next("rstd_full"))

            def norm(n_tiles, src, scale, hi, lo, shift=None):
                inverse_rms()
                for t in range(n_tiles + 1):
                    if t < n_tiles:
                        ve.scalar_tensor_tensor(tmp[:, t % 2, :], src(t), scale(t), rstd,
                                                         ALU.mult, ALU.mult).then_inc(scaled_ready, v.tick("scaled_ready"))
                        dve.wait_ge(scaled_ready, v.own("scaled_ready"))
                    if t:
                        dve.wait_ge(hi_ready, v.next("hi_ready"))
                        h = hi(t - 1).bitcast(F32)
                        if shift is None:
                            ins = ve.tensor_tensor(lo(t - 1), tmp[:, (t - 1) % 2, :], h, ALU.subtract)
                        else:
                            ins = ve.scalar_tensor_tensor(lo(t - 1), tmp[:, (t - 1) % 2, :],
                                                          shift(t - 1), h, ALU.add, ALU.subtract)
                        ins.then_inc(act_ready, v.tick("act_ready"))
                        dve.wait_ge(act_ready, v.own("act_ready"))

            def add_square(t):
                dve.wait_ge(sq_ready, v.next("sq_ready"))
                if t == 0:
                    ins = ve.tensor_copy(ssum[:], sq[:, 0, :])
                else:
                    ins = ve.tensor_tensor(ssum[:], ssum[:], sq[:, t % 2, :], ALU.add)
                ins.then_inc(sum_step, v.tick("sum_step"))
                dve.wait_ge(sum_step, v.own("sum_step"))

            def norm_add(src, w0):
                inverse_rms()
                for t in range(KT + 3):
                    if t < KT:
                        if t >= 2:
                            dve.wait_ge(x_added, v.next("x_added"))
                        ve.scalar_tensor_tensor(tmp[:, t % 2, :], src[:, t, :],
                                                vec2[:, w0 + t:w0 + t + 1], rstd,
                                                ALU.mult, ALU.mult).then_inc(add_ready, v.tick("add_ready"))
                        dve.wait_ge(add_ready, v.own("add_ready"))
                    if t >= 3:
                        add_square(t - 3)
                dve.wait_ge(x_added, v.next("x_added", 2))

            def topk_round(m):
                t = m // 16 + 1
                s0, n = (0, 256, 640)[t - 1], P * (t + 1)
                sc = selm[:, s0:s0 + n]
                if m % 16 == 0:
                    chain(ve.tensor_tensor(sc[:, n - P:n], sc[:, n - P:n], caus[:], ALU.add))
                chain(ve.max(top8[:], sc))
                chain(ve.match_replace(sc, top8[:], sc, TAKEN))
                if m % 16 == 15:
                    chain(ve.tensor_scalar(sc, sc, TAKEN, NEG, ALU.not_equal, ALU.mult))

            def bias_tables(h):
                a0 = relt[:]
                for k in range(3):
                    o = 16 - 8 * k
                    ins = ve.tensor_tensor(
                        comb[:, h % 2, k, :].rearrange("p (j i) -> p j i", i=ROWS),
                        bass.AP(tensor=a0.tensor, offset=a0.offset + 384 * h + 383 - o,
                                ap=[list(a0.ap[0]), [-1, 32], [-48, 8]]), namask[:, k, :].rearrange("p (j i) -> p j i", i=ROWS),
                        ALU.add)
                chain(ins)

            def modulation(summed, h):
                k = h % KT
                dve.wait_ge(ada2_landed[h % 2], v.l * (8 * KT * ADA_LAY) + 16 * (h // 2 + 1))
                if k == 0:
                    if h % (2 * KT):
                        dve.wait_ge(lin_full, v.next("lin_full"))
                    ins = ve.tensor_scalar(summed[:], ada2[:, h % 2, :], cact[:, 0:1], None, ALU.mult)
                else:
                    ins = ve.scalar_tensor_tensor(summed[:], ada2[:, h % 2, :], cact[:, k:k + 1],
                                                  summed[:], ALU.mult, ALU.add)
                ins.then_inc(ada2_used, v.tick("ada2_used"))
                dve.wait_ge(ada2_used, v.own("ada2_used"))
                if k == KT - 1:
                    dve.sem_inc(acc_ready, v.tick("acc_ready"))

            def attend(units, p, sb, obuf, summed=None, h0=0):
                if units is na_units:
                    bias_tables(0)
                for i in range(len(units) + 4):
                    w = i - 2
                    if 0 <= w < len(units):
                        n = units[w]["n"]
                        dve.wait_ge(exp_done, v.count("exp_done", w + 1))
                        chain(ve.reciprocal(rinv[:, w % 4, :], rsum[:, w % 4, :]))
                        ve.tensor_scalar(p[:, w % 4, 0:n], p[:, w % 4, 0:n], rinv[:, w % 4, :], None,
                                         ALU.mult).then_inc(p_ready, v.tick("p_ready"))
                    if i < len(units):
                        u = units[i]
                        n = u["n"]
                        dve.wait_ge(s_full, v.count("s_full", i + 1))
                        src = ps[:, B_S + i % 2, 0:n]
                        if u["sel"] is not None:
                            chain(ve.tensor_tensor(sb[:, i % 2, 0:n], src, u["sel"], ALU.add))
                            src = sb[:, i % 2, 0:n]
                        if u["bias"] is not None:
                            dve.sem_inc(bias_step, v.tick("bias_step"))
                            ins = ve.tensor_tensor_reduce(
                                out=sb[:, i % 2, 0:n], in0=src, in1=u["bias"], scale=-1.0,
                                scalar=-TAKEN, op0=ALU.add, op1=ALU.min, accum_out=nmax[:, i % 4, :])
                        else:
                            ins = ve.tensor_reduce(nmax[:, i % 4, :], src, AX.X, ALU.max, negate=True)
                        ins.then_inc(max_ready, v.tick("max_ready"))
                    if summed is not None and i % 2 == 0 and i < len(units):
                        modulation(summed, h0 + i // 2)
                    if units is na_units and i % TT == 1 and i // TT + 1 < NAH:
                        bias_tables(i // TT + 1)
                    w = i - 4
                    if w >= 0 and w % 8 == 7:
                        dve.wait_ge(pv_done, v.count("pv_done", w + 1))
                        if units is b2_units:
                            dve.wait_ge(o_hi, v.next("o_hi"))
                            t = (6, 7, 4, 5)[w // 8]
                            low(act_lo[:, t, :], ps[:, B_O, :], act_hi[:, t, :], "o_copied")
                        else:
                            ve.tensor_copy(obuf[:, w // 8, :], ps[:, B_O, :]).then_inc(
                                o_copied, v.tick("o_copied"))
                    if units is b2_units and i < 16:
                        topk_round(32 + i)
                dve.wait_ge(o_copied, v.own("o_copied"))
                v.skip("s_full", len(units))
                v.skip("exp_done", len(units))
                v.skip("pv_done", len(units))

            ve.memset(eps[:], EPS)
            dve.wait_ge(c_sig, v.next("c_sig"))
            ve.tensor_tensor(cact[:], cT[:], csig[:], ALU.mult).then_inc(cact_ready, 1)
            dve.wait_ge(cact_ready, 1)
            for t in range(KT):
                add_square(t)
            with dve.Fori(0, ADA_PRO // 2) as i:
                for m in range(2):
                    for k in range(KT):
                        dve.wait_ge(ada_landed[k], 32 * i + (16 * m + 16))
                        if k == 0:
                            ins = ve.tensor_scalar(acc[:, m, :], ada[:, k, :], cact[:, 0:1], None,
                                                   ALU.mult)
                        else:
                            ins = ve.scalar_tensor_tensor(acc[:, m, :], ada[:, k, :],
                                                          cact[:, k:k + 1], acc[:, m, :],
                                                          ALU.mult, ALU.add)
                        ins.then_inc(ada_used, 1)
                        dve.wait_ge(ada_used, 2 * KT * i + (KT * m + k + 1))
                    dve.sem_inc(ada_sum, 1)
                dve.wait_ge(ada_full, 2 * i + 2)
                ve.tensor_tensor(modf[:, bass.ds(16 * i, 16)], ps[:, B_N, 0:16],
                                 modf[:, bass.ds(16 * i, 16)], ALU.add).then_inc(ada_taken, 1)
            dve.wait_ge(ada_taken, ADA_PRO // 2)

            with v.layers():
                ve.tensor_copy(cur[:, 0:NV1], vec1[:, bass.ds(v.l, 1), :].rearrange("p o m -> p (o m)"))
                chain(ve.tensor_copy(cur[:, NV1:NV1 + 16],
                                     mod[:, bass.ds(v.l, 1), 0:16].rearrange("p o m -> p (o m)")))
                ins = ve.scalar_tensor_tensor(scl[:, 0, :], cur[:, M_SCA:M_SCA + 8], 1.0,
                                              cur[:, V_GMIX:V_GMIX + 8], ALU.add, ALU.mult)
                ins.then_inc(vec_ready, v.tick("vec_ready"))
                dve.wait_ge(vec_ready, v.own("vec_ready"))
                dve.wait_ge(vec_ready, v.next("vec_ready"))
                norm(KT, lambda t: x[:, t, :], lambda t: scl[:, 0, t:t + 1],
                     lambda t: act_hi[:, t, :], lambda t: act_lo[:, t, :],
                     lambda t: cur[:, M_SHA + t:M_SHA + t + 1])
                dve.wait_ge(bias_in, v.next("bias_in", NAH, 16))
                v.skip("lin_out", 16)
                v.skip("lin_full", 16)
                attend(na_units, p_sb, s_sb, o_na, acc_na, 0)
                v.skip("lin_out", 2)
                dve.wait_ge(lin_out, v.next("lin_out", 2))
                norm(2, lambda t: craw[:, t, :], lambda t: cur[:, V_GQ + t:V_GQ + t + 1],
                     lambda t: cn_hi[:, t, :], lambda t: cn_lo[:, t, :])
                dve.wait_ge(lin_out, v.next("lin_out", 2))
                norm(1, lambda t: craw[:, 2 + t, :], lambda t: cur[:, V_GKV:V_GKV + 1],
                     lambda t: cn_hi[:, 2 + t, :], lambda t: cn_lo[:, 2 + t, :])
                v.skip("sq_ready", 3)
                ve.tensor_tensor(rmul[0:32, 0, :], rraw[0:32, 2, :], cosT[0:32, :], ALU.mult)
                chain(ve.tensor_tensor(rmul[0:32, 1, :], rraw[32:64, 2, :], sinT[32:64, :], ALU.mult))
                for h in range(MLAH):
                    ins = ve.tensor_tensor(kT[64:96, h, :], rmul[0:32, 0, :], rmul[0:32, 1, :], ALU.add)
                ins.then_inc(rope_done, v.tick("rope_done"))
                dve.wait_ge(rope_done, v.own("rope_done"))
                dve.wait_ge(lin_out, v.next("lin_out", 8))
                for w in range(2):
                    ve.tensor_tensor(rmul[:, 0, :], rraw[:, w, :], cosT[:], ALU.mult)
                    chain(ve.tensor_tensor(rmul[:, 1, :], rraw[:, 2 + w, :], sinT[:], ALU.mult))
                    for h in range(4):
                        r = slice(32 * h, 32 * h + 32)
                        ins = ve.tensor_tensor(qT[64:96, 4 * w + h, :], rmul[r, 0, :], rmul[r, 1, :],
                                               ALU.add)
                    if w == 0:
                        chain(ins)
                ins.then_inc(rope_done, v.tick("rope_done"))
                dve.wait_ge(rope_done, v.own("rope_done"))
                v.skip("lin_out", 8)
                v.skip("lin_full", 1 + 4 + 8 + 8)
                attend(mla_units, p_sb, s_sb, o_mla, acc_mla, 2 * KT)
                dve.wait_ge(lin_out, v.next("lin_out", 2))
                chain(ve.tensor_tensor(modf[:, bass.ds(32 * v.l + 32, 32)], modraw[:],
                                       modf[:, bass.ds(32 * v.l + 32, 32)], ALU.add))
                chain(ve.tensor_copy(cur[:, NV1 + 16:NV1 + 48],
                                     mod[:, bass.ds(v.l, 1), 16:48].rearrange("p o m -> p (o m)")))
                ve.scalar_tensor_tensor(scl[:, 1, :], cur[:, M_SCM:M_SCM + 8], 1.0,
                                        cur[:, V_GMLP:V_GMLP + 8], ALU.add,
                                        ALU.mult).then_inc(vec2_ready, v.tick("vec2_ready"))
                dve.wait_ge(vec2_ready, v.own("vec2_ready"))
                for br in range(2):
                    o = (o_na, o_mla)[br]
                    dve.wait_ge(lin_out, v.count("lin_out", 0))
                    for t in range(4):
                        dve.wait_ge(osplit_hi, v.next("osplit_hi"))
                        low(os_lo[:, t, :], o[:, t, :], os_hi[:, t, :], "osplit_ready")
                    v.skip("lin_out", 8)
                    for t in range(KT):
                        dve.wait_ge(lin_out, v.next("lin_out"))
                        if br == 0:
                            ins = ve.tensor_tensor(merged[:, t, :], ybuf[:, t % 2, :], gsig[:, t, :],
                                                   ALU.mult)
                        else:
                            chain(ve.tensor_tensor(gsig[:, t, :], ybuf[:, t % 2, :], gsig[:, t, :],
                                                   ALU.mult))
                            ins = ve.tensor_tensor(merged[:, t, :], merged[:, t, :], gsig[:, t, :],
                                                   ALU.add)
                        ins.then_inc(merged_ready, v.tick("merged_ready"))
                        dve.wait_ge(merged_ready, v.own("merged_ready"))
                for t in range(KT):
                    dve.wait_ge(hi_ready, v.next("hi_ready"))
                    low(act_lo[:, t, :], merged[:, t, :], act_hi[:, t, :], "act_ready")

                def residual():
                    for t in range(KT + 1):
                        if t < KT:
                            dve.wait_ge(lin_out, v.next("lin_out"))
                            ve.tensor_tensor(x[:, t, :], x[:, t, :], ybuf[:, t % 2, :],
                                             ALU.add).then_inc(x_ready, v.tick("x_ready"))
                            dve.wait_ge(x_ready, v.own("x_ready"))
                        if t:
                            add_square(t - 1)

                residual()
                norm(KT, lambda t: x[:, t, :], lambda t: scl[:, 1, t:t + 1],
                     lambda t: act_hi[:, t, :], lambda t: act_lo[:, t, :],
                     lambda t: cur[:, M_SHM + t:M_SHM + t + 1])
                with v.ff():
                    for t in range(KT + 1):
                        if t < KT:
                            dve.wait_ge(lin_out, v.next("lin_out"))
                            ve.tensor_tensor(squ[:, t % 2, :], rel_u[:, t % 2, :],
                                                      rel_u[:, t % 2, :], ALU.mult).then_inc(square_ready, v.tick("square_ready"))
                            dve.wait_ge(square_ready, v.own("square_ready"))
                        if t:
                            dve.wait_ge(hi_ready, v.next("hi_ready"))
                            low(hid_lo[:, t - 1, :], squ[:, (t - 1) % 2, :], hid_hi[:, t - 1, :],
                                "act_ready")
                    residual()

            inverse_rms()
            for t in range(KT):
                if t >= 2:
                    dve.wait_ge(permuted, v.next("permuted"))
                ve.scalar_tensor_tensor(tmp[:, t % 2, :], x[:, t, :],
                                                 vec2[:, W_GF + t:W_GF + t + 1], rstd,
                                                 ALU.mult, ALU.mult).then_inc(scaled_ready, v.tick("scaled_ready"))
                dve.wait_ge(scaled_ready, v.own("scaled_ready"))
            dve.wait_ge(permuted, v.next("permuted", 2))
            for t in range(KT):
                add_square(t)
            ve.memset(relrow[0:8, 0:P - 1], NEG).then_inc(rel_ready, v.tick("rel_ready"))
            dve.wait_ge(rel_ready, v.own("rel_ready"))
            norm(KT, lambda t: x[:, t, :], lambda t: vec2[:, W_PRE + t:W_PRE + t + 1],
                 lambda t: act_hi[:, t, :], lambda t: act_lo[:, t, :])
            dve.wait_ge(small2_in, v.next("small2_in", 5, 16))
            v.skip("lin_out", 1)

            def convolution(t):
                cw = lambda k: vec2[:, W_CW + 2 * k + t:W_CW + 2 * k + t + 1]
                chain(ve.tensor_tensor(ct[:, 0, :], zc[:, t, :], zc[:, 2 + t, :], ALU.mult))
                chain(ve.tensor_scalar(ct[:, 1, :], ct[:, 0, :], cw(2), None, ALU.mult))
                for k in (1, 0):
                    d = 2 - k
                    chain(ve.scalar_tensor_tensor(ct[:, 1, d:S], ct[:, 0, 0:S - d], cw(k),
                                                  ct[:, 1, d:S], ALU.mult, ALU.add))
                ve.tensor_tensor(zc[:, t, :], ct[:, 1, :], zc[:, 4 + t, :],
                                 ALU.mult).then_inc(ya_ready, v.tick("ya_ready"))
                dve.wait_ge(ya_ready, v.own("ya_ready"))

            def pooling(t):
                src, wins = zc[:, 6 + t, :], []
                for k in range(4 if t else 2):
                    d, dst = 2 ** k, ct[:, k % 3, :]
                    ve.tensor_copy(dst[:, 0:d], src[:, 0:d])
                    chain(ve.tensor_tensor(dst[:, d:S], src[:, d:S], src[:, 0:S - d], ALU.add))
                    src = dst
                    wins.append(dst)
                for k, r in enumerate((slice(0, 64), slice(64, P))):
                    win = wins[2 * t + k]
                    chain(ve.tensor_tensor(win[r], win[r], pcnt[r, t, :], ALU.mult))
                    ins = ve.tensor_tensor(zc[r, 6 + t, :], win[r], zc[r, 6 + t, :], ALU.subtract)
                ins.then_inc(pool_d, v.tick("pool_d"))
                dve.wait_ge(pool_d, v.own("pool_d"))

            dve.wait_ge(lin_out, v.next("lin_out", 8))
            for m in range(24):
                t, h = m // 8 + 1, m % 8
                s0, n = (0, 256, 640)[t - 1], P * (t + 1)
                score = selm[:, s0:s0 + n]
                dve.wait_ge(ix_relu, v.next("ix_relu"))
                if h == 0:
                    ins = ve.tensor_scalar(score, ixr[:, m % 2, 0:n], iw[:, t, 0:1], None, ALU.mult)
                else:
                    ins = ve.scalar_tensor_tensor(score, ixr[:, m % 2, 0:n], iw[:, t, h:h + 1],
                                                  score, ALU.mult, ALU.add)
                ins.then_inc(ix_used, v.tick("ix_used"))
                dve.wait_ge(ix_used, v.own("ix_used"))
                if m == 7:
                    dve.wait_ge(lin_out, v.next("lin_out", 6))
                if m in (8, 9):
                    convolution(m - 8)
                elif m in (10, 11):
                    pooling(m - 10)
                if m >= 8:
                    for r in range(2):
                        topk_round(2 * (m - 8) + r)
            dve.wait_ge(lin_out, v.next("lin_out", 8 + 2 + 8))
            for t in range(4):
                dve.wait_ge(hi_ready, v.next("hi_ready"))
                low(act_lo[:, t, :], zc[:, t if t < 2 else 4 + t, :], act_hi[:, t, :], "act_ready")
            dve.wait_ge(wide_in, v.next("wide_in", 8, 16))
            attend(b2_units, p2_sb, s2_sb, None)
            v.skip("lin_out", KT)
            for t in range(KT):
                add_square(t)
            norm_add(mixr, W_MPOST)
            norm(KT, lambda t: x[:, t, :], lambda t: vec2[:, W_FPRE + t:W_FPRE + t + 1],
                 lambda t: act_hi[:, t, :], lambda t: act_lo[:, t, :])
            for c in range(H2T):
                dve.wait_ge(lin_out, v.next("lin_out", 2))
                chain(ve.tensor_tensor(tmp[:, c % 2, :], sq[:, 0, :], std[:], ALU.mult))
                ve.tensor_tensor(tmp[:, c % 2, :], tmp[:, c % 2, :], sq[:, 1, :], ALU.mult).then_inc(prod_ready, v.tick("prod_ready"))
                dve.wait_ge(prod_ready, v.own("prod_ready"))
                dve.wait_ge(hi_ready, v.next("hi_ready"))
                low(h2_lo[:, c, :], tmp[:, c % 2, :], h2_hi[:, c, :], "act_ready")
            v.skip("lin_out", KT)
            for t in range(KT - 1):
                add_square(t)
            dve.wait_ge(lin_full, v.next("lin_full", 1 + 4 + 1 + 16 + 1 + 2 + 8 + KT + 2 * H2T + KT))
            for t in range(2):
                dve.wait_ge(hi_ready, v.next("hi_ready"))
                low(pT_lo[:, t, :], ps[:, B_S + t, :], pT_hi[:, t, :], "act_ready")
            add_square(KT - 1)
            norm_add(fraw, W_FPOST)
            norm(KT, lambda t: x[:, t, :], lambda t: vec2[:, W_PLE + t:W_PLE + t + 1],
                 lambda t: act_hi[:, t, :], lambda t: act_lo[:, t, :])
            v.skip("lin_out", KT)
            for t in range(KT):
                dve.wait_ge(lin_out, v.next("lin_out"))
                chain(ve.tensor_tensor(pg[:, t, :], pg[:, t, :], pj[:, t, :], ALU.mult))
                ve.tensor_tensor(x[:, t, :], x[:, t, :], pg[:, t, :], ALU.add).then_inc(x_ready, v.tick("x_ready"))
                dve.wait_ge(x_ready, v.own("x_ready"))

        @block.tensor
        def _(pe):
            v = View(pe, made, per, mlp_entered)
            te = nc.tensor

            def bank(n):
                if v.n["lin_out"] >= 1:
                    pe.wait_ge(lin_out, v.count("lin_out", -1))
                v.skip("lin_out")
                return ps[:, n % 2, :]

            def chunk(c):
                n = v.l * C_LAYER + (c + 1)
                if v.j is not None:
                    n = n + v.j * 8
                pe.wait_ge(w_split, n)
                return whi[:, c % 2, :], wlo[:, c % 2, :]

            def three(out, w, a, start, stop, swap=False):
                (wh, wl), (ah, al) = w, a
                if swap:
                    (wh, wl), (ah, al) = a, w
                te.matmul(out, wh, ah, start=start, stop=False)
                te.matmul(out, wh, al, start=False, stop=False)
                return te.matmul(out, wl, ah, start=False, stop=stop)

            def linear(n, c, tiles, kts, cols, src, wait=None, after=None, between=None):
                wh, wl = chunk(c)

                def part(b, i, k):
                    o = k * cols + P * i
                    return three(b, (wh[:, o:o + P], wl[:, o:o + P]), src(k), k == 0, k == kts - 1)

                if wait is not None and tiles == 2:
                    b, lag = [bank(n)], 2
                    for k in range(kts + lag):
                        if k == lag:
                            b.append(bank(n + 1))
                        for i in range(2):
                            kt = k - lag * i
                            if not 0 <= kt < kts:
                                continue
                            if i == 0 and isinstance(wait, list):
                                pe.wait_ge(act_ready, wait[kt])
                            elif i == 0:
                                pe.wait_ge(sems[wait], v.next(wait))
                            ins = part(b[i], i, kt)
                            if kt == kts - 1:
                                ins.then_inc(lin_full, v.tick("lin_full"))
                    return n + tiles
                for i in range(tiles):
                    if i and between:
                        between()
                    b = bank(n + i)
                    for k in range(kts):
                        if i == 0 and wait is not None:
                            pe.wait_ge(sems[wait], v.next(wait))
                        ins = part(b, i, k)
                    ins.then_inc(lin_full, v.tick("lin_full"))
                    if after:
                        after()
                return n + tiles

            def by_token(n, c, kts, cols, src, width, after=None):
                wh, wl = chunk(c)
                for t in range(TT):
                    b = bank(n + t)
                    for k in range(kts):
                        o = k * cols + (cols - width)
                        ah, al = src(k)
                        ins = three(b[:, 0:width], (wh[:, o:o + width], wl[:, o:o + width]),
                                    (ah[:, P * t:P * t + P], al[:, P * t:P * t + P]),
                                    k == 0, k == kts - 1, swap=True)
                    ins.then_inc(lin_full, v.tick("lin_full"))
                    if after:
                        after()
                return n + TT

            def spread():
                pe.wait_ge(diag_ready, v.next("diag_ready"))
                te.matmul(ps[:, B_N, :], ones[:], diag[:].rearrange("p t q -> p (t q)"), start=True,
                          stop=True).then_inc(rstd_full, v.tick("rstd_full"))

            def sum_squares(n_tiles):
                pe.wait_ge(sq_ready, v.next("sq_ready", n_tiles))
                for b in range(TT):
                    for t in range(n_tiles):
                        ins = te.matmul(ps[:, B_N, b:b + 1], sq[:, t, P * b:P * b + P], ones[:, 0:1],
                                        start=(t == 0), stop=(t == n_tiles - 1))
                ins.then_inc(sq_used, v.tick("sq_used"))

            def norm_x(steps=KT):
                pe.wait_ge(sum_step, v.next("sum_step", steps))
                v.skip("sq_ready", steps)
                for b in range(TT):
                    ins = te.matmul(ps[:, B_N, b:b + 1], ssum[:, P * b:P * b + P], ones[:, 0:1],
                                    start=True, stop=True)
                ins.then_inc(sq_used, v.tick("sq_used"))
                spread()

            def attend(units, p, pt, n=0, acc=None):
                for i in range(len(units) + 4):
                    if i < len(units):
                        u = units[i]
                        if i >= 2:
                            pe.wait_ge(exp_done, v.count("exp_done", i - 1))
                        te.matmul(ps[:, B_S + i % 2, 0:u["n"]], u["q"], u["k"], start=True,
                                  stop=True).then_inc(s_full, v.tick("s_full"))
                    if acc is not None and i in (15, len(units) + 2):
                        w = i > 15
                        b = bank(n + w)
                        pe.wait_ge(acc_ready, v.next("acc_ready"))
                        for k in range(KT):
                            ins = te.matmul(b[:, k:k + 1], acc[:, P * k:P * k + P], ones[:, 0:1],
                                            start=True, stop=True)
                        ins.then_inc(lin_full, v.tick("lin_full"))
                    w = i - 3
                    if 0 <= w < len(units):
                        pe.wait_ge(p_ready, v.count("p_ready", w + 1))
                        if w >= 2:
                            pe.wait_ge(pt_copied, v.count("pt_copied", w - 1))
                        for b_ in range(units[w]["n"] // P):
                            ins = te.transpose(ps[:, B_T + w % 2, P * b_:P * b_ + P],
                                               p[:, w % 4, P * b_:P * b_ + P], ident[:])
                        ins.then_inc(pt_full, v.tick("pt_full"))
                    w = i - 4
                    if w >= 0:
                        u = units[w]
                        if w % 8 == 0 and w:
                            pe.wait_ge(o_copied, v.count("o_copied", w // 8))
                        pe.wait_ge(pt_copied, v.count("pt_copied", w + 1))
                        r = 64 * (u["head"] % 2)
                        o = ps[r:r + 64, B_O, P * u["t"]:P * u["t"] + P]
                        nb = u["n"] // P
                        for b_ in range(nb):
                            ins = te.matmul(o, u["v"][b_], pt[:, w % 2, P * b_:P * b_ + P],
                                            start=(b_ == 0), stop=(b_ == nb - 1))
                        ins.then_inc(pv_done, v.tick("pv_done"))
                for name in ("exp_done", "p_ready", "pt_copied"):
                    v.skip(name, len(units))
                pe.wait_ge(o_copied, v.next("o_copied", len(units) // 8))

            pe.wait_ge(consts_in, v.next("consts_in", 8, 16))
            pe.wait_ge(x_in, v.next("x_in", TT, 16))
            for t in range(KT):
                b = bank(t)
                for k in range(TT):
                    ins = te.transpose(b[:, P * k:P * k + P], xin[:, k, P * t:P * t + P], ident[:])
                ins.then_inc(lin_full, v.tick("lin_full"))
            with pe.Fori(0, ADA_PRO // 2) as i:
                for m in range(2):
                    pe.wait_ge(ada_sum, 2 * i + (m + 1))
                    for k in range(KT):
                        ins = te.matmul(ps[:, B_N, KT * m + k:KT * m + k + 1],
                                        acc[:, m, P * k:P * k + P], ones[:, 0:1],
                                        start=True, stop=True)
                    ins.then_inc(ada_full, 1)
            pe.wait_ge(ada_taken, ADA_PRO // 2)

            h = lambda k: (act_hi[:, k, :], act_lo[:, k, :])
            with v.layers():
                norm_x(0)
                n = linear(0, C_Q, 2, KT, 256, h, wait="act_ready")
                for c in range(C_Q + 1, C_V):
                    n = linear(n, c, 2, KT, 256, h)
                for c in (C_V, C_V + 1):
                    n = by_token(n, c, KT, 256, h, 256)
                pe.wait_ge(lin_out, v.count("lin_out", 0))
                pe.wait_ge(vodd_in, v.next("vodd_in", 6, 16))
                attend(na_units, p_sb, pt_sb, n, acc_na)
                n += 2
                n = linear(n, C_CQ, 2, KT, 256, h)
                n = linear(n, C_CKV, 2, KT, 256, h, between=lambda: sum_squares(2))
                spread()
                cn = lambda k: (cn_hi[:, k, :], cn_lo[:, k, :])
                steps = iter([lambda: sum_squares(1), spread] + 6 * [lambda: None])
                n = linear(n, C_UQ, 8, 2, 1024, cn, wait="act_ready", after=lambda: next(steps)())
                pe.wait_ge(act_ready, v.next("act_ready"))
                ckv = lambda k: (cn_hi[:, 2, :], cn_lo[:, 2, :])
                n = linear(n, C_UKV, 4, 1, 1024, ckv)
                n = by_token(n, C_UKV, 1, 1024, ckv, 512)
                pe.wait_ge(lin_out, v.count("lin_out", 0))
                pe.wait_ge(rope_done, v.next("rope_done", 2))
                attend(mla_units, p_sb, pt_sb, n, acc_mla)
                n += 2
                os = lambda k: (os_hi[:, k, :], os_lo[:, k, :])
                for br in range(2):
                    for c in range(4):
                        n = linear(n, (C_GNA, C_GMLA)[br] + c, 2, KT, 256, h)
                    for c in range(2):
                        n = linear(n, (C_BNA, C_BMLA)[br] + c, 4, 4, 512, os,
                                   wait="osplit_ready" if c == 0 else None)
                for c in range(4):
                    n = linear(n, C_OUT + c, 2, KT, 256, h, wait="act_ready" if c == 0 else None)
                norm_x()
                normed = [v.next("act_ready") for _ in range(KT)]
                hid = lambda k: (hid_hi[:, k, :], hid_lo[:, k, :])
                with v.ff():
                    n = linear(n, C_FF, 2, KT, 256, h, wait=normed)
                    for c in range(1, 4):
                        n = linear(n, C_FF + c, 2, KT, 256, h)
                    for c in range(4, 8):
                        n = linear(n, C_FF + c, 2, KT, 256, hid, wait="act_ready" if c == 4 else None)

            norm_x(0)
            pe.wait_ge(small2_in, v.next("small2_in", 5, 16))
            v.skip("lin_out")
            te.matmul(ps[0:8, 0, :], relT[0:32, :], onehot[0:32, 0:S], start=True, stop=True).then_inc(lin_full, v.tick("lin_full"))
            norm_x()
            n = 1
            for c in range(2):
                n = linear(n, C2_IX + c, 2, KT, 256, h, wait="act_ready" if c == 0 else None)
            n = linear(n, C2_IX + 2, 1, KT, 256, h)
            index = iter(range(24))

            def index_product():
                m = next(index)
                t, hh = m // 8 + 1, m % 8
                r = slice(64 * (hh % 2), 64 * (hh % 2) + 64)
                if m >= 2:
                    pe.wait_ge(ix_relu, v.next("ix_relu"))
                te.matmul(ps[:, B_S + m % 2, 0:P * (t + 1)], iq[r, hh // 2, P * t:P * t + P],
                          ik[r, 0:P * (t + 1)], start=True, stop=True).then_inc(ix_full, v.tick("ix_full"))

            pe.wait_ge(lin_out, v.count("lin_out", 0))
            for c in range(8):
                n = linear(n, C2_Z + c, 2, KT, 256, h, after=index_product)
                if c == 0:
                    b = bank(n)
                    for t in range(TT):
                        ins = te.transpose(b[:, 8 * t:8 * t + 8], iwT[0:8, P * t:P * t + P],
                                           ident[0:8, 0:8])
                    ins.then_inc(lin_full, v.tick("lin_full"))
                    n += 1
            pe.wait_ge(pool_d, v.next("pool_d", 2))
            for t in range(2):
                b = bank(n)
                te.matmul(b, poolw[:, t, :], zc[:, 6 + t, :], start=True,
                          stop=True).then_inc(lin_full, v.tick("lin_full"))
                n += 1
            for c in range(2):
                n = by_token(n, C2_V + c, KT, 256, h, 256, after=index_product)
            pe.wait_ge(lin_out, v.count("lin_out", 0))
            pe.wait_ge(ix_relu, v.next("ix_relu", 2))
            attend(b2_units, p2_sb, pt2_sb)
            pe.wait_ge(act_ready, v.next("act_ready", 4))
            for c in range(4):
                n = linear(n, C2_OUT + c, 2, KT, 256, h)
            norm_x()
            norm_x()
            for c in range(H2T):
                n = linear(n, C2_GU + c, 2, KT, 256, h, wait="act_ready" if c == 0 else None)
            for t in range(KT):
                if t == 1:
                    pe.wait_ge(p_in, v.next("p_in", 1, 16))
                    for m in range(2):
                        for k in range(TT):
                            ins = te.transpose(ps[:, B_S + m, P * k:P * k + P],
                                               pin[:, k, P * m:P * m + P], ident[:])
                    ins.then_inc(p_full, v.tick("p_full"))
                b = bank(n)
                for half in range(2):
                    wh, wl = chunk(C2_DOWN + 2 * t + half)
                    for k in range(11):
                        kk_ = 11 * half + k
                        if t == 0:
                            pe.wait_ge(act_ready, v.next("act_ready"))
                        ins = three(b, (wh[:, P * k:P * k + P], wl[:, P * k:P * k + P]),
                                    (h2_hi[:, kk_, :], h2_lo[:, kk_, :]), kk_ == 0, kk_ == H2T - 1)
                    if half == 0:
                        ins.then_inc(half_used, v.tick("half_used"))
                ins.then_inc(lin_full, v.tick("lin_full"))
                n += 1
            pT = lambda k: (pT_hi[:, k, :], pT_lo[:, k, :])
            wh, wl = chunk(C2_PP)

            def project(n, tiles):
                for t in tiles:
                    b = bank(n)
                    for k in range(2):
                        o = 1024 * k + P * t
                        ins = three(b, (wh[:, o:o + P], wl[:, o:o + P]), pT(k), k == 0, k == 1)
                    ins.then_inc(lin_full, v.tick("lin_full"))
                    n += 1
                return n

            pe.wait_ge(act_ready, v.next("act_ready", 2))
            n = project(n, range(2))
            norm_x()
            n = project(n, range(2, KT))
            norm_x()
            for c in range(4):
                n = linear(n, C2_PG + c, 2, KT, 256, h, wait="act_ready" if c == 0 else None)
            pe.wait_ge(x_ready, v.next("x_ready", KT))
            for t in range(TT):
                for k in range(2):
                    b = bank(n)
                    for f in range(4):
                        ins = te.transpose(b[:, P * f:P * f + P], x[:, 4 * k + f, P * t:P * t + P],
                                           ident[:])
                    ins.then_inc(lin_full, v.tick("lin_full"))
                    n += 1

    return made


def host_constants():
    p = np.arange(P)
    f32 = np.float32
    ident = np.eye(P, dtype=f32)
    ones = np.ones((P, P), f32)
    namask = np.full((P, 3, 32, 8), NEG, f32)
    for kind, (tile, c0) in enumerate(((0, 0), (1, 8), (3, 32))):
        col = 16 * tile + p // 8
        start = np.clip(col - 8, 0, COLS - 16)
        j = c0 + np.arange(32)
        ok = (j[None] >= start[:, None]) & (j[None] < start[:, None] + 16)
        namask[:, kind][ok] = 0.0
    invf = np.empty((P, 2), f32)
    invf[:, 0] = f32(1.0) / np.power(f32(10000.0), (np.arange(0, 32, 2, dtype=f32) / f32(32)))[p % 16]
    invf[:, 1] = np.where(p % 32 < 16, -1.0, 1.0)
    dist = np.arange(S)
    n = np.maximum(dist, 0)
    nf = np.maximum(n, 1).astype(f32)
    large = 16 + (np.log(nf / f32(16)) / f32(np.log(8.0)) * f32(16)).astype(np.int32)
    bucket = np.where(n < 16, n, np.minimum(large, 31))
    onehot = (np.arange(32)[:, None] == bucket[None]).astype(f32)
    pcnt = np.empty((P, 2, S), f32)
    for t in range(2):
        for k in range(2):
            pcnt[64 * k:64 * k + 64, t] = 1.0 / np.minimum(np.arange(S) + 1, 2 ** (2 * t + k + 1))
    caus = np.where(p[None] > p[:, None], NEG, 0.0).astype(f32)
    return dict(ident=ident, ones=ones, namask=namask.reshape(P, 3, 256), invf=invf, onehot=onehot,
                pcnt=pcnt, caus=caus)


def chunks(w, cols):
    k, n = w.shape
    c = w.reshape(k // P, P, n // cols, cols).transpose(2, 1, 0, 3).reshape(n // cols, P, -1)
    return np.pad(c, ((0, 0), (0, 0), (0, CH - c.shape[2])))


def columns(v):
    return v.reshape(-1, P).T


def kernel(**inputs):
    import concourse.bacc as bacc
    from concourse.bass_utils import run_bass_kernel_spmd

    i = {k: np.asarray(v) for k, v in inputs.items()}
    stream, vec1 = [], []
    for l in range(DEPTH):
        w = i["w_in"][l]
        kr = w[:, 1920:1952]
        stream += [chunks(w[:, 0:512], 256), chunks(w[:, 512:1024], 256), chunks(w[:, 1024:1536], 256),
                   chunks(w[:, 1536:1792], 256),
                   chunks(np.concatenate([w[:, 1792:1920], kr, kr[:, 16:], kr[:, :16],
                                          np.zeros((D, 64), w.dtype)], 1), 256)]
        uq = i["w_uq"][l].reshape(256, 8, 96)
        stream.append(chunks(np.concatenate([
            uq[:, :, :64].reshape(256, 512), uq[:, :, 64:].reshape(256, 256),
            np.concatenate([uq[:, :, 80:], uq[:, :, 64:80]], 2).reshape(256, 256)], 1), 1024))
        ukv = i["w_ukv"][l].reshape(P, 8, 128)
        stream.append(chunks(np.concatenate([ukv[:, :, :64].reshape(P, 512),
                                             ukv[:, :, 64:].reshape(P, 512)], 1), 1024))
        for k, br in enumerate(("w_br_na", "w_br_mla")):
            stream += [chunks(w[:, 1952 + D * k:1952 + D * k + D], 256), chunks(i[br][l], 512)]
        stream.append(chunks(i["w_out"][l], 256))
        for j in range(FFJ):
            stream += [chunks(i["w_ff1"][l][:, D * j:D * j + D], 256),
                       chunks(i["w_ff2"][l][D * j:D * j + D], 256)]
        vec1.append(np.concatenate([columns(i[k][l]) for k in ("g_mix", "g_mlp", "b_gate", "g_q", "g_kv")], 1))
    w = i["w_in_2"][0]
    o = np.cumsum([0] + [256] * 7 + [512, 64, 8, 256, 256, 256])
    part = lambda k: w[:, o[k]:o[k + 1]]
    stream.append(chunks(part(7), 256))
    stream.append(chunks(np.concatenate([part(8), part(9), np.zeros((D, 184), w.dtype)], 1), 256))
    for k in (0, 1, 2, 3, 4, 5, 10, 11):
        stream.append(chunks(part(k), 256))
    stream += [chunks(part(6), 256), chunks(part(12), 256), chunks(i["w_out_2"][0], 256)]
    gu = i["w_gate_up_2"][0].reshape(D, 2, H2T, P).transpose(0, 2, 1, 3).reshape(D, -1)
    stream.append(chunks(gu, 256))
    down = chunks_down(i["w_down_2"][0])
    stream += [down, chunks(i["w_ple_proj_2"][0], 1024), chunks(i["w_ple_gate_2"][0], 256)]
    stream = np.concatenate(stream)
    assert stream.shape == (N_CHUNK, P, CH)

    ada = i["w_ada"].reshape(DEPTH, KT, P, 6, D).transpose(0, 3, 1, 2, 4).reshape(-1, P, D)
    rpb = np.zeros((DEPTH, NAH, 16, 48), np.float32)
    rpb[:, :, :15, 16:47] = i["rpb"]
    rpb = rpb.reshape(DEPTH, NAH, -1)[:, :, ::-1]
    poolw = np.zeros((P, 2, P), np.float32)
    for k in range(4):
        r = slice(64 * (k % 2), 64 * (k % 2) + 64)
        poolw[r, k // 2, r] = i["pool_w_2"][0, k]
    vec2 = np.concatenate([columns(v) for v in (
        i["g_final"], i["g_mix_pre_2"][0], i["pool_scale_2"][0], i["conv_w_2"][0].reshape(-1),
        i["g_mix_post_2"][0], i["g_ffn_pre_2"][0], i["g_ffn_post_2"][0], i["g_ple_2"][0])], 1)
    arrays = dict(
        x=i["x"], positions=i["positions"], w_stream=stream, w_ada=ada,
        vec1=np.stack(vec1, 1), vec2=vec2,
        bada=np.concatenate([columns(i["b_ada"][l]) for l in range(DEPTH)], 1), cT=columns(i["c"]),
        rpb_rev=rpb, relT=i["rel_bias_2"].T, poolw=poolw, p_2=i["p_2"], **host_constants())
    arrays = {k: np.ascontiguousarray(v) for k, v in arrays.items()}

    counts = {}
    for final in (False, True):
        nc = bacc.Bacc("TRN2", target_bir_lowering=False, num_devices=1)
        aps = {k: nc.dram_tensor("in_" + k, v.shape, mybir.dt.from_np(v.dtype), kind="ExternalInput").ap()
               for k, v in arrays.items()}
        out = nc.dram_tensor("out", (1, S, D), F32, kind="ExternalOutput").ap()
        made = build(nc, counts, aps, out)
        counts = {k: (m[0], m[1], m[2]) for k, m in made.items()}
    r = run_bass_kernel_spmd(nc, [{"in_" + k: v for k, v in arrays.items()}], core_ids=[0])
    return r.results[0]["out"]


def chunks_down(w):
    c = w.reshape(2, 11, P, KT, P).transpose(3, 0, 2, 1, 4).reshape(2 * KT, P, 11 * P)
    return np.pad(c, ((0, 0), (0, 0), (0, CH - 11 * P)))
```
